# Optimizing a Trainium2 kernel written in Bass

```python
import math
import jax, jax.numpy as jnp
from jax import lax
import numpy as np

D_MODEL = 1024
BATCH = 1
SEQ = 1024
DEPTH = 1

MIX_WIDTH = D_MODEL
ATT_WIDTH = MIX_WIDTH // 2
POOL_WIDTH = MIX_WIDTH - ATT_WIDTH
HEAD_DIM = 64
N_Q_HEADS = ATT_WIDTH // HEAD_DIM
N_KV_HEADS = 2
Q_PER_KV = N_Q_HEADS // N_KV_HEADS
KV_WIDTH = N_KV_HEADS * HEAD_DIM
Q_BLOCK = 128
GRID_W = 64
AXIS_ROPE_DIM = HEAD_DIM // 2
ROPE_THETA = 10000.0
POOL_WINDOWS = (2, 4, 8, 16)
N_POOL_GROUPS = len(POOL_WINDOWS)
POOL_GROUP_DIM = POOL_WIDTH // N_POOL_GROUPS
IN_PROJ_WIDTH = ATT_WIDTH + 2 * KV_WIDTH + POOL_WIDTH
D_FF = 2816
CONV_W = 3
N_MOD = 6
EPS = 1e-6


def rmsnorm(x, g):
    xf = x.astype(jnp.float32)
    y = xf * lax.rsqrt(jnp.mean(xf * xf, axis=-1, keepdims=True) + EPS)
    return (y * g.astype(jnp.float32)).astype(x.dtype)

def axial_rope_tables(T):
    rows = T // GRID_W
    row = jnp.repeat(jnp.arange(rows), GRID_W).astype(jnp.float32)
    col = jnp.tile(jnp.arange(GRID_W), rows).astype(jnp.float32)
    inv = 1.0 / (ROPE_THETA ** (jnp.arange(0, AXIS_ROPE_DIM, 2, dtype=jnp.float32) / AXIS_ROPE_DIM))
    ang_r = row[:, None] * inv[None, :]
    ang_c = col[:, None] * inv[None, :]
    return jnp.cos(ang_r), jnp.sin(ang_r), jnp.cos(ang_c), jnp.sin(ang_c)

def rotate_chunk(u, cos, sin):
    half = AXIS_ROPE_DIM // 2
    u1, u2 = u[..., :half], u[..., half:]
    cos = cos[None, :, None, :]
    sin = sin[None, :, None, :]
    return jnp.concatenate([u1 * cos - u2 * sin, u2 * cos + u1 * sin], axis=-1)

def apply_axial_rope(u, tables):
    cr, sr, cc, sc = tables
    uf = u.astype(jnp.float32)
    out = jnp.concatenate([rotate_chunk(uf[..., :AXIS_ROPE_DIM], cr, sr),
                           rotate_chunk(uf[..., AXIS_ROPE_DIM:], cc, sc)], axis=-1)
    return out.astype(u.dtype)

def blocked_gqa(q, k, v):
    B, T = q.shape[0], q.shape[1]
    nb = T // Q_BLOCK
    q = q * jnp.asarray(1.0 / math.sqrt(HEAD_DIM), q.dtype)
    qb = q.reshape(B, nb, Q_BLOCK, N_KV_HEADS, Q_PER_KV, HEAD_DIM).transpose(1, 0, 2, 3, 4, 5)

    def one_block(qblk):
        s = jnp.einsum('bqkgd,bskd->bkgqs', qblk, k).astype(jnp.float32)
        p = jax.nn.softmax(s, axis=-1).astype(v.dtype)
        return jnp.einsum('bkgqs,bskd->bqkgd', p, v)

    o = lax.map(one_block, qb)
    return o.transpose(1, 0, 2, 3, 4, 5).reshape(B, T, N_Q_HEADS * HEAD_DIM)

def centred_mean_minus_self(u, w):
    B, T, C = u.shape
    uf = u.astype(jnp.float32)
    S = jnp.concatenate([jnp.zeros((B, 1, C), jnp.float32), jnp.cumsum(uf, axis=1)], axis=1)
    t = jnp.arange(T)
    lo = jnp.maximum(t - w // 2, 0)
    hi = jnp.minimum(t + w // 2 - 1, T - 1)
    win = S[:, hi + 1] - S[:, lo]
    cnt = (hi - lo + 1).astype(jnp.float32)[None, :, None]
    return (win / cnt - uf).astype(u.dtype)

def pool_mixer(u, w_pool, pool_scale):
    B, T, _ = u.shape
    ug = u.reshape(B, T, N_POOL_GROUPS, POOL_GROUP_DIM)
    pooled = jnp.stack([centred_mean_minus_self(ug[:, :, g], POOL_WINDOWS[g])
                        for g in range(N_POOL_GROUPS)], axis=2)
    mixed = jnp.einsum('btgc,gcd->btgd', pooled, w_pool)
    return mixed.reshape(B, T, POOL_WIDTH) * pool_scale

def conv_gated_ffn(h, w_up, conv_w, conv_b, w_down):
    u = h @ w_up
    up = jnp.pad(u, ((0, 0), (1, 1), (0, 0)))
    u = up[:, :-2] * conv_w[0] + up[:, 1:-1] * conv_w[1] + up[:, 2:] * conv_w[2] + conv_b
    gate, val = u[..., :D_FF], u[..., D_FF:]
    return (jax.nn.silu(gate) * val) @ w_down

def first_inputs(seed: int = 0) -> dict:
    key = jax.random.key(seed)
    ks = jax.random.split(key, 16)
    f32 = jnp.float32
    nrm = lambda k, shape, s: jax.random.normal(k, shape, f32) * s
    return {
        "x": nrm(ks[0], (BATCH, SEQ, D_MODEL), 1.0),
        "c": nrm(ks[1], (BATCH, D_MODEL), 1.0),
        "w_ada": nrm(ks[2], (DEPTH, D_MODEL, N_MOD * D_MODEL), 0.5 * D_MODEL ** -0.5),
        "b_ada": nrm(ks[3], (DEPTH, N_MOD * D_MODEL), 0.01),
        "norm1_g": 1.0 + nrm(ks[4], (DEPTH, D_MODEL), 0.02),
        "w_in": nrm(ks[5], (DEPTH, D_MODEL, IN_PROJ_WIDTH), D_MODEL ** -0.5),
        "q_norm_g": 1.0 + nrm(ks[6], (DEPTH, HEAD_DIM), 0.02),
        "k_norm_g": 1.0 + nrm(ks[7], (DEPTH, HEAD_DIM), 0.02),
        "w_pool": nrm(ks[8], (DEPTH, N_POOL_GROUPS, POOL_GROUP_DIM, POOL_GROUP_DIM), POOL_GROUP_DIM ** -0.5),
        "pool_scale": 1.0 + nrm(ks[9], (DEPTH, POOL_WIDTH), 0.1),
        "w_out": nrm(ks[10], (DEPTH, MIX_WIDTH, D_MODEL), MIX_WIDTH ** -0.5),
        "norm2_g": 1.0 + nrm(ks[11], (DEPTH, D_MODEL), 0.02),
        "w_up": nrm(ks[12], (DEPTH, D_MODEL, 2 * D_FF), D_MODEL ** -0.5),
        "conv_w": nrm(ks[13], (DEPTH, CONV_W, 2 * D_FF), CONV_W ** -0.5),
        "conv_b": nrm(ks[14], (DEPTH, 2 * D_FF), 0.01),
        "w_down": nrm(ks[15], (DEPTH, D_FF, D_MODEL), D_FF ** -0.5),
    }

def first_block(x, c, w_ada, b_ada, norm1_g, w_in, q_norm_g, k_norm_g, w_pool, pool_scale,
              w_out, norm2_g, w_up, conv_w, conv_b, w_down):
    B, T, D = x.shape
    tables = axial_rope_tables(T)
    c_act = jax.nn.silu(c)
    for l in range(DEPTH):
        mod = c_act @ w_ada[l] + b_ada[l]
        sh1, sc1, g1, sh2, sc2, g2 = [m[:, None, :] for m in jnp.split(mod, N_MOD, axis=-1)]

        h = rmsnorm(x, norm1_g[l]) * (1.0 + sc1) + sh1
        proj = h @ w_in[l]
        o0 = ATT_WIDTH
        o1 = o0 + KV_WIDTH
        o2 = o1 + KV_WIDTH
        q = proj[..., :o0].reshape(B, T, N_Q_HEADS, HEAD_DIM)
        k = proj[..., o0:o1].reshape(B, T, N_KV_HEADS, HEAD_DIM)
        v = proj[..., o1:o2].reshape(B, T, N_KV_HEADS, HEAD_DIM)
        u_pool = proj[..., o2:]

        q = apply_axial_rope(rmsnorm(q, q_norm_g[l]), tables)
        k = apply_axial_rope(rmsnorm(k, k_norm_g[l]), tables)
        att = blocked_gqa(q, k, v)
        pool = pool_mixer(u_pool, w_pool[l], pool_scale[l])

        mix = jnp.concatenate([att, pool], axis=-1) @ w_out[l]
        x = x + g1 * mix

        h2 = rmsnorm(x, norm2_g[l]) * (1.0 + sc2) + sh2
        x = x + g2 * conv_gated_ffn(h2, w_up[l], conv_w[l], conv_b[l], w_down[l])
    return x


CTX_LEN = 256
W_CONV = 512
W_FNO = 512
N_FGROUPS = 4
N_HEADS = 8
W_ATTN = N_HEADS * HEAD_DIM
WIN_H = 8
WIN_W = 16
Q_BLOCK_W = 16
K_BLOCK_W = 2 * WIN_W
N_BRANCH = 3
NEG_INF = -1e30
D_IN = 4 * W_CONV + 2 * W_FNO + 4 * W_ATTN + N_BRANCH * D_MODEL
KV_LO = 4 * W_CONV + 2 * W_FNO + W_ATTN
KV_HI = KV_LO + 2 * W_ATTN


def rmsnorm_2(x, g):
    xf = x.astype(jnp.float32)
    y = xf * lax.rsqrt(jnp.mean(xf * xf, axis=-1, keepdims=True) + EPS)
    return (y * g.astype(jnp.float32)).astype(x.dtype)

def split_proj(p):
    sizes = (W_CONV,) * 4 + (W_FNO,) * 2 + (W_ATTN,) * 4 + (D_MODEL,) * N_BRANCH
    points = np.cumsum(sizes)[:-1].tolist()
    return jnp.split(p, points, axis=-1)

def heads(t):
    return t.reshape(t.shape[0], t.shape[1], N_HEADS, HEAD_DIM)

def short_conv(u, w_conv, b_conv):
    up = jnp.pad(u, ((0, 0), (1, 1), (0, 0)))
    return up[:, :-2] * w_conv[0] + up[:, 1:-1] * w_conv[1] + up[:, 2:] * w_conv[2] + b_conv

def fourier_mix(u):
    b, l, w = u.shape
    ug = u.reshape(b, l, N_FGROUPS, w // N_FGROUPS).astype(jnp.float32)
    y = jnp.fft.fft2(ug, axes=(1, 3), norm='ortho').real
    return y.reshape(b, l, w).astype(u.dtype)

def context_attention(q, k, v):
    s = jnp.einsum('bqhd,bkhd->bhqk', q, k).astype(jnp.float32) * (HEAD_DIM ** -0.5)
    p = jax.nn.softmax(s, axis=-1).astype(v.dtype)
    o = jnp.einsum('bhqk,bkhd->bqhd', p, v)
    return o.reshape(o.shape[0], o.shape[1], W_ATTN)

def neighbourhood_attention(q, k, v, k_ctx, v_ctx, rpb):
    b, s, h, dh = q.shape
    rows = s // GRID_W
    kh = min(WIN_H, rows)
    n_cb = GRID_W // Q_BLOCK_W
    scale = HEAD_DIM ** -0.5
    q = q.reshape(b, rows, n_cb, Q_BLOCK_W, h, dh)
    k = k.reshape(b, rows, GRID_W, h, dh)
    v = v.reshape(b, rows, GRID_W, h, dh)
    qcol = np.arange(GRID_W).reshape(n_cb, Q_BLOCK_W)
    kcs = np.clip(np.arange(n_cb) * Q_BLOCK_W - WIN_W // 2, 0, GRID_W - K_BLOCK_W)
    kcol = kcs[:, None] + np.arange(K_BLOCK_W)[None, :]
    cs = np.clip(qcol - WIN_W // 2, 0, GRID_W - WIN_W)
    col_ok = (kcol[:, None, :] >= cs[..., None]) & (kcol[:, None, :] < cs[..., None] + WIN_W)
    dc_idx = np.clip(kcol[:, None, :] - qcol[..., None] + WIN_W - 1, 0, 2 * WIN_W - 2)
    rpb_col = rpb[:, :, dc_idx]
    mask = col_ok[:, :, None, :]

    def row_block(r):
        rs = jnp.clip(r - kh // 2, 0, rows - kh)
        qr = lax.dynamic_index_in_dim(q, r, axis=1, keepdims=False)
        kb = lax.dynamic_slice_in_dim(k, rs, kh, axis=1)[:, :, kcol]
        vb = lax.dynamic_slice_in_dim(v, rs, kh, axis=1)[:, :, kcol]
        dr_idx = rs + jnp.arange(kh) - r + (WIN_H - 1)
        bias = jnp.take(rpb_col, dr_idx, axis=1).transpose(0, 2, 3, 1, 4).astype(jnp.float32)
        s_loc = jnp.einsum('bnqhd,binchd->bhnqic', qr, kb).astype(jnp.float32) * scale + bias
        s_loc = jnp.where(mask, s_loc, NEG_INF)
        s_ctx = jnp.einsum('bnqhd,bkhd->bhnqk', qr, k_ctx).astype(jnp.float32) * scale
        n_loc = kh * K_BLOCK_W
        sc = jnp.concatenate([s_loc.reshape(b, h, n_cb, Q_BLOCK_W, n_loc), s_ctx], axis=-1)
        p = jax.nn.softmax(sc, axis=-1).astype(v.dtype)
        p_loc = p[..., :n_loc].reshape(b, h, n_cb, Q_BLOCK_W, kh, K_BLOCK_W)
        p_ctx = p[..., n_loc:]
        return (jnp.einsum('bhnqic,binchd->bnqhd', p_loc, vb)
                + jnp.einsum('bhnqk,bkhd->bnqhd', p_ctx, v_ctx))

    o = lax.map(row_block, jnp.arange(rows))
    return o.transpose(1, 0, 2, 3, 4, 5).reshape(b, s, W_ATTN)

def merge_branches(pieces, attn_o, w_conv, b_conv, w_br_a, w_br_f, w_br_c, w_out):
    a_x, a_b, a_c, a_z, f_u, f_z, _q, _k, _v, c_z, g_a, g_f, g_c = pieces
    silu, sig = jax.nn.silu, jax.nn.sigmoid
    y_a = (a_b * short_conv(a_c * a_x, w_conv, b_conv) * silu(a_z)) @ w_br_a
    y_f = (fourier_mix(f_u) * silu(f_z)) @ w_br_f
    y_c = (attn_o * silu(c_z)) @ w_br_c
    return (sig(g_a) * y_a + sig(g_f) * y_f + sig(g_c) * y_c) @ w_out

def hybrid_layer(x, ctx, c, c_ctx, norm_g, w_ada, b_ada, w_in, b_in, w_conv, b_conv,
                 rpb, w_br_a, w_br_f, w_br_c, w_out, update_ctx):
    mod_l = jax.nn.silu(c) @ w_ada + b_ada
    mod_c = jax.nn.silu(c_ctx) @ w_ada + b_ada
    sh_l, sc_l, gt_l = jnp.split(mod_l[:, None, :], 3, axis=-1)
    sh_c, sc_c, gt_c = jnp.split(mod_c, 3, axis=-1)
    h_lat = rmsnorm_2(x, norm_g) * (1.0 + sc_l) + sh_l
    h_ctx = rmsnorm_2(ctx, norm_g) * (1.0 + sc_c) + sh_c

    pl = split_proj(h_lat @ w_in + b_in)
    if update_ctx:
        pc = split_proj(h_ctx @ w_in + b_in)
        k_c, v_c = pc[7], pc[8]
    else:
        k_c, v_c = jnp.split(h_ctx @ w_in[:, KV_LO:KV_HI] + b_in[KV_LO:KV_HI], 2, axis=-1)
    k_c, v_c = heads(k_c), heads(v_c)

    o_lat = neighbourhood_attention(heads(pl[6]), heads(pl[7]), heads(pl[8]), k_c, v_c, rpb)
    x_new = x + gt_l * merge_branches(pl, o_lat, w_conv, b_conv, w_br_a, w_br_f, w_br_c, w_out)
    if update_ctx:
        o_ctx = context_attention(heads(pc[6]), k_c, v_c)
        ctx = ctx + gt_c * merge_branches(pc, o_ctx, w_conv, b_conv, w_br_a, w_br_f, w_br_c, w_out)
    return x_new, ctx

def second_inputs(seed: int = 0) -> dict:
    key = jax.random.key(seed)
    ks = jax.random.split(key, 17)
    f32 = jnp.float32
    nrm = lambda k, shape, s: jax.random.normal(k, shape, f32) * s
    return {
        'x': nrm(ks[0], (BATCH, SEQ, D_MODEL), 1.0),
        'c': nrm(ks[1], (BATCH, D_MODEL), 1.0),
        'ctx': nrm(ks[2], (BATCH, CTX_LEN, D_MODEL), 1.0),
        'c_ctx': nrm(ks[3], (D_MODEL,), 1.0),
        'norm_g': 1.0 + nrm(ks[4], (DEPTH, D_MODEL), 0.05),
        'w_ada': nrm(ks[5], (DEPTH, D_MODEL, 3 * D_MODEL), 0.5 * D_MODEL ** -0.5),
        'b_ada': nrm(ks[6], (DEPTH, 3 * D_MODEL), 0.01),
        'w_in': nrm(ks[7], (DEPTH, D_MODEL, D_IN), D_MODEL ** -0.5),
        'b_in': nrm(ks[8], (DEPTH, D_IN), 0.01),
        'w_conv': nrm(ks[9], (DEPTH, 3, W_CONV), 3 ** -0.5),
        'b_conv': nrm(ks[10], (DEPTH, W_CONV), 0.01),
        'rpb': nrm(ks[11], (DEPTH, N_HEADS, 2 * WIN_H - 1, 2 * WIN_W - 1), 0.1),
        'w_br_a': nrm(ks[12], (DEPTH, W_CONV, D_MODEL), W_CONV ** -0.5),
        'w_br_f': nrm(ks[13], (DEPTH, W_FNO, D_MODEL), W_FNO ** -0.5),
        'w_br_c': nrm(ks[14], (DEPTH, W_ATTN, D_MODEL), W_ATTN ** -0.5),
        'w_out': nrm(ks[15], (DEPTH, D_MODEL, D_MODEL), D_MODEL ** -0.5),
        'final_g': 1.0 + nrm(ks[16], (D_MODEL,), 0.05),
    }

def second_block(x, c, ctx, c_ctx, norm_g, w_ada, b_ada, w_in, b_in, w_conv, b_conv,
              rpb, w_br_a, w_br_f, w_br_c, w_out, final_g):
    for l in range(DEPTH):
        x, ctx = hybrid_layer(x, ctx, c, c_ctx, norm_g[l], w_ada[l], b_ada[l], w_in[l], b_in[l],
                              w_conv[l], b_conv[l], rpb[l], w_br_a[l], w_br_f[l], w_br_c[l],
                              w_out[l], update_ctx=(l < DEPTH - 1))
    return rmsnorm_2(x, final_g)


def setup_inputs(seed=0):
    out = dict(first_inputs(seed))
    for name, value in second_inputs(seed + 1).items():
        if name != "x":
            out[name + "_2"] = value
    return out


def reference(
    x, c, w_ada, b_ada, norm1_g, w_in, q_norm_g, k_norm_g, w_pool, pool_scale, w_out, norm2_g,
    w_up, conv_w, conv_b, w_down, c_2, ctx_2, c_ctx_2, norm_g_2, w_ada_2, b_ada_2, w_in_2,
    b_in_2, w_conv_2, b_conv_2, rpb_2, w_br_a_2, w_br_f_2, w_br_c_2, w_out_2, final_g_2,
):
    x = first_block(
        x, c, w_ada, b_ada, norm1_g, w_in, q_norm_g, k_norm_g, w_pool, pool_scale, w_out,
        norm2_g, w_up, conv_w, conv_b, w_down,
    )
    return second_block(
        x, c_2, ctx_2, c_ctx_2, norm_g_2, w_ada_2, b_ada_2, w_in_2, b_in_2, w_conv_2, b_conv_2,
        rpb_2, w_br_a_2, w_br_f_2, w_br_c_2, w_out_2, final_g_2,
    )


_drawn_inputs = setup_inputs


def setup_inputs(seed=0):
    import zlib

    import numpy as np

    out = dict(_drawn_inputs(seed))
    spreads = {}
    factors = {'b_ada': 5.099,
     'norm1_g': 8.0,
     'q_norm_g': 8.0,
     'k_norm_g': 8.0,
     'pool_scale': 2.876,
     'norm2_g': 8.0,
     'conv_b': 8.0,
     'ctx_2': 6.136,
     'c_ctx_2': 2.859,
     'norm_g_2': 3.98,
     'b_ada_2': 8.0,
     'b_in_2': 8.0,
     'b_conv_2': 64.0,
     'rpb_2': 200.0}
    for name, (base, spread) in spreads.items():
        noise = np.random.default_rng([zlib.crc32(name.encode()), seed]).standard_normal(out[name].shape)
        drawn = base * np.exp(spread * noise) if base else spread * noise
        out[name] = __import__('jax').numpy.asarray(drawn.astype(out[name].dtype))
    for name, factor in factors.items():
        out[name] = (out[name] * factor).astype(out[name].dtype)
    return out
```

```python
import math
from contextlib import ExitStack, contextmanager

import numpy as np

import concourse.bass as bass
from concourse import mybir

F32 = mybir.dt.float32
F32R = mybir.dt.float32r
ACT = mybir.ActivationFunctionType
ALU = mybir.AluOpType
AX = mybir.AxisListType

P = 128
D = 1024
T = 1024
KD = D // P
TT = T // P
HALF = 512
HD = 64
NQ, NKV = 8, 2
FF = 2816
FC = FF // P
GROUPS = (8, 8, 6)
POOL_W = (2, 4, 8, 16)
GRID = 64
ROWS = T // GRID
CTX = 256
KH, KW, QW = 8, 32, 16
NLOC = 12 * KW
NB = GRID // QW
EPS = 1e-6
NEG = -1e30
FEW = 16
KCS = [min(max(n * QW - 8, 0), GRID - KW) for n in range(NB)]
KIND = [0, 1, 1, 2]
SCALE = HD ** -0.5

NKEY = NLOC + CTX
NCH = 4 * NB + 2
NDFT = 2 * 4 * HALF + 2 * P + HALF

N_IN, N_OUT1 = 0, 14
MIXES = {8: 0, 10: 1, 12: 2, 13: 3}
POOLS = {6: 0, 7: 1, 9: 2, 11: 3}
N_UP, N_DOWN = [], []
_n = N_OUT1 + KD
for _g in GROUPS:
    N_UP.append(_n)
    N_DOWN.append(_n + 2 * _g)
    _n += 2 * _g + KD
N_ATT2 = _n
N_F = N_ATT2 + 16
N_GF = N_F + 8
N_GC = N_GF + 16
N_A = N_GC + 16
N_GA = N_A + 16
N_OUT2 = N_GA + 16
N_ALL = N_OUT2 + KD

_VECS = [("b_ada", 48), ("norm1_g", 8), ("pool_scale", 4), ("norm2_g", 8), ("conv_w", 132), ("conv_b", 44),
         ("b_ada_2", 24), ("norm_g_2", 8), ("b_in_2", 64), ("w_conv_2", 12), ("b_conv_2", 4), ("final_g_2", 8),
         ("c", 8), ("c_2", 16), ("q_norm_g", 1), ("k_norm_g", 1)]
VCOL, NVEC = {}, 0
for _name, _w in _VECS:
    VCOL[_name] = NVEC
    NVEC += _w
_CONSTS = [("ident", 128), ("headmean", 128), ("rot", 128), ("headsel", 2), ("one", 1), ("eps", 1), ("zero", 1), ("edge", 64)]
CCOL, NCONST = {}, 0
for _name, _w in _CONSTS:
    CCOL[_name] = NCONST
    NCONST += _w


class Steps:

    def __init__(self, eng, sem):
        self.eng, self.sem, self.done, self.before = eng, sem, 0, 0

    def did(self, ins):
        ins.then_inc(self.sem, 1)
        self.done += 1

    def settle(self):
        self.eng.wait_ge(self.sem, self.before + self.done)

    @contextmanager
    def loop(self, count, each):
        first = self.done
        with self.eng.Fori(0, count) as it:
            self.before = it * each
            yield it
        assert self.done - first == each, (self.done - first, each)
        self.before, self.done = 0, first + count * each


def build(nc, A, out):
    ctx = ExitStack()
    with ctx:
        BASE = 16512

        def at(name, kb, shape, dt=F32):
            return nc.alloc_sbuf_tensor_at(name, shape, dt, offset=BASE + int(kb * 1024))

        def sem(name):
            return ctx.enter_context(nc.semaphore(name))

        XT = at("XT", 0, [P, KD, T])
        QN = at("QN", 0, [P, 4, T])
        KN = at("KN", 16, [P, T])
        VN = at("VN", 20, [P, T])
        ROPE1 = at("ROPE1", 24, [P, T])
        ROPE2 = at("ROPE2", 28, [P, T])
        KHI = at("KHI", 24, [P, T], F32R)
        KLO = at("KLO", 28, [P, T])
        QST = [at(f"QST{s}", 24 + 4 * s, [P, NQ, P], F32R) for s in range(2)]
        HH = at("HH", 32, [P, KD, T], F32R)
        HL = at("HL", 64, [P, KD, T], F32R)
        SQ = [at(f"SQ{s}", 64 + 4 * s, [P, T]) for s in range(2)]
        PTH = at("PTH", 32, [P, TT, 4, P], F32R)
        PTL = at("PTL", 48, [P, TT, 4, P], F32R)
        EX = [at(f"EX{s}", 64 + 4 * s, [P, T]) for s in range(2)]
        VTOK = at("VTOK", 72, [P, TT, NKV, P], F32R)
        AR = [at(f"AR{s}", 80 + 4 * s, [P, KD, P]) for s in range(2)]
        QH = at("QH", 88, [P, 4, P], F32R)
        QL = at("QL", 90, [P, 4, P])
        OT = at("OT", 92, [P, 4, P])
        OTMP = at("OTMP", 94, [P, HALF])
        WADA = at("WADA", 96, [P, 4, KD, 4 * P])
        MH = at("MH", 96, [P, KD, T], F32R)
        ML = at("ML", 128, [P, KD, T], F32R)
        COS = at("COS", 96, [P, T])
        SIN = at("SIN", 100, [P, T])
        PLH = at("PLH", 104, [P, T], F32R)
        PLL = at("PLL", 108, [P, T], F32R)
        PAD = 8
        UP = at("UP", 128, [P, T + 2 * PAD])
        WINS = [at("WIN0", 132.5, [P, T + 2 * PAD]), at("WIN1", 137, [P, T + 2 * PAD])]
        GH = at("GH", 96, [P, 8, T], F32R)
        GL = at("GL", 128, [P, 8, T], F32R)
        CX = at("CX", 152, [P, KD, CTX])
        SQC = at("SQC", 120, [P, KD, CTX])
        HCH = at("HCH", 120, [P, KD, CTX], F32R)
        HCL = at("HCL", 152, [P, KD, CTX], F32R)
        BIAS = [at(f"BIAS{j}", 9 * j, [P, 6, NLOC]) for j in range(2)]
        VTOK2 = at("VTOK2", 18, [P, NCH, P])
        DG = [at(f"DG{s}", 27 + 0.5 * s, [P, P]) for s in range(2)]
        PT2 = [at("PT20", 28, [P, NKEY]), at("PT21", 117, [P, NKEY])]
        EX2 = [at(f"EX2{s}", 112 + 2.5 * s, [P, NKEY]) for s in range(2)]
        Q2 = at("Q2", 128, [P, T])
        K2 = at("K2", 132, [P, T + CTX])
        SZ = at("SZ", 137, [P, T])
        VT2 = at("VT2", 141, [P, NB * ROWS * KW + CTX])
        CBF = at("CBF", 96, [P, 4, T])
        DFT = at("DFT", 0, [P, NDFT])
        VW = at("VW", 20, [P, 8, P])
        VROW = at("VROW", 24, [P, P])
        FE = at("FE", 25, [P, HALF + 1])
        FO = at("FO", 27.25, [P, HALF])
        SB = at("SB", 29.25, [P, HALF])
        ALT = at("ALT", 31.25, [P, 4])
        BRH = at("BRH", 128, [P, 4, T], F32R)
        BRL = at("BRL", 144, [P, 4, T], F32R)
        CBL = at("CBL", 96, [P, 4, T], F32R)
        CBH = at("CBH", 112, [P, 4, T], F32R)
        S = at("S", 0, [P, KD, T])
        SL = at("SL", 0, [P, KD, T], F32R)
        SH = at("SH", 96, [P, KD, T], F32R)
        XT2 = at("XT2", 32, [P, KD, T])
        WF = [at(f"WF{s}", 160 + 4 * s, [P, KD, P]) for s in range(2)]
        WH = [at(f"WH{s}", 168 + 4 * s, [P, KD, P], F32R) for s in range(2)]
        WL = [at(f"WL{s}", 176 + 4 * s, [P, KD, P], F32R) for s in range(2)]
        EV = [at(f"EV{s}", 184 + 4 * s, [P, T]) for s in range(2)]
        CV = [at(f"CV{s}", 192 + 4 * s, [P, T]) for s in range(2)]
        KSH = at("KSH", 184, [P, NKV, T], F32R)
        KSL = at("KSL", 192, [P, NKV, T], F32R)
        VEC = at("VEC", 200, [P, NVEC])
        CON = at("CON", 200 + 1.5625, [P, NCONST])
        small = 200 + 1.5625 + 1.8125
        MOD1 = at("MOD1", small, [P, 48])
        MOD2 = at("MOD2", small + 0.1875, [P, 24, 2])
        A1 = at("A1", small + 0.375, [P, KD])
        A2 = at("A2", small + 0.40625, [P, KD])
        A3 = at("A3", small + 0.4375, [P, KD, 2])
        SC1 = at("SC1", small + 0.5, [P, KD])
        SC2 = at("SC2", small + 0.53125, [P, KD, 2])
        SD = at("SD", small + 0.59375, [P, TT])
        RS = at("RS", small + 0.625, [P, TT])
        QSD = at("QSD", small + 0.65625, [P, TT, NQ])
        RSP = at("RSP", small + 0.90625, [P, TT, NQ])
        RSN = at("RSN", small + 1.15625, [P, TT, NQ])
        MX = at("MX", small + 1.40625, [P, 8])
        NBI = at("NBI", small + 1.4375, [P, 8])
        SUM = at("SUM", small + 1.46875, [P, 8])
        RC = at("RC", small + 1.5, [P, 8])
        BQ8 = at("BQ8", small + 1.53125, [P, 8])

        def vec(name, j=0, w=1):
            c = VCOL[name] + j
            return VEC[:, c:c + w] if isinstance(j, int) else VEC[:, bass.ds(c, w)]

        def con(name, w, j=0):
            return CON[:, CCOL[name] + j:CCOL[name] + j + w]

        ident, one, eps, zero = con("ident", P), con("one", 1), con("eps", 1), con("zero", 1)

        acc = ctx.enter_context(nc.psum_tensor("acc", [P, 2, T], F32))
        turn = ctx.enter_context(nc.psum_tensor("turn", [P, T], F32))
        bank6 = ctx.enter_context(nc.psum_tensor("bank6", [P, HALF], F32))
        bank7 = ctx.enter_context(nc.psum_tensor("bank7", [P, HALF], F32))

        consts_in, x_in, rope_in = sem("consts_in"), sem("x_in"), sem("rope_in")
        ada_first = [sem(f"ada_first{j}") for j in range(4)]
        w_in = [sem("w_in0"), sem("w_in1")]
        w_hi, w_split = sem("w_hi"), sem("w_split")
        acc_done, acc_read, post_done = sem("acc_done"), sem("acc_read"), sem("post_done")
        act_step, dve_step, pool_step = sem("act_step"), sem("dve_step"), sem("pool_step")
        sq_ready, sq_used = sem("sq_ready"), sem("sq_used")
        sd_ready, rs_ready, rb_done = sem("sd_ready"), sem("rs_ready"), sem("rb_done")
        xn_ready, hf_ready, hh_ready, hl_ready = sem("xn_ready"), sem("hf_ready"), sem("hh_ready"), sem("hl_ready")
        silu_ready, mod1_done, mods_ready = sem("silu_ready"), sem("mod1_done"), sem("mods_ready")
        sqh_ready, qstat_done, rot_done, kms_done = sem("sqh_ready"), sem("qstat_done"), sem("rot_done"), sem("kms_done")
        ksd_ready, qsd_ready, pooled, plh_ready, pll_ready = (
            sem("ksd_ready"), sem("qsd_ready"), sem("pooled"), sem("plh_ready"), sem("pll_ready"))
        mixh_ready = sem("mixh_ready")
        khi_ready, klo_ready, kst_act, kst_dve = sem("khi_ready"), sem("klo_ready"), sem("kst_act"), sem("kst_dve")
        vt_done, vh_ready, vl_ready = sem("vt_done"), sem("vh_ready"), sem("vl_ready")
        qh_ready, qst_act, qst_dve = sem("qh_ready"), sem("qst_act"), sem("qst_dve")
        scores_done, nb_ready, exp_done, rc_ready, p_ready = (
            sem("scores_done"), sem("nb_ready"), sem("exp_done"), sem("rc_ready"), sem("p_ready"))
        pt_done, pth_ready, ptl_ready, pv_done, otmp_ready, o_ready, mh_ready, ml_ready = (
            sem("pt_done"), sem("pth_ready"), sem("ptl_ready"), sem("pv_done"), sem("otmp_ready"), sem("o_ready"),
            sem("mh_ready"), sem("ml_ready"))
        ada_in, ada_done, ada_read = [sem("ada_in0"), sem("ada_in1")], sem("ada_done"), sem("ada_read")
        x_again = [sem(f"x_again{k}") for k in range(KD)]
        gated, gh_ready = sem("gated"), sem("gh_ready")
        silu_done = sem("silu_done")
        cx_in, csq_ready, cstat_done, csd_ready, crs_ready, crb_done = (
            sem("cx_in"), sem("csq_ready"), sem("cstat_done"), sem("csd_ready"), sem("crs_ready"), sem("crb_done"))
        cxn_ready, ch_ready, hch_ready, hcl_ready = sem("cxn_ready"), sem("ch_ready"), sem("hch_ready"), sem("hcl_ready")
        x_saved, x_back = sem("x_saved"), sem("x_back")
        bias_in = [sem("bias_in0"), sem("bias_in1")]
        vt2_done, vtok2_ready = sem("vt2_done"), sem("vtok2_ready")
        scores2_done, nb2_ready, exp2_done, dg_ready, pt2_done, pt2_ready, pv2_done, o2_ready = (
            sem("scores2_done"), sem("nb2_ready"), sem("exp2_done"), sem("dg_ready"), sem("pt2_done"), sem("pt2_ready"),
            sem("pv2_done"), sem("o2_ready"))
        cbh_ready, cbl_ready = sem("cbh_ready"), sem("cbl_ready")
        dft_in, fold_ready, chan_done, vw_ready, seq_done, sb_ready, y_ready, brh_ready = (
            sem("dft_in"), sem("fold_ready"), sem("chan_done"), sem("vw_ready"), sem("seq_done"), sem("sb_ready"),
            sem("y_ready"), sem("brh_ready"))
        sums_ready, sh_ready = sem("sums_ready"), sem("sh_ready")
        out_ready, out_sent = sem("out_ready"), sem("out_sent")

        block = ctx.enter_context(nc.Block())

        @block.sync
        def _(sp):
            def load_w(n, slot, name, index, k, first=False):
                if not first:
                    sp.wait_ge(w_split, n - 1)
                sp.dma_start(WF[slot][:, 0:k, :], A[name][index, :, :].rearrange("p (k n) -> p k n", n=P)
                             if isinstance(index, int) else
                             A[name][bass.ds(index, 1), :, :].rearrange("a p (k n) -> (a p) k n", n=P)
                             ).then_inc(w_in[slot], 16)

            sp.dma_start(VEC[:, :], A["vecs"]).then_inc(consts_in, 16)
            sp.dma_start(CON[:, :], A["consts"]).then_inc(consts_in, 16)
            for j in range(2):
                sp.dma_start(WADA[:, 2 * j], A["ada_head"][2 * j]).then_inc(ada_first[2 * j], 16)
                sp.dma_start(WADA[:, 2 * j + 1], A["ada_head"][2 * j + 1]).then_inc(ada_first[2 * j + 1], 16)
                if j == 0:
                    sp.dma_start(XT[:, :, :], A["xT"].rearrange("k p t -> p k t")).then_inc(x_in, 16)
            w8 = 0
            for n in range(2):
                load_w(n, n % 2, "w8", w8, KD, first=True)
                w8 += 1
            sp.wait_ge(mod1_done, 4)
            sp.dma_start(COS[:, :], A["rope"][0]).then_inc(rope_in, 16)
            sp.dma_start(SIN[:, :], A["rope"][1]).then_inc(rope_in, 16)
            for n in range(2, N_OUT1 + 2):
                if n in MIXES:
                    load_w(n, n % 2, "w1", MIXES[n], 1)
                else:
                    load_w(n, n % 2, "w8", w8, KD)
                    w8 += 1
            sp.wait_ge(acc_done, N_OUT1)
            sp.wait_ge(hl_ready, KD)
            with sp.Fori(0, 4) as it:
                for j in range(14):
                    s, h = j // 7, j % 7
                    i1 = it * 8 + (16 + 4 * s + h) if h < 4 else it * 6 + (48 + 3 * s + h - 4)
                    src = A["ada"][bass.ds(i1, 1), :, :].rearrange("a p (k n) -> (a p) k n", n=P)
                    sp.wait_ge(ada_done, it * 14 + (j + 1))
                    sp.dma_start(AR[j % 2][:, :, :], src).then_inc(ada_in[j % 2], 16)
            sp.wait_ge(pv_done, 16)
            for k in range(KD):
                sp.dma_start(XT[:, k, :], A["xT"][k]).then_inc(x_again[k], 16)
            with sp.Fori(0, 3) as it:
                for s in range(2):
                    load_w(it * 2 + (N_OUT1 + 2 + s), s, "w8", it * 2 + (w8 + s), KD)
            w8 += 6
            for g, gk in enumerate(GROUPS):
                with sp.Fori(0, gk) as it:
                    for s in range(2):
                        load_w(it * 2 + (N_UP[g] + s), s, "w8", it * 2 + (w8 + s), KD)
                w8 += 2 * gk
                if g == 2:
                    sp.wait_ge(acc_done, N_UP[2])
                    sp.dma_start(CX[:, :, :], A["ctxT"].rearrange("k p t -> p k t")).then_inc(cx_in, 16)
                name, first = ("w8", w8) if gk == KD else ("w6", 0)
                with sp.Fori(0, 4) as it:
                    for s in range(2):
                        load_w(it * 2 + (N_DOWN[g] + s), s, name, it * 2 + (first + s), gk)
                if gk == KD:
                    w8 += KD
            for s in range(2):
                load_w(N_ATT2 + s, s, "w8", w8 + s, KD)
            sp.wait_ge(post_done, N_ATT2)
            sp.dma_start(out.rearrange("k p t -> p k t"), XT[:, :, :]).then_inc(x_saved, 16)
            sp.wait_ge(x_saved, 16)
            sp.wait_ge(xn_ready, 3 * KD)
            for j in range(2):
                sp.dma_start(BIAS[j][:, :, :], A["bias"][j]).then_inc(bias_in[j], 16)
            for s in range(2):
                load_w(N_ATT2 + 2 + s, s, "w8", w8 + 2 + s, KD)
            with sp.Fori(1, 4) as it:
                for s in range(2):
                    load_w(it * 4 + (N_ATT2 + s), s, "w8", it * 4 + (w8 + s), KD)
                for j in range(2):
                    src = A["bias"][bass.ds(it * 2 + j, 1), :, :, :].rearrange("a p k n -> (a p) k n")
                    sp.wait_ge(nb2_ready, it * 16 + (8 * j - 8))
                    sp.dma_start(BIAS[j][:, :, :], src).then_inc(bias_in[j], 16)
                for s in range(2):
                    load_w(it * 4 + (N_ATT2 + 2 + s), s, "w8", it * 4 + (w8 + 2 + s), KD)
            w8 += 16
            for s in range(2):
                load_w(N_F + s, s, "w8", w8 + s, KD)
            sp.wait_ge(nb2_ready, 64)
            sp.wait_ge(pt2_done, 64)
            sp.wait_ge(pv2_done, 64)
            sp.dma_start(DFT[:, :], A["dft"]).then_inc(dft_in, 16)
            with sp.Fori(1, 4) as it:
                for s in range(2):
                    load_w(it * 2 + (N_F + s), s, "w8", it * 2 + (w8 + s), KD)
            w8 += 8

            def gate_weights(n0, w8, w4):
                with sp.Fori(0, KD) as it:
                    load_w(it * 2 + n0, 0, "w8", it + w8, KD)
                    load_w(it * 2 + (n0 + 1), 1, "w4", it + w4, 4)

            gate_weights(N_GF, w8, 0)
            gate_weights(N_GC, w8 + KD, KD)
            w8 += 2 * KD
            with sp.Fori(0, 8) as it:
                for s in range(2):
                    load_w(it * 2 + (N_A + s), s, "w8", it * 2 + (w8 + s), KD)
            w8 += 16
            gate_weights(N_GA, w8, 2 * KD)
            w8 += KD
            for s in range(2):
                load_w(N_OUT2 + s, s, "w8", w8 + s, KD)
            sp.wait_ge(acc_done, N_OUT2 - 1)
            sp.dma_start(XT2[:, :, :], out.rearrange("k p t -> p k t")).then_inc(x_back, 16)
            with sp.Fori(1, 4) as it:
                for s in range(2):
                    load_w(it * 2 + (N_OUT2 + s), s, "w8", it * 2 + (w8 + s), KD)
            for k in range(KD):
                sp.wait_ge(out_ready, k + 1)
                sp.dma_start(out[k], XT2[:, k, :]).then_inc(out_sent, 16)
            sp.wait_ge(out_sent, 16 * KD)

        @block.gpsimd
        def _(pool):
            steps = Steps(pool, pool_step)

            def split_w(n, slot, k, first=False):
                pool.wait_ge(w_in[slot], (n - slot) * 8 + 16)
                if not first:
                    pool.wait_ge(acc_done, n - 1)
                f, h = WF[slot][:, :, :].rearrange("p k n -> p (k n)"), WH[slot][:, :, :].rearrange("p k n -> p (k n)")
                pool.tensor_tensor(h[:, 0:FEW], f[:, 0:FEW], zero.to_broadcast([P, FEW]), ALU.add).then_inc(w_hi, 1)
                pool.tensor_scalar(h[:, FEW:k * P], f[:, FEW:k * P], 1.0, 1.0, ALU.mult, ALU.mult).then_inc(w_hi, 1)
                pool.wait_ge(w_hi, n * 2 + 2)
                pool.tensor_tensor(WL[slot][:, 0:k, :], WF[slot][:, 0:k, :], WH[slot][:, 0:k, :].bitcast(F32),
                                   ALU.subtract).then_inc(w_split, 1)

            pool.wait_ge(consts_in, 32)
            for n in range(N_OUT1 + 2):
                split_w(n, n % 2, 1 if n in MIXES else KD, first=n < 2)
            with pool.Fori(0, 4) as it:
                for u in range(16):
                    pool.wait_ge(rc_ready, it * 16 + (u + 1))
                    rc = RC[:, u % 2:u % 2 + 1]
                    e = EX[u % 2]
                    pool.tensor_tensor(e[:, 0:FEW], e[:, 0:FEW], rc.to_broadcast([P, FEW]), ALU.mult)
                    pool.tensor_scalar(e[:, FEW:], e[:, FEW:], rc, 1.0, ALU.mult, ALU.mult).then_inc(p_ready, 1)
            with pool.Fori(0, 3) as it:
                for s in range(2):
                    split_w(it * 2 + (N_OUT1 + 2 + s), s, KD)
            for g, gk in enumerate(GROUPS):
                with pool.Fori(0, gk) as it:
                    for s in range(2):
                        split_w(it * 2 + (N_UP[g] + s), s, KD)
                with pool.Fori(0, 4) as it:
                    for s in range(2):
                        split_w(it * 2 + (N_DOWN[g] + s), s, gk)
            for n0, count, k1 in ((N_ATT2, 12, KD), (N_GF, 16, 4), (N_A, 8, KD), (N_GA, 8, 4), (N_OUT2, 4, KD)):
                with pool.Fori(0, count) as it:
                    split_w(it * 2 + n0, 0, KD)
                    split_w(it * 2 + (n0 + 1), 1, k1)

        @block.tensor
        def _(pe):
            def gemm(n, slot, hi, lo, k_n=KD, ready=None, context=None):
                pe.wait_ge(w_split, n + 1)
                if not isinstance(n, int) or n >= 2:
                    pe.wait_ge(acc_read, n - 1)
                for k in range(k_n):
                    if ready is not None:
                        pe.wait_ge(ready, hl_base[0] + k + 1)
                    for w, x in ((WH, hi), (WH, lo), (WL, hi)):
                        for c in range(2):
                            last = pe.matmul(acc[:, slot, HALF * c:HALF * c + HALF], w[slot][:, k, :],
                                             x[:, k, HALF * c:HALF * c + HALF],
                                             start=(k == 0 and w is WH and x is hi), stop=(k == k_n - 1 and w is WL))
                if context is not None:
                    for k in range(k_n):
                        for w, x in ((WH, HCH), (WH, HCL), (WL, HCH)):
                            last = pe.matmul(context[:, 0:CTX], w[slot][:, k, :], x[:, k, :],
                                             start=(k == 0 and w is WH and x is HCH), stop=(k == k_n - 1 and w is WL))
                last.then_inc(acc_done, 1)

            hl_base = [0]

            def stats(q, k, first, last, nt=TT):
                pe.wait_ge(sq_ready, q * KD + k + 1)
                for t in range(nt):
                    mm = pe.matmul(bank6[:, t:t + 1], SQ[slot_of(k)][:, P * t:P * t + P], one,
                                   start=(first and t == 0), stop=last, skip_group_check=True)
                mm.then_inc(sq_used, 1)

            slot_now = [0]

            def slot_of(k):
                return k % 2 if isinstance(k, int) else slot_now[0]

            def spread_rs(q, nt=TT):
                pe.wait_ge(rs_ready, q + 1)
                for t in range(nt):
                    mm = pe.matmul(turn[:, P * t:P * t + P], RS[:, t:t + 1].to_broadcast([P, P]), ident,
                                   start=True, stop=True)
                mm.then_inc(rb_done, 1)

            pe.wait_ge(consts_in, 32)
            pe.wait_ge(silu_ready, 1)
            for j in range(4):
                pe.wait_ge(ada_first[j], 16)
                for b in range(4):
                    for k in range(KD):
                        mm = pe.matmul(bank7[:, 4 * j + b:4 * j + b + 1], WADA[:, j, k, P * b:P * b + P],
                                       SC1[:, k:k + 1], start=(k == 0), stop=(k == KD - 1))
                    if j == 0 and b < 2:
                        mm.then_inc(ada_done, 1)
                mm.then_inc(mod1_done, 1)
                if j == 1:
                    for k in range(KD):
                        stats(0, k, k == 0, k == KD - 1)
                if j == 2:
                    spread_rs(0)

            def rotate(m):
                n = [0, 2, 3, 4, 5][m]
                pe.wait_ge(sqh_ready, m + 1)
                if m == 0:
                    for c in range(2):
                        mm = pe.matmul(turn[:, HALF * c:HALF * c + HALF], con("headmean", P),
                                       CV[n % 2][:, HALF * c:HALF * c + HALF], start=True, stop=True)
                    mm.then_inc(kms_done, 1)
                    pe.wait_ge(ksd_ready, 1)
                else:
                    for t in range(TT):
                        mm = pe.matmul(bank6[:, 64 + t * NQ + 2 * (m - 1):64 + t * NQ + 2 * m],
                                       CV[n % 2][:, P * t:P * t + P], con("headsel", 2), start=True, stop=True)
                    mm.then_inc(qstat_done, 1)
                if m > 0:
                    pe.wait_ge(post_done, [0, 2, 3, 4, 5][m - 1] + 1)
                for c in range(2):
                    mm = pe.matmul(turn[:, HALF * c:HALF * c + HALF], con("rot", P), EV[n % 2][:, HALF * c:HALF * c + HALF],
                                   start=True, stop=True)
                mm.then_inc(rot_done, 1)

            for n in range(N_OUT1):
                if n in MIXES:
                    g = MIXES[n]
                    pe.wait_ge(w_split, n + 1)
                    pe.wait_ge(acc_read, n - 1)
                    pe.wait_ge(pll_ready, g + 1)
                    for w, x in ((WH, PLH), (WH, PLL), (WL, PLH)):
                        for c in range(2):
                            mm = pe.matmul(acc[:, n % 2, HALF * c:HALF * c + HALF], w[n % 2][:, 0, :],
                                           x[:, HALF * c:HALF * c + HALF],
                                           start=(w is WH and x is PLH), stop=(w is WL))
                    mm.then_inc(acc_done, 1)
                else:
                    gemm(n, n % 2, HH, HL, ready=hl_ready if n == 0 else None)
                if n == 1:
                    rotate(0)
                if 3 <= n <= 6:
                    rotate(n - 2)
            for t in range(TT):
                mm = pe.transpose(turn[:, P * t:P * t + P], VN[:, P * t:P * t + P], ident)
            mm.then_inc(vt_done, 1)
            pe.wait_ge(kst_act, 4)
            pe.wait_ge(kst_dve, 4)
            pe.wait_ge(acc_read, N_OUT1)
            pe.wait_ge(vl_ready, 1)

            def ada_tile(it, j):
                s, h = j // 7, j % 7
                if j == 0:
                    pe.wait_ge(ada_read, it * 4 + 1)
                pe.wait_ge(ada_in[j % 2], it * 112 + 16 * (j // 2 + 1))
                for k in range(KD):
                    if h < 4:
                        mm = pe.matmul(bank7[:, 16 + 32 * s + h:17 + 32 * s + h], AR[j % 2][:, k, :], SC1[:, k:k + 1],
                                       start=(k == 0), stop=(k == KD - 1))
                    else:
                        c = 16 + 32 * s + 4 + 2 * (h - 4)
                        mm = pe.matmul(bank7[:, c:c + 2], AR[j % 2][:, k, :], SC2[:, k, :],
                                       start=(k == 0), stop=(k == KD - 1))
                mm.then_inc(ada_done, 1)

            with pe.Fori(0, 4) as it:
                def scores(u):
                    s, h = u // 8, u % 8
                    if u % 8 == 0:
                        pe.wait_ge(qst_act, it * 4 + (2 * s + 2))
                        pe.wait_ge(qst_dve, it * 4 + (2 * s + 2))
                    if u >= 2:
                        pe.wait_ge(exp_done, it * 16 + (u - 1))
                    for ks in (KSH, KSL):
                        for c in range(2):
                            mm = pe.matmul(acc[:, u % 2, HALF * c:HALF * c + HALF], QST[s][:, h, :],
                                           ks[:, h // 4, HALF * c:HALF * c + HALF], start=(ks is KSH), stop=(ks is KSL))
                    mm.then_inc(scores_done, 1)

                def values(b):
                    pe.wait_ge(ptl_ready, it * 16 + 4 * (b + 1))
                    if b > 0:
                        pe.wait_ge(o_ready, it * 4 + b)
                    for k in range(TT):
                        for x in (PTH, PTL):
                            mm = pe.matmul(bank6[:, :], VTOK[:, k, b % 2, :], x[:, k, :, :],
                                           start=(k == 0 and x is PTH), stop=(k == TT - 1 and x is PTL))
                    mm.then_inc(pv_done, 1)

                scores(0)
                for u in range(16):
                    if u < 15:
                        scores(u + 1)
                    if u % 8 < 7:
                        ada_tile(it, 7 * (u // 8) + u % 8)
                    if u % 4 == 0 and u > 0:
                        values(u // 4 - 1)
                    pe.wait_ge(p_ready, it * 16 + (u + 1))
                    if u > 0:
                        pe.wait_ge(ptl_ready, it * 16 + u)
                    for k in range(TT):
                        mm = pe.transpose(turn[:, P * k:P * k + P], EX[u % 2][:, P * k:P * k + P], ident)
                    mm.then_inc(pt_done, 1)
                values(3)
                pe.wait_ge(o_ready, it * 4 + 4)
            pe.wait_ge(ml_ready, 8)
            pe.wait_ge(mh_ready, 8)
            pe.wait_ge(exp_done, 64)

            def residual_tiles(q, n0, hi, lo, k_n, with_stats):
                def pair(it, first):
                    for s in range(2):
                        gemm(it * 2 + (n0 + s), s, hi, lo, k_n)
                        if with_stats and not (first and s == 0):
                            slot_now[0] = 1 - s
                            stats(q, it * 2 + (s - 1), first and s == 1, False)
                pair(0, True)
                with pe.Fori(1, 4) as it:
                    pair(it, False)
                if with_stats:
                    stats(q, KD - 1, False, True)

            residual_tiles(1, N_OUT1, MH, ML, KD, True)
            spread_rs(1)
            for g, gk in enumerate(GROUPS):
                hl_base[0] = KD
                gemm(N_UP[g], 0, HH, HL, ready=hl_ready if g == 0 else None)
                gemm(N_UP[g] + 1, 1, HH, HL)
                with pe.Fori(1, gk) as it:
                    for s in range(2):
                        gemm(it * 2 + (N_UP[g] + s), s, HH, HL)
                pe.wait_ge(post_done, N_UP[g] + 2 * gk)
                if g == 2:
                    pe.wait_ge(csq_ready, 1)
                    for t in range(2):
                        for k in range(KD):
                            mm = pe.matmul(bank6[:, 16 + t:17 + t], SQC[:, k, P * t:P * t + P], one,
                                           start=(k == 0), stop=(k == KD - 1))
                    mm.then_inc(cstat_done, 1)
                    pe.wait_ge(crs_ready, 1)
                    for t in range(2):
                        mm = pe.matmul(turn[:, P * t:P * t + P], RS[:, t:t + 1].to_broadcast([P, P]), ident,
                                       start=True, stop=True)
                    mm.then_inc(crb_done, 1)
                residual_tiles(2, N_DOWN[g], GH, GL, gk, g == 2)

            pe.wait_ge(cxn_ready, 1)
            spread_rs(2)
            hl_base[0] = 2 * KD

            def att_pair(n, pair, first):
                u0 = pair * 16
                if not first:
                    pe.wait_ge(exp2_done, u0)
                    pe.wait_ge(o2_ready, u0)
                else:
                    pe.wait_ge(hcl_ready, 1)
                gemm(n, 0, HH, HL, ready=hl_ready if first else None, context=bank7)
                gemm(n + 1, 1, HH, HL, context=bank6)
                gemm(n + 2, 0, HH, HL)
                pe.wait_ge(acc_read, n + 2)
                if first:
                    pe.wait_ge(xn_ready, 3 * KD)

                def turn_values(b, c0, c1):
                    if b > 0:
                        pe.wait_ge(vtok2_ready, pair * 3 + b)
                    for c in range(c0, c1):
                        mm = pe.transpose(turn[:, P * (c - c0):P * (c - c0) + P], VT2[:, P * c:P * c + P], ident)
                    mm.then_inc(vt2_done, 1)

                turn_values(0, 0, 8)
                gemm(n + 3, 1, HH, HL)
                turn_values(1, 8, 16)
                turn_values(2, 16, 18)

                def scores(u):
                    j, half, c = u // 8, u // 4 % 2, u % NB
                    a = acc[:, u % 2, :]
                    if u < 2:
                        pe.wait_ge(acc_read, n + 4)
                    else:
                        pe.wait_ge(exp2_done, u0 + (u - 1))
                    rows = K2[HD * j:HD * j + HD, 0:T].rearrange("p (r c) -> p r c", c=GRID)
                    q = Q2[HD * j:HD * j + HD, HALF * half + P * c:HALF * half + P * c + P]
                    pe.matmul(a[:, P:P + NLOC], q, rows[:, 4 * half:4 * half + 12, KCS[c]:KCS[c] + KW], start=True, stop=True)
                    pe.matmul(a[:, HALF:HALF + CTX], q, K2[HD * j:HD * j + HD, T:T + CTX], start=True, stop=True
                              ).then_inc(scores2_done, 1)

                def turn_probs(u):
                    pe.wait_ge(dg_ready, u0 + (u + 1))
                    if u == 0:
                        pe.wait_ge(vtok2_ready, pair * 3 + 3)
                    else:
                        pe.wait_ge(pt2_ready, u0 + u)
                    for k in range(NKEY // P):
                        mm = pe.matmul(turn[:, P * k:P * k + P], EX2[u % 2][:, P * k:P * k + P], DG[u % 2][:, :],
                                       start=True, stop=True)
                    mm.then_inc(pt2_done, 1)

                def values(u):
                    half, c = u // 4 % 2, u % NB
                    pe.wait_ge(pt2_ready, u0 + (u + 1))
                    if u >= 2:
                        pe.wait_ge(o2_ready, u0 + (u - 1))
                    bank = (bank6, bank7)[u % 2]
                    for k in range(NKEY // P):
                        kc = 4 * c + half + k if k < 3 else 4 * NB + k - 3
                        mm = pe.matmul(bank[:, 0:P], VTOK2[:, kc, :], PT2[u % 2][:, P * k:P * k + P],
                                       start=(k == 0), stop=(k == NKEY // P - 1))
                    mm.then_inc(pv2_done, 1)

                scores(0)
                for u in range(16):
                    if u < 15:
                        scores(u + 1)
                    if u > 0:
                        values(u - 1)
                    turn_probs(u)
                values(15)

            att_pair(N_ATT2, 0, True)
            with pe.Fori(1, 4) as it:
                att_pair(it * 4 + N_ATT2, it, False)

            pe.wait_ge(exp2_done, 64)
            pe.wait_ge(o2_ready, 64)
            pe.wait_ge(dft_in, 16)
            COS_T, SIN_T = DFT[:, 0:4 * HALF], DFT[:, 4 * HALF:8 * HALF]
            COS_C, SIN_C = DFT[:, 8 * HALF:8 * HALF + P], DFT[:, 8 * HALF + P:8 * HALF + 2 * P]
            SIGNS = DFT[0:1, 8 * HALF + 2 * P:NDFT]

            with pe.Fori(0, 4) as it:
                n = it * 2 + N_F
                gemm(n, 0, HH, HL)
                pe.wait_ge(fold_ready, it + 1)
                pe.wait_ge(y_ready, it * 2 + 1)
                for f, c, o in ((FE, COS_C, 0), (FO, SIN_C, HALF)):
                    for t in range(4):
                        pe.matmul(turn[:, o + P * t:o + P * t + P], f[:, P * t:P * t + P], c, start=True, stop=True)
                pe.matmul(bank6[0:1, 0:P], FE[:, HALF:HALF + 1], COS_C, start=True, stop=True)
                pe.matmul(bank6[:, P:P + 1], COS_C, ALT[:, 2:3], start=True, stop=True).then_inc(chan_done, 1)
                gemm(n + 1, 1, HH, HL)
                pe.wait_ge(vw_ready, it * 2 + 2)
                for t in range(4):
                    pe.matmul(bank7[:, :], VW[:, t, :], COS_T[:, HALF * t:HALF * t + HALF], start=(t == 0), stop=False)
                pe.matmul(bank7[:, :], VROW[0:1, :], SIGNS, start=False, stop=True)
                for t in range(4):
                    mm = pe.matmul(bank6[:, :], VW[:, 4 + t, :], SIN_T[:, HALF * t:HALF * t + HALF], start=(t == 0), stop=(t == 3))
                mm.then_inc(seq_done, 1)

            def gates(n0, hi, lo, sem_, value):
                with pe.Fori(0, KD) as it:
                    gemm(it * 2 + n0, 0, HH, HL)
                    pe.wait_ge(sem_, value)
                    gemm(it * 2 + (n0 + 1), 1, hi, lo, 4)

            gates(N_GF, BRH, BRL, post_done, N_GF)
            gates(N_GC, CBH, CBL, cbl_ready, 1)
            with pe.Fori(0, 8) as it:
                for s in range(2):
                    gemm(it * 2 + (N_A + s), s, HH, HL)
            gates(N_GA, BRH, BRL, post_done, N_GA)
            pe.wait_ge(post_done, N_OUT2)
            residual_tiles(3, N_OUT2, SH, SL, KD, True)
            spread_rs(3)

        @block.scalar
        def _(act):
            steps = Steps(act, act_step)

            def evac_wait(n):
                act.wait_ge(acc_done, n + 1)
                if not isinstance(n, int) or n >= 2:
                    act.wait_ge(post_done, n - 1)

            def square(q, k, slot, src):
                if not isinstance(k, int) or q * KD + k >= 2:
                    act.wait_ge(sq_used, q * KD + k - 1)
                act.activation(SQ[slot][:, :], src, ACT.Square).then_inc(sq_ready, 1)

            def root(q, nt=TT):
                act.wait_ge(sq_used, q * KD + KD)
                act.activation(SD[:, 0:nt], bank6[:, 0:nt], ACT.Sqrt, bias=eps, scale=1.0 / D).then_inc(sd_ready, 1)

            def modulate(q, scale, shift, hh):
                for k in range(KD):
                    act.wait_ge(xn_ready, q * KD + k + 1)
                    if k >= 2:
                        act.wait_ge(hl_ready, q * KD + k - 1)
                    act.activation(CV[k % 2][:, :], EV[k % 2][:, :], ACT.Identity, bias=shift(k), scale=scale(k)
                                   ).then_inc(hf_ready, 1)
                    act.wait_ge(hf_ready, q * KD + k + 1)
                    act.activation(hh[:, k, :], CV[k % 2][:, :], ACT.Copy).then_inc(hh_ready, 1)

            act.wait_ge(consts_in, 32)
            steps.did(act.activation(SC2[:, :, :], VEC[:, VCOL["c_2"]:VCOL["c_2"] + 16].rearrange("p (k a) -> p k a", a=2),
                                     ACT.Silu))
            act.activation(SC1[:, :], vec("c", 0, KD), ACT.Silu).then_inc(silu_ready, 1)
            act.wait_ge(x_in, 16)
            for k in range(KD):
                square(0, k, k % 2, XT[:, k, :])
            root(0)
            act.wait_ge(mods_ready, 1)
            modulate(0, lambda k: A1[:, k:k + 1], lambda k: MOD1[:, k:k + 1], HH)

            def pool_first(g):
                act.wait_ge(pooled, g + 1)
                if g > 0:
                    act.wait_ge(acc_done, [8, 10, 12, 13][g - 1] + 1)
                act.activation(PLH[:, :], UP[:, PAD:PAD + T], ACT.Copy).then_inc(plh_ready, 1)

            for n in range(N_OUT1):
                evac_wait(n)
                src, slot = acc[:, n % 2, :], n % 2
                if n == 1 or n in POOLS:
                    act.activation(EV[slot][:, :], src, ACT.Copy).then_inc(acc_read, 1)
                elif n in MIXES:
                    g = MIXES[n]
                    act.activation(EV[slot][:, :], src, ACT.Copy, scale=vec("pool_scale", g)).then_inc(acc_read, 1)
                    act.wait_ge(acc_read, n + 1)
                    act.activation(MH[:, 4 + g, :], EV[slot][:, :], ACT.Copy).then_inc(mixh_ready, 1)
                else:
                    m = [0, None, 1, 2, 3, 4][n]
                    if m > 1:
                        act.wait_ge(qstat_done, m - 1)
                    steps.did(act.activation(CV[slot][:, :], src, ACT.Square))
                    act.activation(EV[slot][:, :], src, ACT.Copy, scale=vec("k_norm_g" if n == 0 else "q_norm_g")
                                   ).then_inc(acc_read, 1)
                    act.wait_ge(acc_read, n + 1)
                    steps.settle()
                    act.activation(SUM[:, 7:8], eps, ACT.Copy).then_inc(sqh_ready, 1)
                    if m == 0:
                        act.wait_ge(kms_done, 1)
                        act.activation(CV[1][:, :], turn[:, :], ACT.Sqrt, bias=eps).then_inc(ksd_ready, 1)
                if n in (7, 9, 11, 12):
                    pool_first([7, 9, 11, 12].index(n))
            act.wait_ge(qstat_done, 4)
            act.activation(QSD[:, :, :], bank6[:, 64:64 + TT * NQ].rearrange("p (t h) -> p t h", h=NQ), ACT.Sqrt, bias=eps,
                           scale=1.0 / HD).then_inc(qsd_ready, 1)
            act.wait_ge(post_done, N_OUT1)
            act.activation(KHI[:, :], KN[:, :], ACT.Copy).then_inc(khi_ready, 1)
            act.wait_ge(khi_ready, 1)
            for kv in range(NKV):
                for b in range(2):
                    act.activation(KSH[64 * b:64 * b + 64, kv, :], KHI[64 * kv:64 * kv + 64, :].bitcast(F32), ACT.Copy
                                   ).then_inc(kst_act, 1)
            act.wait_ge(vt_done, 1)
            vt = turn[:, :].rearrange("p (a d) -> p a d", d=HD)
            vdst = VTOK[:, :, :, :].rearrange("p t v d -> p (t v) d")
            act.wait_ge(acc_done, N_OUT1)
            act.wait_ge(kst_act, 4)
            act.activation(vdst[:, :, 0:HD], vt, ACT.Copy).then_inc(vh_ready, 1)

            act.wait_ge(kst_dve, 4)
            with steps.loop(4, 2) as it:
                for s in range(2):
                    if s > 0:
                        act.wait_ge(qst_dve, it * 4 + 2 * s)
                        act.wait_ge(qst_act, it * 4 + 2 * s)
                    act.activation(QH[:, :, :], QN[:, :, bass.ds(it * 256 + 128 * s, P)], ACT.Copy).then_inc(qh_ready, 1)
                    act.wait_ge(qh_ready, it * 2 + (s + 1))
                    for b in range(2):
                        dst = QST[s][0:64, :, :].rearrange("p (i j) q -> p i j q", j=2)[:, :, b, :]
                        act.activation(dst, QH[64 * b:64 * b + 64, :, :].bitcast(F32), ACT.Copy).then_inc(qst_act, 1)

                def turned(u):
                    act.wait_ge(pt_done, it * 16 + (u + 1))
                    if u % 4 == 0 and u > 0:
                        act.wait_ge(pv_done, it * 4 + u // 4)
                    act.activation(PTH[:, :, u % 4, :], turn[:, :].rearrange("p (k q) -> p k q", q=P), ACT.Copy
                                   ).then_inc(pth_ready, 1)

                def gather_o(b):
                    act.wait_ge(pv_done, it * 4 + (b + 1))
                    if b > 0:
                        act.wait_ge(o_ready, it * 4 + b)
                    act.activation(OTMP[0:64, :], bank6[64:128, :], ACT.Copy).then_inc(otmp_ready, 1)
                    if b % 2 == 1:
                        act.wait_ge(o_ready, it * 4 + (b + 1))
                        act.activation(MH[:, 0:4, bass.ds(it * 256 + 128 * (b // 2), P)], OT[:, :, :], ACT.Copy
                                       ).then_inc(mh_ready, 1)

                for u in range(16):
                    act.wait_ge(nb_ready, it * 16 + (u + 1))
                    if u >= 2:
                        act.wait_ge(pt_done, it * 16 + (u - 1))
                    qb = it * 16 + u
                    act.activation(EX[u % 2][:, :], acc[:, u % 2, :], ACT.Exp, bias=NBI[:, u % 2:u % 2 + 1],
                                   scale=RSP[:, :, :].rearrange("p t h -> p (t h)")[:, bass.ds(qb, 1)],
                                   accum_out=SUM[:, u % 2:u % 2 + 1]).then_inc(exp_done, 1)
                    if u > 0:
                        turned(u - 1)
                    if u % 4 == 1 and u > 1:
                        gather_o(u // 4 - 1)
                turned(15)
                gather_o(3)
                steps.did(act.activation(SUM[:, 6:7], eps, ACT.Copy))
                act.wait_ge(ml_ready, it * 2 + 2)
                steps.did(act.activation(SUM[:, 5:6], eps, ACT.Copy))

            def residual_tiles(q, n0, gate, with_stats, stream=XT):
                with act.Fori(0, 4) as it:
                    for s in range(2):
                        n = it * 2 + (n0 + s)
                        evac_wait(n)
                        act.activation(EV[s][:, :], acc[:, s, :], ACT.Copy,
                                       scale=gate(it * 2 + s)).then_inc(acc_read, 1)
                        if with_stats:
                            act.wait_ge(post_done, n + 1)
                            square(q, it * 2 + s, s, stream[:, bass.ds(it * 2 + s, 1), :])

            residual_tiles(1, N_OUT1, lambda k: MOD1[:, bass.ds(k + 16, 1)], True)
            root(1)
            modulate(1, lambda k: A2[:, k:k + 1], lambda k: MOD1[:, 24 + k:25 + k], HH)
            for g, gk in enumerate(GROUPS):
                with act.Fori(0, gk) as it:
                    f0 = sum(GROUPS[:g])
                    p0 = f0
                    for s in range(2):
                        n = it * 2 + (N_UP[g] + s)
                        evac_wait(n)
                        if s == 0:
                            act.wait_ge(post_done, n)
                        act.activation(EV[s][:, :], acc[:, s, :], ACT.Copy).then_inc(act_step, 1)
                        f = it + (f0 + FC * s)
                        act.activation(CV[s][:, :], acc[:, s, :], ACT.Identity, bias=vec("conv_b", f), scale=vec("conv_w", f + 44)
                                       ).then_inc(acc_read, 1)
                    act.wait_ge(gated, it * 3 + (3 * p0 + 1))
                    act.activation(EV[0][:, :], CV[0][:, :], ACT.Silu).then_inc(silu_done, 1)
                    act.wait_ge(gated, it * 3 + (3 * p0 + 3))
                    act.activation(GH[:, bass.ds(it, 1), :], CV[0][:, :], ACT.Copy).then_inc(gh_ready, 1)
                if g == 2:
                    act.wait_ge(cx_in, 16)
                    act.activation(SQC[:, :, :], CX[:, :, :], ACT.Square).then_inc(csq_ready, 1)
                    act.wait_ge(cstat_done, 1)
                    act.activation(SD[:, 0:2], bank6[:, 16:18], ACT.Sqrt, bias=eps, scale=1.0 / D).then_inc(csd_ready, 1)
                residual_tiles(2, N_DOWN[g], lambda k: MOD1[:, bass.ds(k + 40, 1)], g == 2)

            root(2)
            modulate(2, lambda k: A3[:, k, 0:1], lambda k: MOD2[:, k, 0:1], HH)
            act.wait_ge(cxn_ready, 1)
            for k in range(KD):
                act.activation(CX[:, k, :], CX[:, k, :], ACT.Identity, bias=MOD2[:, k, 1:2], scale=A3[:, k, 1:2]
                               ).then_inc(ch_ready, 1)
            act.wait_ge(ch_ready, KD)
            act.activation(HCH[:, :, :], CX[:, :, :], ACT.Copy).then_inc(hch_ready, 1)

            def b_in(j):
                return vec("b_in_2", j)

            with act.Fori(0, 4) as it:
                n, u0 = it * 4 + N_ATT2, it * 16
                act.wait_ge(acc_done, n + 1)
                steps.did(act.activation(K2[:, 0:T], acc[:, 0, :], ACT.Identity, bias=b_in(it + 28)))
                act.activation(K2[:, T:], bank7[:, 0:CTX], ACT.Identity, bias=b_in(it + 28)).then_inc(acc_read, 1)
                act.wait_ge(acc_done, n + 2)
                v = acc[:, 1, :].rearrange("p (r c) -> p r c", c=GRID)
                for b in range(NB):
                    dst = VT2[:, HALF * b:HALF * b + HALF].rearrange("p (r c) -> p r c", c=KW)
                    act.activation(dst, v[:, :, KCS[b]:KCS[b] + KW], ACT.Identity, bias=b_in(it + 32))
                act.activation(VT2[:, NB * HALF:], bank6[:, 0:CTX], ACT.Identity, bias=b_in(it + 32)).then_inc(acc_read, 1)
                act.wait_ge(acc_done, n + 3)
                for half in range(2):
                    src = acc[:, 0, HALF * half:HALF * half + HALF].rearrange("p (r n c) -> p n r c", n=NB, c=QW)
                    dst = Q2[:, HALF * half:HALF * half + HALF].rearrange("p (n r c) -> p n r c", n=NB, c=QW)
                    ins = act.activation(dst, src, ACT.Identity, bias=BQ8[:, bass.ds(it, 1)], scale=SCALE)
                ins.then_inc(acc_read, 1)

                def values_by_key(b, c0, c1):
                    act.wait_ge(vt2_done, it * 3 + (b + 1))
                    act.activation(VTOK2[:, c0:c1, :], turn[:, 0:P * (c1 - c0)].rearrange("p (c d) -> p c d", d=P), ACT.Copy
                                   ).then_inc(vtok2_ready, 1)

                act.wait_ge(x_saved, 16)
                values_by_key(0, 0, 8)
                act.wait_ge(acc_done, n + 4)
                act.activation(SZ[:, :], acc[:, 1, :], ACT.Silu, bias=b_in(it + 36)).then_inc(acc_read, 1)
                values_by_key(1, 8, 16)
                values_by_key(2, 16, 18)

                def turned(u):
                    act.wait_ge(pt2_done, u0 + (u + 1))
                    if u >= 2:
                        act.wait_ge(pv2_done, u0 + (u - 1))
                    act.activation(PT2[u % 2][:, :], turn[:, 0:NKEY], ACT.Copy).then_inc(pt2_ready, 1)

                for u in range(16):
                    act.wait_ge(nb2_ready, u0 + (u + 1))
                    if u >= 2:
                        act.wait_ge(pt2_done, u0 + (u - 1))
                    act.activation(EX2[u % 2][:, :], acc[:, u % 2, P:P + NKEY], ACT.Exp, bias=NBI[:, u % 2:u % 2 + 1],
                                   accum_out=SUM[:, u % 2:u % 2 + 1]).then_inc(exp2_done, 1)
                    if u > 0:
                        turned(u - 1)
                turned(15)
                act.wait_ge(pv2_done, u0 + 16)

            act.wait_ge(o2_ready, 64)
            act.activation(CBH[:, :, :], CBF[:, :, :], ACT.Copy).then_inc(cbh_ready, 1)

            with act.Fori(0, 4) as it:
                n = it * 2 + N_F
                evac_wait(n)
                act.activation(EV[0][:, :], acc[:, 0, :], ACT.Identity, bias=b_in(it + 16)).then_inc(acc_read, 1)
                act.wait_ge(chan_done, it + 1)
                act.activation(VW[:, :, :], turn[:, :].rearrange("p (c d) -> p c d", d=P), ACT.Copy).then_inc(vw_ready, 1)
                act.activation(VROW[0:1, :], bank6[0:1, 0:P], ACT.Copy)
                act.activation(ALT[:, 3:4], bank6[:, P:P + 1], ACT.Copy).then_inc(vw_ready, 1)
                evac_wait(n + 1)
                act.activation(EV[1][:, :], acc[:, 1, :], ACT.Silu, bias=b_in(it + 20)).then_inc(acc_read, 1)
                act.wait_ge(seq_done, it + 1)
                act.activation(SB[:, :], bank6[:, :], ACT.Copy).then_inc(sb_ready, 1)
                act.wait_ge(y_ready, it * 2 + 3)
                act.activation(BRH[:, bass.ds(it, 1), :], CV[1][:, :], ACT.Copy).then_inc(brh_ready, 1)

            def gates(n0, b0, last=False):
                with act.Fori(0, KD) as it:
                    n = it * 2 + n0
                    evac_wait(n)
                    act.activation(EV[0][:, :], acc[:, 0, :], ACT.Sigmoid, bias=b_in(it + b0)).then_inc(acc_read, 1)
                    evac_wait(n + 1)
                    act.activation(EV[1][:, :], acc[:, 1, :], ACT.Copy).then_inc(acc_read, 1)
                    if last:
                        act.wait_ge(sums_ready, it + 1)
                        act.activation(SH[:, bass.ds(it, 1), :], S[:, bass.ds(it, 1), :], ACT.Copy).then_inc(sh_ready, 1)

            gates(N_GF, 56 - 8)
            gates(N_GC, 56)
            with act.Fori(0, 4) as it:
                n = it * 4 + N_A
                for j, (s, b0, fn) in enumerate(((0, 0, ACT.Identity), (1, 8, ACT.Identity), (0, 4, ACT.Identity),
                                                 (1, 12, ACT.Silu))):
                    evac_wait(n + j)
                    act.activation(EV[s][:, :], acc[:, s, :], fn, bias=b_in(it + b0)).then_inc(acc_read, 1)
                act.wait_ge(y_ready, it + 10)
                act.activation(BRH[:, bass.ds(it, 1), :], CV[0][:, :], ACT.Copy).then_inc(brh_ready, 1)
            gates(N_GA, 40, last=True)

            residual_tiles(3, N_OUT2, lambda k: MOD2[:, bass.ds(k + 16, 1), 0], True, XT2)
            root(3)

        @block.vector
        def _(dve):
            steps = Steps(dve, dve_step)

            def link(ins):
                steps.did(ins)
                steps.settle()

            def invert(q, nt=TT):
                dve.wait_ge(sd_ready, q + 1)
                dve.reciprocal(RS[:, 0:nt], SD[:, 0:nt]).then_inc(rs_ready, 1)

            def normed(q, src, hh, hl, w=T):
                dve.wait_ge(rb_done, q + 1)

                def second(k):
                    dve.wait_ge(hh_ready, q * KD + k + 1)
                    dve.tensor_tensor(hl[:, k, :], CV[k % 2][:, 0:w], hh[:, k, :].bitcast(F32), ALU.subtract
                                      ).then_inc(hl_ready, 1)

                for k in range(KD):
                    if k >= 2:
                        dve.wait_ge(hf_ready, q * KD + k - 1)
                    dve.tensor_tensor(EV[k % 2][:, 0:w], src(k), turn[:, 0:w], ALU.mult).then_inc(xn_ready, 1)
                    if k > 0:
                        second(k - 1)
                second(KD - 1)

            invert(0)
            dve.wait_ge(mod1_done, 4)
            dve.tensor_tensor(MOD1[:, 0:16], bank7[:, 0:16], vec("b_ada", 0, 16), ALU.add).then_inc(ada_read, 1)
            dve.wait_ge(ada_read, 1)
            dve.scalar_tensor_tensor(out=A1[:, :], in0=MOD1[:, 8:16], scalar=1.0, in1=vec("norm1_g", 0, KD), op0=ALU.add,
                                     op1=ALU.mult).then_inc(mods_ready, 1)
            normed(0, lambda k: XT[:, k, :], HH, HL)
            dve.wait_ge(rope_in, 32)
            for b in (UP, *WINS):
                steps.did(dve.memset(b[:, 0:PAD], 0.0))
                steps.did(dve.memset(b[:, PAD + T:], 0.0))
            steps.settle()

            def rope(n, m):
                dst = KN[:, :] if m == 0 else QN[:, m - 1, :]
                e = EV[n % 2]
                steps.settle()
                if n > 0:
                    dve.wait_ge(post_done, n)
                if m == 0:
                    dve.wait_ge(ksd_ready, 1)
                    link(dve.reciprocal(CV[1][:, :], CV[1][:, :]))
                dve.wait_ge(acc_read, n + 1)
                steps.did(dve.tensor_tensor(ROPE1[:, :], e[:, :], COS[:, :], ALU.mult))
                dve.wait_ge(rot_done, m + 1)
                link(dve.tensor_tensor(ROPE2[:, :], turn[:, :], SIN[:, :], ALU.mult))
                if m == 0:
                    link(dve.tensor_tensor(ROPE1[:, :], ROPE1[:, :], ROPE2[:, :], ALU.add))
                    dve.tensor_tensor(dst, ROPE1[:, :], CV[1][:, :], ALU.mult).then_inc(post_done, 1)
                else:
                    dve.tensor_tensor(dst, ROPE1[:, :], ROPE2[:, :], ALU.add).then_inc(post_done, 1)

            def windows(n, g):
                dve.wait_ge(acc_read, n + 1)
                if g > 0:
                    dve.wait_ge(plh_ready, g)
                    dve.wait_ge(pll_ready, g)
                dve.tensor_copy(UP[:, PAD:PAD + T], EV[n % 2][:, :]).then_inc(post_done, 1)
                dve.wait_ge(post_done, n + 1)
                w, half = POOL_W[g], POOL_W[g] // 2
                src, r = UP, 0
                link(dve.tensor_tensor(WINS[0][:, 1:T + 2 * PAD], UP[:, 1:T + 2 * PAD], UP[:, 0:T + 2 * PAD - 1], ALU.add))
                h = 1
                while 2 * h < w:
                    a, b = WINS[r], WINS[1 - r]
                    lo, hi = 2 * h, T + 2 * PAD - 2 * h + 1
                    link(dve.tensor_tensor(b[:, lo:hi], a[:, lo + h:hi + h], a[:, lo - h:hi - h], ALU.add))
                    r, h = 1 - r, 2 * h
                win = WINS[r]
                edge = con("edge", 16, 16 * g)
                steps.did(dve.tensor_tensor(win[:, PAD:PAD + 8], win[:, PAD:PAD + 8], edge[:, 0:8], ALU.mult))
                link(dve.tensor_tensor(win[:, PAD + T - 8:PAD + T], win[:, PAD + T - 8:PAD + T], edge[:, 8:16], ALU.mult))
                dve.scalar_tensor_tensor(out=UP[:, PAD:PAD + T], in0=win[:, PAD:PAD + T], scalar=1.0 / w, in1=UP[:, PAD:PAD + T],
                                         op0=ALU.mult, op1=ALU.subtract).then_inc(pooled, 1)
                dve.wait_ge(plh_ready, g + 1)
                dve.tensor_tensor(PLL[:, :], UP[:, PAD:PAD + T], PLH[:, :].bitcast(F32), ALU.subtract).then_inc(pll_ready, 1)
                dve.wait_ge(pll_ready, g + 1)

            def mix_second(n, g):
                dve.wait_ge(mixh_ready, g + 1)
                dve.tensor_tensor(ML[:, 4 + g, :], EV[n % 2][:, :], MH[:, 4 + g, :].bitcast(F32), ALU.subtract
                                  ).then_inc(post_done, 1)

            for n in range(N_OUT1):
                if n == 1:
                    dve.wait_ge(acc_read, 2)
                    dve.tensor_copy(VN[:, :], EV[1][:, :]).then_inc(post_done, 1)
                elif n in POOLS:
                    windows(n, POOLS[n])
                elif n in MIXES:
                    mix_second(n, MIXES[n])
                else:
                    rope(n, [0, None, 1, 2, 3, 4][n])
            dve.wait_ge(qsd_ready, 1)
            link(dve.reciprocal(QSD[:, :, :], QSD[:, :, :]))
            steps.did(dve.tensor_scalar(RSP[:, :, :], QSD[:, :, :], SCALE, None, ALU.mult))
            steps.did(dve.tensor_scalar(RSN[:, :, :], QSD[:, :, :], -SCALE, None, ALU.mult))
            dve.wait_ge(khi_ready, 1)
            dve.tensor_tensor(KLO[:, :], KN[:, :], KHI[:, :].bitcast(F32), ALU.subtract).then_inc(klo_ready, 1)
            dve.wait_ge(klo_ready, 1)
            for kv in range(NKV):
                for b in range(2):
                    dve.tensor_copy(KSL[64 * b:64 * b + 64, kv, :], KLO[64 * kv:64 * kv + 64, :]).then_inc(kst_dve, 1)
            dve.wait_ge(vh_ready, 1)
            vt = turn[:, :].rearrange("p (a d) -> p a d", d=HD)
            vdst = VTOK[:, :, :, :].rearrange("p t v d -> p (t v) d")
            dve.tensor_tensor(vdst[:, :, HD:P], vt, vdst[:, :, 0:HD].bitcast(F32), ALU.subtract).then_inc(vl_ready, 1)
            dve.wait_ge(vl_ready, 1)
            dve.wait_ge(kst_dve, 4)
            dve.wait_ge(kst_act, 4)

            with steps.loop(4, 22) as it:
                for s in range(2):
                    dve.wait_ge(qh_ready, it * 2 + (s + 1))
                    link(dve.tensor_tensor(QL[:, :, :], QN[:, :, bass.ds(it * 256 + 128 * s, P)], QH[:, :, :].bitcast(F32),
                                           ALU.subtract))
                    for b in range(2):
                        dst = QST[s][64:128, :, :].rearrange("p (i j) q -> p i j q", j=2)[:, :, b, :]
                        dve.tensor_copy(dst, QL[64 * b:64 * b + 64, :, :]).then_inc(qst_dve, 1)
                    dve.wait_ge(qst_dve, it * 4 + (2 * s + 2))

                def turned(u):
                    dve.wait_ge(pth_ready, it * 16 + (u + 1))
                    dve.tensor_tensor(PTL[:, :, u % 4, :], turn[:, :].rearrange("p (k q) -> p k q", q=P),
                                      PTH[:, :, u % 4, :].bitcast(F32), ALU.subtract).then_inc(ptl_ready, 1)

                def gather_o(b):
                    dve.wait_ge(otmp_ready, it * 4 + (b + 1))
                    if b % 2 == 0 and b > 0:
                        dve.wait_ge(ml_ready, it * 2 + b // 2)
                    g = b % 2
                    o = bank6[0:64, :].rearrange("p (i j q) -> p i j q", j=2, q=P)
                    m = OTMP[0:64, :].rearrange("p (i j q) -> p i j q", j=2, q=P)
                    link(dve.tensor_tensor(OT[0:64, 2 * g:2 * g + 2, :], o[:, :, 0, :], m[:, :, 0, :], ALU.add))
                    dve.tensor_tensor(OT[64:128, 2 * g:2 * g + 2, :], o[:, :, 1, :], m[:, :, 1, :], ALU.add).then_inc(o_ready, 1)
                    if g == 1:
                        dve.wait_ge(mh_ready, it * 2 + (b // 2 + 1))
                        sl = bass.ds(it * 256 + 128 * (b // 2), P)
                        dve.tensor_tensor(ML[:, 0:4, sl], OT[:, :, :], MH[:, 0:4, sl].bitcast(F32), ALU.subtract
                                          ).then_inc(ml_ready, 1)

                def ada_out(s):
                    dve.wait_ge(ada_done, it * 14 + (2 + 14))
                    b1, b2 = it * 8 + (16 + 4 * s), it * 6 + 3 * s
                    c = 16 + 32 * s
                    dve.tensor_tensor(MOD1[:, bass.ds(b1, 4)], bank7[:, c:c + 4], vec("b_ada", b1, 4), ALU.add
                                      ).then_inc(ada_read, 1)
                    dve.tensor_tensor(MOD2[:, bass.ds(b2, 3), :], bank7[:, c + 4:c + 10].rearrange("p (a b) -> p a b", b=2),
                                      vec("b_ada_2", b2, 3).unsqueeze(2).to_broadcast([P, 3, 2]), ALU.add).then_inc(ada_read, 1)

                for u in range(16):
                    j = u % 2
                    dve.wait_ge(scores_done, it * 16 + (u + 1))
                    link(dve.tensor_reduce(MX[:, j:j + 1], acc[:, j, :], AX.X, ALU.max))
                    dve.tensor_tensor(NBI[:, j:j + 1], MX[:, j:j + 1],
                                      RSN[:, :, :].rearrange("p t h -> p (t h)")[:, bass.ds(it * 16 + u, 1)], ALU.mult
                                      ).then_inc(nb_ready, 1)
                    if u > 0:
                        turned(u - 1)
                    if u % 4 == 1 and u > 1:
                        gather_o(u // 4 - 1)
                    if u == 15:
                        ada_out(0)
                        ada_out(1)
                    dve.wait_ge(exp_done, it * 16 + (u + 1))
                    if u >= 2:
                        dve.wait_ge(p_ready, it * 16 + (u - 1))
                    dve.reciprocal(RC[:, j:j + 1], SUM[:, j:j + 1]).then_inc(rc_ready, 1)
                turned(15)
                gather_o(3)
                dve.wait_ge(ada_read, it * 4 + 5)
                dve.wait_ge(ml_ready, it * 2 + 2)
            link(dve.scalar_tensor_tensor(out=A2[:, :], in0=MOD1[:, 32:40], scalar=1.0, in1=vec("norm2_g", 0, KD), op0=ALU.add,
                                          op1=ALU.mult))
            for v in range(2):
                link(dve.scalar_tensor_tensor(out=A3[:, :, v], in0=MOD2[:, 8:16, v], scalar=1.0, in1=vec("norm_g_2", 0, KD),
                                              op0=ALU.add, op1=ALU.mult))

            def residual_tiles(n0, arrivals=None, stream=XT):
                def pair(it):
                    for s in range(2):
                        if arrivals:
                            dve.wait_ge(arrivals[2 * it + s], 16)
                        dve.wait_ge(acc_read, it * 2 + (n0 + s + 1))
                        x = stream[:, 2 * it + s, :] if isinstance(it, int) else stream[:, bass.ds(it * 2 + s, 1), :]
                        dve.tensor_tensor(x, x, EV[s][:, :], ALU.add).then_inc(post_done, 1)
                if arrivals:
                    for it in range(4):
                        pair(it)
                else:
                    with dve.Fori(0, 4) as it:
                        pair(it)

            residual_tiles(N_OUT1, x_again)
            invert(1)
            normed(1, lambda k: XT[:, k, :], HH, HL)

            def shifted(s, f):
                link(dve.scalar_tensor_tensor(out=CV[s][:, 1:T], in0=EV[s][:, 0:T - 1], scalar=vec("conv_w", f), in1=CV[s][:, 1:T],
                                              op0=ALU.mult, op1=ALU.add))
                return dve.scalar_tensor_tensor(out=CV[s][:, 0:T - 1], in0=EV[s][:, 1:T], scalar=vec("conv_w", f + 88),
                                                in1=CV[s][:, 0:T - 1], op0=ALU.mult, op1=ALU.add)

            for g, gk in enumerate(GROUPS):
                f0 = sum(GROUPS[:g])
                with steps.loop(gk, 2) as it:
                    n = it * 2 + N_UP[g]
                    dve.wait_ge(acc_read, n + 1)
                    shifted(0, it + f0).then_inc(gated, 1)
                    dve.wait_ge(acc_read, n + 2)
                    shifted(1, it + (f0 + FC)).then_inc(gated, 1)
                    dve.wait_ge(silu_done, it + (f0 + 1))
                    dve.wait_ge(gated, it * 3 + (3 * f0 + 2))
                    dve.tensor_tensor(CV[0][:, :], EV[0][:, :], CV[1][:, :], ALU.mult).then_inc(gated, 1)
                    dve.wait_ge(gh_ready, it + (f0 + 1))
                    dve.tensor_tensor(GL[:, bass.ds(it, 1), :], CV[0][:, :], GH[:, bass.ds(it, 1), :].bitcast(F32), ALU.subtract
                                      ).then_inc(post_done, 1)
                    dve.tensor_copy(MX[:, 6:7], eps).then_inc(post_done, 1)
                    dve.wait_ge(post_done, n + 2)
                if g == 2:
                    dve.wait_ge(csd_ready, 1)
                    dve.reciprocal(RS[:, 0:2], SD[:, 0:2]).then_inc(crs_ready, 1)
                    dve.wait_ge(crb_done, 1)
                    dve.tensor_tensor(CX[:, :, :], CX[:, :, :], turn[:, 0:CTX].unsqueeze(1).to_broadcast([P, KD, CTX]), ALU.mult
                                      ).then_inc(cxn_ready, 1)
                residual_tiles(N_DOWN[g])

            invert(2)
            normed(2, lambda k: XT[:, k, :], HH, HL)
            link(dve.tensor_scalar(BQ8[:, 0:4], vec("b_in_2", 24, 4), SCALE, None, ALU.mult))
            dve.wait_ge(hch_ready, 1)
            dve.tensor_tensor(HCL[:, :, :], CX[:, :, :], HCH[:, :, :].bitcast(F32), ALU.subtract).then_inc(hcl_ready, 1)

            with steps.loop(4, 32) as it:
                n, u0 = it * 4 + N_ATT2, it * 16

                def largest(u):
                    j, half, c, a = u // 8, u // 4 % 2, u % NB, acc[:, u % 2, :]
                    if u % 8 == 0:
                        dve.wait_ge(bias_in[j], it * 16 + 16)
                    dve.wait_ge(scores2_done, u0 + (u + 1))
                    link(dve.tensor_tensor(a[:, P:P + NLOC], a[:, P:P + NLOC], BIAS[j][:, 3 * half + KIND[c], :], ALU.add))
                    link(dve.tensor_reduce(MX[:, u % 2:u % 2 + 1], a[:, P:P + NKEY], AX.X, ALU.max))
                    dve.tensor_scalar(NBI[:, u % 2:u % 2 + 1], MX[:, u % 2:u % 2 + 1], -1.0, None, ALU.mult).then_inc(nb2_ready, 1)

                def diagonal(u):
                    dve.wait_ge(exp2_done, u0 + (u + 1))
                    dve.reciprocal(RC[:, u % 2:u % 2 + 1], SUM[:, u % 2:u % 2 + 1]).then_inc(rc_ready, 1)
                    dve.wait_ge(rc_ready, u0 + (64 + u + 1))
                    dve.tensor_scalar(DG[u % 2][:, :], ident, RC[:, u % 2:u % 2 + 1], None, ALU.mult).then_inc(dg_ready, 1)

                def gather(u):
                    j, half, c = u // 8, u // 4 % 2, u % NB
                    if u == 0:
                        dve.wait_ge(acc_read, n + 4)
                    dve.wait_ge(pv2_done, u0 + (u + 1))
                    rows = slice(HD * j, HD * j + HD)

                    def grid(x):
                        return x[rows, HALF * half:HALF * half + HALF].rearrange("p (r c) -> p r c", c=GRID)[:, :, QW * c:QW * c + QW]

                    branch = CBF[rows, bass.ds(it, 1), :].rearrange("p a t -> p (a t)")
                    dve.tensor_tensor(branch[:, HALF * half:HALF * half + HALF].rearrange("p (r c) -> p r c", c=GRID)
                                      [:, :, QW * c:QW * c + QW],
                                      (bank6, bank7)[u % 2][rows, 0:P].rearrange("p (r c) -> p r c", c=QW), grid(SZ), ALU.mult
                                      ).then_inc(o2_ready, 1)

                for u in range(16):
                    largest(u)
                    if u >= 2:
                        gather(u - 2)
                    diagonal(u)
                gather(14)
                gather(15)
                dve.wait_ge(o2_ready, u0 + 16)
                dve.tensor_copy(MX[:, 6:7], eps).then_inc(post_done, 4)
                dve.wait_ge(post_done, n + 4)
            dve.wait_ge(cbh_ready, 1)
            dve.tensor_tensor(CBL[:, :, :], CBF[:, :, :], CBH[:, :, :].bitcast(F32), ALU.subtract).then_inc(cbl_ready, 1)

            dve.wait_ge(dft_in, 16)
            dve.tensor_copy(FO[:, 0:1], zero).then_inc(y_ready, 1)
            with steps.loop(4, 5) as it:
                n = it * 2 + N_F
                u = EV[0]
                dve.wait_ge(acc_read, n + 1)
                steps.did(dve.tensor_tensor(FE[:, 1:HALF], u[:, 1:HALF], u[:, T - 1:HALF:-1], ALU.add))
                steps.did(dve.tensor_tensor(FO[:, 1:HALF], u[:, 1:HALF], u[:, T - 1:HALF:-1], ALU.subtract))
                steps.did(dve.tensor_copy(FE[:, 0:HALF + 1:HALF], u[:, 0:HALF + 1:HALF]))
                pairs = u[:, :].rearrange("p (t a) -> p a t", a=2)
                link(dve.tensor_reduce(ALT[:, 0:2], pairs, AX.X, ALU.add))
                dve.tensor_tensor(ALT[:, 2:3], ALT[:, 0:1], ALT[:, 1:2], ALU.subtract).then_inc(fold_ready, 1)
                dve.tensor_copy(MX[:, 6:7], eps).then_inc(post_done, 1)
                dve.wait_ge(sb_ready, it + 1)
                y = CV[0]
                dve.tensor_tensor(y[:, 0:HALF], bank7[:, :], SB[:, :], ALU.subtract)
                dve.tensor_tensor(y[:, HALF + 1:T], bank7[:, HALF - 1:0:-1], SB[:, HALF - 1:0:-1], ALU.add).then_inc(y_ready, 1)
                steps.did(dve.tensor_copy(y[:, HALF:HALF + 1], ALT[:, 3:4]))
                dve.wait_ge(y_ready, it * 2 + 2)
                steps.settle()
                dve.wait_ge(acc_read, n + 2)
                dve.tensor_tensor(CV[1][:, :], y[:, :], EV[1][:, :], ALU.mult).then_inc(y_ready, 1)
                dve.wait_ge(brh_ready, it + 1)
                dve.tensor_tensor(BRL[:, bass.ds(it, 1), :], CV[1][:, :], BRH[:, bass.ds(it, 1), :].bitcast(F32), ALU.subtract
                                  ).then_inc(post_done, 1)
                dve.wait_ge(post_done, n + 2)

            with dve.Fori(0, KD) as it:
                dve.wait_ge(acc_read, it * 2 + (N_GF + 2))
                dve.tensor_tensor(S[:, bass.ds(it, 1), :], EV[0][:, :], EV[1][:, :], ALU.mult).then_inc(post_done, 2)

            def gates(n0, last=False):
                with steps.loop(KD, 1) as it:
                    s = S[:, bass.ds(it, 1), :]
                    dve.wait_ge(acc_read, it * 2 + (n0 + 2))
                    link(dve.tensor_tensor(CV[0][:, :], EV[0][:, :], EV[1][:, :], ALU.mult))
                    if last:
                        dve.tensor_tensor(s, s, CV[0][:, :], ALU.add).then_inc(sums_ready, 1)
                        dve.wait_ge(sh_ready, it + 1)
                        dve.tensor_tensor(SL[:, bass.ds(it, 1), :], s, SH[:, bass.ds(it, 1), :].bitcast(F32), ALU.subtract
                                          ).then_inc(post_done, 2)
                    else:
                        dve.tensor_tensor(s, s, CV[0][:, :], ALU.add).then_inc(post_done, 2)
                    dve.wait_ge(post_done, it * 2 + (n0 + 2))

            dve.wait_ge(post_done, N_GC)
            gates(N_GC)
            with steps.loop(4, 5) as it:
                n = it * 4 + N_A
                dve.wait_ge(acc_read, n + 2)
                dve.tensor_tensor(CV[1][:, :], EV[0][:, :], EV[1][:, :], ALU.mult).then_inc(post_done, 2)
                dve.wait_ge(post_done, n + 2)

                def tap(i):
                    return vec("w_conv_2", it + 4 * i)

                link(dve.tensor_scalar(CV[0][:, :], CV[1][:, :], tap(1), vec("b_conv_2", it), ALU.mult, ALU.add))
                link(dve.scalar_tensor_tensor(out=CV[0][:, 1:T], in0=CV[1][:, 0:T - 1], scalar=tap(0), in1=CV[0][:, 1:T],
                                              op0=ALU.mult, op1=ALU.add))
                link(dve.scalar_tensor_tensor(out=CV[0][:, 0:T - 1], in0=CV[1][:, 1:T], scalar=tap(2), in1=CV[0][:, 0:T - 1],
                                              op0=ALU.mult, op1=ALU.add))
                dve.wait_ge(acc_read, n + 3)
                link(dve.tensor_tensor(CV[0][:, :], CV[0][:, :], EV[0][:, :], ALU.mult))
                dve.tensor_copy(MX[:, 6:7], eps).then_inc(post_done, 1)
                dve.wait_ge(acc_read, n + 4)
                dve.tensor_tensor(CV[0][:, :], CV[0][:, :], EV[1][:, :], ALU.mult).then_inc(y_ready, 1)
                dve.wait_ge(brh_ready, it + 5)
                steps.did(dve.tensor_tensor(BRL[:, bass.ds(it, 1), :], CV[0][:, :], BRH[:, bass.ds(it, 1), :].bitcast(F32),
                                            ALU.subtract))
                steps.settle()
                dve.tensor_copy(MX[:, 6:7], eps).then_inc(post_done, 1)
                dve.wait_ge(post_done, n + 4)
            gates(N_GA, last=True)

            dve.wait_ge(x_back, 16)
            residual_tiles(N_OUT2, stream=XT2)
            invert(3)
            dve.wait_ge(rb_done, 4)
            for k in range(KD):
                dve.scalar_tensor_tensor(out=XT2[:, k, :], in0=XT2[:, k, :], scalar=vec("final_g_2", k), in1=turn[:, :],
                                         op0=ALU.mult, op1=ALU.mult).then_inc(out_ready, 1)


def tiles_of(w):
    i, o = w.shape
    return np.ascontiguousarray(w.reshape(i // P, P, o // P, P).transpose(2, 1, 0, 3)).reshape(o // P, P, -1)


def cols_of(v):
    return np.asarray(v).reshape(-1, P).T


def layout(x):
    f = {k: np.asarray(v) for k, v in x.items()}
    vec = {
        "b_ada": cols_of(f["b_ada"]), "norm1_g": cols_of(f["norm1_g"]), "pool_scale": cols_of(f["pool_scale"]),
        "norm2_g": cols_of(f["norm2_g"]), "conv_w": cols_of(f["conv_w"]), "conv_b": cols_of(f["conv_b"]),
        "b_ada_2": cols_of(f["b_ada_2"]), "norm_g_2": cols_of(f["norm_g_2"]), "b_in_2": cols_of(f["b_in_2"]),
        "w_conv_2": cols_of(f["w_conv_2"]), "b_conv_2": cols_of(f["b_conv_2"]), "final_g_2": cols_of(f["final_g_2"]),
        "c": cols_of(f["c"]),
        "c_2": np.stack([cols_of(f["c_2"]), cols_of(f["c_ctx_2"])], axis=2).reshape(P, 16),
        "q_norm_g": np.concatenate([f["q_norm_g"][0]] * 2)[:, None],
        "k_norm_g": np.concatenate([f["k_norm_g"][0]] * 2)[:, None],
    }
    w_in, w_up, w_down = (f[k][0] for k in ("w_in", "w_up", "w_down"))
    tin, tup = tiles_of(w_in), tiles_of(w_up)
    stream = [tin[4:5], tin[5:6], tin[0:4], tin[6:10], tiles_of(f["w_out"][0])]
    w6, f0 = None, 0
    for gk in GROUPS:
        stream.append(np.stack([tup[f0:f0 + gk], tup[FC + f0:FC + f0 + gk]], axis=1).reshape(2 * gk, P, -1))
        down = tiles_of(w_down[f0 * P:(f0 + gk) * P])
        if gk == KD:
            stream.append(down)
        else:
            w6 = down
        f0 += gk
    w2 = tiles_of(f["w_in_2"][0])
    col = {name: o // P for name, o in (("a_x", 0), ("a_b", 512), ("a_c", 1024), ("a_z", 1536), ("f_u", 2048), ("f_z", 2560),
                                        ("q", 3072), ("k", 3584), ("v", 4096), ("c_z", 4608), ("g_a", 5120), ("g_f", 6144),
                                        ("g_c", 7168))}

    def in_turn(names, count):
        return w2[[col[name] + i for i in range(count) for name in names]]

    stream += [in_turn(("k", "v", "q", "c_z"), 4), in_turn(("f_u", "f_z"), 4), in_turn(("g_f",), 8), in_turn(("g_c",), 8),
               in_turn(("a_x", "a_c", "a_b", "a_z"), 4), in_turn(("g_a",), 8), tiles_of(f["w_out_2"][0])]
    w4 = np.concatenate([tiles_of(f[name][0]) for name in ("w_br_f_2", "w_br_c_2", "w_br_a_2")])
    ada = np.concatenate([tiles_of(f["w_ada"][0]), tiles_of(f["w_ada_2"][0])])
    head = f["w_ada"][0][:, 0:2048].reshape(KD, P, 4, 512).transpose(2, 1, 0, 3)
    con = np.zeros((P, NCONST), np.float32)
    con[:, CCOL["ident"]:CCOL["ident"] + P] = np.eye(P)
    r = np.arange(P)
    con[:, CCOL["headmean"]:CCOL["headmean"] + P] = (r[:, None] // HD == r[None, :] // HD) / HD
    rot = np.zeros((P, P))
    for i in range(P):
        if i % 32 < 16:
            rot[i + 16, i] = -1.0
        else:
            rot[i - 16, i] = 1.0
    con[:, CCOL["rot"]:CCOL["rot"] + P] = rot
    con[:, CCOL["headsel"]:CCOL["headsel"] + 2] = r[:, None] // HD == np.arange(2)[None, :]
    con[:, CCOL["one"]] = 1.0
    con[:, CCOL["eps"]] = EPS
    for g, w in enumerate(POOL_W):
        t = np.r_[0:8, T - 8:T]
        count = np.minimum(t + w // 2 - 1, T - 1) - np.maximum(t - w // 2, 0) + 1
        con[:, CCOL["edge"] + 16 * g:CCOL["edge"] + 16 * g + 16] = w / count
    inv = (1.0 / (10000.0 ** (np.arange(0, 32, 2, dtype=np.float32) / 32))).astype(np.float32)
    pos = np.stack([np.repeat(np.arange(ROWS), GRID), np.tile(np.arange(GRID), ROWS)]).astype(np.float32)
    d = r % HD
    ang = pos[d // 32] * inv[d % 16][:, None]
    rope = np.stack([np.cos(ang), np.sin(ang)]).astype(np.float32)
    query, key = np.arange(P), np.arange(NLOC)
    bias = np.full((NQ, P, 6, NLOC), NEG, np.float32)
    for half in range(2):
        qr, kr = 8 * half + query // QW, 4 * half + key // KW
        r0 = np.clip(qr - KH // 2, 0, ROWS - KH)
        row_ok = (kr[None] >= r0[:, None]) & (kr[None] < r0[:, None] + KH)
        for kind, b in enumerate((0, 1, 3)):
            qc, kc = QW * b + query % QW, KCS[b] + key % KW
            c0 = np.clip(qc - QW // 2, 0, GRID - QW)
            ok = row_ok & (kc[None] >= c0[:, None]) & (kc[None] < c0[:, None] + QW)
            dr = np.clip(kr[None] - qr[:, None] + KH - 1, 0, 2 * KH - 2)
            dc = np.clip(kc[None] - qc[:, None] + QW - 1, 0, 2 * QW - 2)
            bias[:, :, 3 * half + kind] = np.where(ok[None], f["rpb_2"][0][:, dr, dc], np.float32(NEG))
    t = np.arange(HALF)
    ang_t = 2 * np.pi / T * (np.outer(t, t) % T)
    ang_c = 2 * np.pi / P * (np.outer(r, r) % P)
    rows = lambda m: m.reshape(4, P, HALF).transpose(1, 0, 2).reshape(P, -1)
    norm = 1.0 / math.sqrt(T * P)
    dft = np.concatenate([rows(np.cos(ang_t)), rows(np.sin(ang_t)), np.cos(ang_c) * norm, np.sin(ang_c) * norm,
                          np.tile(1.0 - 2.0 * (t % 2), (P, 1))], axis=1).astype(np.float32)
    return {
        "ctxT": np.ascontiguousarray(f["ctx_2"][0].T).reshape(KD, P, CTX), "bias": bias, "dft": dft, "w4": w4,
        "xT": np.ascontiguousarray(f["x"][0].T).reshape(KD, P, T),
        "vecs": np.ascontiguousarray(np.concatenate([vec[n] for n, _ in _VECS], axis=1)),
        "consts": con, "rope": rope,
        "w8": np.concatenate(stream), "w6": w6, "w1": np.ascontiguousarray(f["w_pool"][0]),
        "ada": ada, "ada_head": np.ascontiguousarray(head),
    }


def kernel(**inputs):
    import concourse.bacc as bacc
    from concourse.bass_utils import run_bass_kernel_spmd as run

    nc = bacc.Bacc("TRN2", target_bir_lowering=False, num_devices=1)
    arrays = layout(inputs)
    aps = {name: nc.dram_tensor(f"in_{name}", a.shape, mybir.dt.from_np(a.dtype), kind="ExternalInput").ap()
           for name, a in arrays.items()}
    out = nc.dram_tensor("out_xT", (KD, P, T), F32, kind="ExternalOutput").ap()
    build(nc, aps, out)
    r = run(nc, [{f"in_{name}": a for name, a in arrays.items()}], core_ids=[0])
    return np.ascontiguousarray(r.results[0]["out_xT"].reshape(D, T).T).reshape(1, T, D)
```

```python
import math
from contextlib import ExitStack, contextmanager

import numpy as np

import concourse.bass as bass
from concourse import mybir

F32 = mybir.dt.float32
F32R = mybir.dt.float32r
ACT = mybir.ActivationFunctionType
ALU = mybir.AluOpType
AX = mybir.AxisListType

P = 128
D = 1024
T = 1024
KD = D // P
TT = T // P
HALF = 512
HD = 64
NQ, NKV = 8, 2
FF = 2816
FC = FF // P
GROUPS = (8, 8, 6)
POOL_W = (2, 4, 8, 16)
GRID = 64
ROWS = T // GRID
CTX = 256
KH, KW, QW = 8, 32, 16
NLOC = 12 * KW
NB = GRID // QW
EPS = 1e-6
NEG = -1e30
FEW = 16
KCS = [min(max(n * QW - 8, 0), GRID - KW) for n in range(NB)]
KIND = [0, 1, 1, 2]
SCALE = HD ** -0.5

NKEY = NLOC + CTX
NCH = 4 * NB + 2
NDFT = 2 * 4 * HALF + 2 * P + HALF

N_IN, N_OUT1 = 0, 14
MIXES = {8: 0, 10: 1, 12: 2, 13: 3}
POOLS = {6: 0, 7: 1, 9: 2, 11: 3}
N_UP, N_DOWN = [], []
_n = N_OUT1 + KD
for _g in GROUPS:
    N_UP.append(_n)
    N_DOWN.append(_n + 2 * _g)
    _n += 2 * _g + KD
N_ATT2 = _n
N_F = N_ATT2 + 16
N_GF = N_F + 8
N_GC = N_GF + 16
N_A = N_GC + 16
N_GA = N_A + 16
N_OUT2 = N_GA + 16
N_ALL = N_OUT2 + KD

_VECS = [("b_ada", 48), ("norm1_g", 8), ("pool_scale", 4), ("norm2_g", 8), ("conv_w", 132), ("conv_b", 44),
         ("b_ada_2", 24), ("norm_g_2", 8), ("b_in_2", 64), ("w_conv_2", 12), ("b_conv_2", 4), ("final_g_2", 8),
         ("q_norm_g", 1), ("k_norm_g", 1)]
VCOL, NVEC = {}, 0
for _name, _w in _VECS:
    VCOL[_name] = NVEC
    NVEC += _w
_CONSTS = [("ident", 128), ("headmean", 128), ("rot", 128), ("headsel", 2), ("one", 1), ("eps", 1), ("zero", 1), ("edge", 64)]
CCOL, NCONST = {}, 0
for _name, _w in _CONSTS:
    CCOL[_name] = NCONST
    NCONST += _w


class Steps:

    def __init__(self, eng, sem):
        self.eng, self.sem, self.done, self.before = eng, sem, 0, 0

    def did(self, ins):
        ins.then_inc(self.sem, 1)
        self.done += 1

    def settle(self):
        self.eng.wait_ge(self.sem, self.before + self.done)

    @contextmanager
    def loop(self, count, each):
        first = self.done
        with self.eng.Fori(0, count) as it:
            self.before = it * each
            yield it
        assert self.done - first == each, (self.done - first, each)
        self.before, self.done = 0, first + count * each


def build(nc, A, out):
    ctx = ExitStack()
    with ctx:
        BASE = 16512

        def at(name, kb, shape, dt=F32):
            return nc.alloc_sbuf_tensor_at(name, shape, dt, offset=BASE + int(kb * 1024))

        def sem(name):
            return ctx.enter_context(nc.semaphore(name))

        XT = at("XT", 0, [P, KD, T])
        QN = at("QN", 0, [P, 4, T])
        KN = at("KN", 16, [P, T])
        VN = at("VN", 20, [P, T])
        ROPE1 = at("ROPE1", 24, [P, T])
        ROPE2 = at("ROPE2", 28, [P, T])
        KHI = at("KHI", 24, [P, T], F32R)
        KLO = at("KLO", 28, [P, T])
        QST = [at(f"QST{s}", 24 + 4 * s, [P, NQ, P], F32R) for s in range(2)]
        HH = at("HH", 32, [P, KD, T], F32R)
        HL = at("HL", 64, [P, KD, T], F32R)
        SQ = [at(f"SQ{s}", 64 + 4 * s, [P, T]) for s in range(2)]
        PTH = at("PTH", 32, [P, TT, 4, P], F32R)
        PTL = at("PTL", 48, [P, TT, 4, P], F32R)
        EX = [at(f"EX{s}", kb, [P, T]) for s, kb in enumerate((64, 68, 16, 20))]
        VTOK = at("VTOK", 72, [P, TT, NKV, P], F32R)
        C1B = at("C1B", 80, [P, D])
        QH = at("QH", 88, [P, 4, P], F32R)
        QL = at("QL", 90, [P, 4, P])
        OT = at("OT", 92, [P, 4, P])
        OTMP = at("OTMP", 94, [P, HALF])
        ADA1 = [at(f"ADA1{j}", 96 + 16 * j, [P, 4, D]) for j in range(4)]
        C1A = at("C1A", 56, [P, D])
        SQ1 = at("SQ1", 64, [P, KD, T])
        ADA2 = [at(f"ADA2{s}", 144 + 8 * s, [P, 2, D]) for s in range(2)]
        C2B = [at(f"C2B{v}", 120 + 4 * v, [P, D]) for v in range(2)]
        MH = at("MH", 96, [P, KD, T], F32R)
        ML = at("ML", 128, [P, KD, T], F32R)
        COS = at("COS", 96, [P, T])
        SIN = at("SIN", 100, [P, T])
        PLH = at("PLH", 104, [P, T], F32R)
        PLL = at("PLL", 108, [P, T], F32R)
        PAD = 8
        UP = at("UP", 128, [P, T + 2 * PAD])
        WINS = [at("WIN0", 132.5, [P, T + 2 * PAD]), at("WIN1", 137, [P, T + 2 * PAD])]
        GH = at("GH", 96, [P, 8, T], F32R)
        GL = at("GL", 128, [P, 8, T], F32R)
        CX = at("CX", 152, [P, KD, CTX])
        SQC = at("SQC", 120, [P, KD, CTX])
        HCH = at("HCH", 120, [P, KD, CTX], F32R)
        HCL = at("HCL", 152, [P, KD, CTX], F32R)
        BIAS = [at(f"BIAS{j}", 9 * j, [P, 6, NLOC]) for j in range(2)]
        VTOK2 = at("VTOK2", 18, [P, NCH, P])
        PT2 = [at("PT20", 27, [P, NKEY]), at("PT21", 117, [P, NKEY])]
        EX2 = [at(f"EX2{s}", kb, [P, NKEY]) for s, kb in enumerate((112, 114.5, 29.5, 141))]
        Q2 = at("Q2", 128, [P, T])
        K2 = at("K2", 132, [P, T + CTX])
        SZ = at("SZ", 137, [P, T])
        VT2 = at("VT2", 141, [P, NB * ROWS * KW + CTX])
        CBF = at("CBF", 96, [P, 4, T])
        DFT = at("DFT", 0, [P, NDFT])
        VW = at("VW", 20, [P, 8, P])
        VROW = at("VROW", 24, [P, P])
        FE = at("FE", 25, [P, HALF + 1])
        FO = at("FO", 27.25, [P, HALF])
        SB = at("SB", 29.25, [P, HALF])
        ALT = at("ALT", 31.25, [P, 4])
        BRH = at("BRH", 128, [P, 4, T], F32R)
        BRL = at("BRL", 144, [P, 4, T], F32R)
        CBL = at("CBL", 96, [P, 4, T], F32R)
        CBH = at("CBH", 112, [P, 4, T], F32R)
        S = at("S", 0, [P, KD, T])
        SL = at("SL", 0, [P, KD, T], F32R)
        SH = at("SH", 96, [P, KD, T], F32R)
        XT2 = at("XT2", 32, [P, KD, T])
        WF = [at(f"WF{s}", 160 + 4 * s, [P, KD, P]) for s in range(2)]
        ADA3 = [at(f"ADA3{s}", 160 + 4 * s, [P, D]) for s in range(2)]
        WH = [at(f"WH{s}", 168 + 4 * s, [P, KD, P], F32R) for s in range(2)]
        WL = [at(f"WL{s}", 176 + 4 * s, [P, KD, P], F32R) for s in range(2)]
        EV = [at(f"EV{s}", 184 + 4 * s, [P, T]) for s in range(2)]
        CV = [at(f"CV{s}", 192 + 4 * s, [P, T]) for s in range(2)]
        KSH = at("KSH", 184, [P, NKV, T], F32R)
        KSL = at("KSL", 192, [P, NKV, T], F32R)
        VEC = at("VEC", 200, [P, NVEC])
        CON = at("CON", 200 + 1.5625, [P, NCONST])
        small = 200 + 1.5625 + 1.8125
        MOD1 = at("MOD1", small, [P, 48])
        MOD2 = at("MOD2", small + 0.1875, [P, 24, 2])
        A1 = at("A1", small + 0.375, [P, KD])
        A2 = at("A2", small + 0.40625, [P, KD])
        A3 = at("A3", small + 0.4375, [P, KD, 2])
        SD = at("SD", small + 0.59375, [P, TT])
        RS = at("RS", small + 0.625, [P, TT])
        QSD = at("QSD", small + 0.65625, [P, TT, NQ])
        RSP = at("RSP", small + 0.90625, [P, TT, NQ])
        RSN = at("RSN", small + 1.15625, [P, TT, NQ])
        RC2 = at("RC2", small + 0.5, [P, 2])
        SD2 = at("SD2", small + 0.53125, [P, 2])
        MX = at("MX", small + 1.40625, [P, 8])
        NBI = at("NBI", small + 1.4375, [P, 8])
        SUM = at("SUM", small + 1.46875, [P, 8])
        RC = at("RC", small + 1.5, [P, 8])
        DG = [at(f"DG{s}", small + 1.625 + 0.5 * s, [P, P]) for s in range(2)]
        BQ8 = at("BQ8", small + 1.53125, [P, 8])

        def vec(name, j=0, w=1):
            c = VCOL[name] + j
            return VEC[:, c:c + w] if isinstance(j, int) else VEC[:, bass.ds(c, w)]

        def con(name, w, j=0):
            return CON[:, CCOL[name] + j:CCOL[name] + j + w]

        ident, one, eps, zero = con("ident", P), con("one", 1), con("eps", 1), con("zero", 1)

        acc = ctx.enter_context(nc.psum_tensor("acc", [P, 2, T], F32))
        turn = ctx.enter_context(nc.psum_tensor("turn", [P, T], F32))
        bank6 = ctx.enter_context(nc.psum_tensor("bank6", [P, HALF], F32))
        bank7 = ctx.enter_context(nc.psum_tensor("bank7", [P, HALF], F32))

        consts_in, x_in, rope_in = sem("consts_in"), [sem("x_in0"), sem("x_in1")], sem("rope_in")
        cond_in, cond_ready = sem("cond_in"), sem("cond_ready")
        ada1_in = [sem(f"ada1_in{j}") for j in range(4)]
        ada2_in, ada3_in = [sem("ada2_in0"), sem("ada2_in1")], [sem("ada3_in0"), sem("ada3_in1")]
        ada_used = sem("ada_used")
        w_in = [sem("w_in0"), sem("w_in1")]
        w_hi, w_split = sem("w_hi"), sem("w_split")
        acc_done, acc_read, post_done = sem("acc_done"), sem("acc_read"), sem("post_done")
        act_step, dve_step, pool_step = sem("act_step"), sem("dve_step"), sem("pool_step")
        sq_ready, sq_used = sem("sq_ready"), sem("sq_used")
        sd_ready, rs_ready, rb_done = sem("sd_ready"), sem("rs_ready"), sem("rb_done")
        xn_ready, hf_ready, hh_ready, hl_ready = sem("xn_ready"), sem("hf_ready"), sem("hh_ready"), sem("hl_ready")
        mods_ready = sem("mods_ready")
        sqh_ready, qstat_done, rot_done, kms_done = sem("sqh_ready"), sem("qstat_done"), sem("rot_done"), sem("kms_done")
        ksd_ready, qsd_ready, pooled, plh_ready, pll_ready = (
            sem("ksd_ready"), sem("qsd_ready"), sem("pooled"), sem("plh_ready"), sem("pll_ready"))
        mixh_ready = sem("mixh_ready")
        khi_ready, klo_ready, kst_act, kst_dve = sem("khi_ready"), sem("klo_ready"), sem("kst_act"), sem("kst_dve")
        vt_done, vh_ready, vl_ready = sem("vt_done"), sem("vh_ready"), sem("vl_ready")
        qh_ready, qst_act, qst_dve = sem("qh_ready"), sem("qst_act"), sem("qst_dve")
        scores_done, nb_ready, exp_done, rc_ready, dga_ready = (
            sem("scores_done"), sem("nb_ready"), sem("exp_done"), sem("rc_ready"), sem("dga_ready"))
        pt_done, pth_ready, ptl_ready, pv_done, otmp_ready, o_ready, mh_ready, ml_ready = (
            sem("pt_done"), sem("pth_ready"), sem("ptl_ready"), sem("pv_done"), sem("otmp_ready"), sem("o_ready"),
            sem("mh_ready"), sem("ml_ready"))
        x_again = [sem(f"x_again{k}") for k in range(KD)]
        gated, gh_ready = sem("gated"), sem("gh_ready")
        silu_done = sem("silu_done")
        cx_in, csq_ready, cstat_done, csd_ready, crs_ready, crb_done = (
            sem("cx_in"), sem("csq_ready"), sem("cstat_done"), sem("csd_ready"), sem("crs_ready"), sem("crb_done"))
        cxn_ready, ch_ready, hch_ready, hcl_ready = sem("cxn_ready"), sem("ch_ready"), sem("hch_ready"), sem("hcl_ready")
        x_saved, x_back = sem("x_saved"), sem("x_back")
        bias_in = [sem("bias_in0"), sem("bias_in1")]
        vt2_done, vtok2_ready = sem("vt2_done"), sem("vtok2_ready")
        scores2_done, nb2_ready, exp2_done, dg_ready, pt2_done, pt2_ready, pv2_done, o2_ready = (
            sem("scores2_done"), sem("nb2_ready"), sem("exp2_done"), sem("dg_ready"), sem("pt2_done"), sem("pt2_ready"),
            sem("pv2_done"), sem("o2_ready"))
        cbh_ready, cbl_ready = sem("cbh_ready"), sem("cbl_ready")
        dft_in, fold_ready, chan_done, vw_ready, seq_done, sb_ready, y_ready, brh_ready = (
            sem("dft_in"), sem("fold_ready"), sem("chan_done"), sem("vw_ready"), sem("seq_done"), sem("sb_ready"),
            sem("y_ready"), sem("brh_ready"))
        sums_ready, sh_ready = sem("sums_ready"), sem("sh_ready")
        out_ready, out_sent = sem("out_ready"), sem("out_sent")

        def span(t):
            return slice(t, t + P) if isinstance(t, int) else bass.ds(t, P)

        def block_of(k):
            return slice(k, k + 1) if isinstance(k, int) else bass.ds(k, 1)

        def column(x, c):
            x = x[:, :, :].rearrange("p t h -> p (t h)")
            return x[:, c:c + 1] if isinstance(c, int) else x[:, bass.ds(c, 1)]

        block = ctx.enter_context(nc.Block())

        @block.sync
        def _(sp):
            def load_w(n, slot, name, index, k, first=False):
                if not first:
                    sp.wait_ge(w_split, n - 1)
                sp.dma_start(WF[slot][:, 0:k, :], A[name][index, :, :].rearrange("p (k n) -> p k n", n=P)
                             if isinstance(index, int) else
                             A[name][bass.ds(index, 1), :, :].rearrange("a p (k n) -> (a p) k n", n=P)
                             ).then_inc(w_in[slot], 16)

            sp.dma_start(VEC[:, :], A["vecs"]).then_inc(consts_in, 16)
            sp.dma_start(CON[:, :], A["consts"]).then_inc(consts_in, 16)
            sp.dma_start(C1A[:, :], A["conds"][0]).then_inc(cond_in, 16)
            for j in range(2):
                sp.dma_start(XT[:, 4 * j:4 * j + 4, :], A["xT"][4 * j:4 * j + 4].rearrange("k p t -> p k t")).then_inc(x_in[j], 16)
            for j in range(4):
                sp.dma_start(ADA1[j][:, :, :], A["ada"][4 * j:4 * j + 4].rearrange("a p i -> p a i")).then_inc(ada1_in[j], 16)
            w8 = 0
            for n in range(2):
                load_w(n, n % 2, "w8", w8, KD, first=True)
                w8 += 1
            sp.wait_ge(mods_ready, 1)
            sp.dma_start(COS[:, :], A["rope"][0]).then_inc(rope_in, 16)
            sp.dma_start(SIN[:, :], A["rope"][1]).then_inc(rope_in, 16)
            for v in range(2):
                sp.dma_start(C2B[v][:, :], A["conds"][1 + v]).then_inc(cond_in, 16)

            def load_ada2(h):
                if h >= 2:
                    sp.wait_ge(ada_used, 16 + 2 * h - 2)
                sp.dma_start(ADA2[h % 2][:, :, :], A["ada"][48 + 2 * h:50 + 2 * h].rearrange("a p i -> p a i")
                             ).then_inc(ada2_in[h % 2], 16)

            load_ada2(0)
            load_ada2(1)
            for n in range(2, N_OUT1 + 2):
                if n in MIXES:
                    load_w(n, n % 2, "w1", MIXES[n], 1)
                else:
                    load_w(n, n % 2, "w8", w8, KD)
                    w8 += 1
                if n < 10:
                    for h in range(2 + 10 * (n - 2) // 8, 2 + 10 * (n - 1) // 8):
                        load_ada2(h)
            sp.wait_ge(acc_done, N_OUT1)
            sp.wait_ge(hl_ready, KD)
            sp.dma_start(C1B[:, :], A["conds"][0]).then_inc(cond_in, 16)
            sp.wait_ge(w_split, N_OUT1 + 2)
            for s in range(2):
                sp.dma_start(ADA3[s][:, :], A["ada"][16 + s]).then_inc(ada3_in[s], 16)
            with sp.Fori(1, 16) as it:
                for s in range(2):
                    src = A["ada"][bass.ds(it * 2 + (16 + s), 1), :, :].rearrange("a p i -> (a p) i")
                    sp.wait_ge(ada_used, it * 2 + (40 + s - 1))
                    sp.dma_start(ADA3[s][:, :], src).then_inc(ada3_in[s], 16)
            sp.wait_ge(pv_done, 16)
            for k in range(KD):
                sp.dma_start(XT[:, k, :], A["xT"][k]).then_inc(x_again[k], 16)
            sp.wait_ge(ada_used, 72)
            with sp.Fori(0, 3) as it:
                for s in range(2):
                    load_w(it * 2 + (N_OUT1 + 2 + s), s, "w8", it * 2 + (w8 + s), KD)
            w8 += 6
            for g, gk in enumerate(GROUPS):
                for s in range(2):
                    load_w(N_UP[g] + s, s, "w8", w8 + s, KD)
                if g == 2:
                    sp.wait_ge(acc_done, N_UP[2])
                    sp.dma_start(CX[:, :, :], A["ctxT"].rearrange("k p t -> p k t")).then_inc(cx_in, 16)
                with sp.Fori(1, gk) as it:
                    for s in range(2):
                        load_w(it * 2 + (N_UP[g] + s), s, "w8", it * 2 + (w8 + s), KD)
                w8 += 2 * gk
                name, first = ("w8", w8) if gk == KD else ("w6", 0)
                with sp.Fori(0, 4) as it:
                    for s in range(2):
                        load_w(it * 2 + (N_DOWN[g] + s), s, name, it * 2 + (first + s), gk)
                if gk == KD:
                    w8 += KD
            for s in range(2):
                load_w(N_ATT2 + s, s, "w8", w8 + s, KD)
            sp.wait_ge(post_done, N_ATT2)
            sp.dma_start(out.rearrange("k p t -> p k t"), XT[:, :, :]).then_inc(x_saved, 16)
            sp.wait_ge(x_saved, 16)
            sp.wait_ge(xn_ready, 3 * KD)
            for j in range(2):
                sp.dma_start(BIAS[j][:, :, :], A["bias"][j]).then_inc(bias_in[j], 16)
            for s in range(2):
                load_w(N_ATT2 + 2 + s, s, "w8", w8 + 2 + s, KD)
            with sp.Fori(1, 4) as it:
                for s in range(2):
                    load_w(it * 4 + (N_ATT2 + s), s, "w8", it * 4 + (w8 + s), KD)
                for j in range(2):
                    src = A["bias"][bass.ds(it * 2 + j, 1), :, :, :].rearrange("a p k n -> (a p) k n")
                    sp.wait_ge(nb2_ready, it * 16 + (8 * j - 8))
                    sp.dma_start(BIAS[j][:, :, :], src).then_inc(bias_in[j], 16)
                for s in range(2):
                    load_w(it * 4 + (N_ATT2 + 2 + s), s, "w8", it * 4 + (w8 + 2 + s), KD)
            w8 += 16
            for s in range(2):
                load_w(N_F + s, s, "w8", w8 + s, KD)
            sp.wait_ge(nb2_ready, 64)
            sp.wait_ge(pt2_done, 64)
            sp.wait_ge(pv2_done, 64)
            sp.dma_start(DFT[:, :], A["dft"]).then_inc(dft_in, 16)
            with sp.Fori(1, 4) as it:
                for s in range(2):
                    load_w(it * 2 + (N_F + s), s, "w8", it * 2 + (w8 + s), KD)
            w8 += 8

            def gate_weights(n0, w8, w4):
                with sp.Fori(0, KD) as it:
                    load_w(it * 2 + n0, 0, "w8", it + w8, KD)
                    load_w(it * 2 + (n0 + 1), 1, "w4", it + w4, 4)

            gate_weights(N_GF, w8, 0)
            gate_weights(N_GC, w8 + KD, KD)
            w8 += 2 * KD
            with sp.Fori(0, 8) as it:
                for s in range(2):
                    load_w(it * 2 + (N_A + s), s, "w8", it * 2 + (w8 + s), KD)
            w8 += 16
            gate_weights(N_GA, w8, 2 * KD)
            w8 += KD
            for s in range(2):
                load_w(N_OUT2 + s, s, "w8", w8 + s, KD)
            sp.wait_ge(acc_done, N_OUT2 - 1)
            sp.dma_start(XT2[:, :, :], out.rearrange("k p t -> p k t")).then_inc(x_back, 16)
            with sp.Fori(1, 4) as it:
                for s in range(2):
                    load_w(it * 2 + (N_OUT2 + s), s, "w8", it * 2 + (w8 + s), KD)
            for k in range(KD):
                sp.wait_ge(out_ready, k + 1)
                sp.dma_start(out[k], XT2[:, k, :]).then_inc(out_sent, 16)
            sp.wait_ge(out_sent, 16 * KD)

        @block.gpsimd
        def _(pool):
            steps = Steps(pool, pool_step)

            def split_w(n, slot, k, first=False):
                pool.wait_ge(w_in[slot], (n - slot) * 8 + 16)
                if not first:
                    pool.wait_ge(acc_done, n - 1)
                f, h = WF[slot][:, :, :].rearrange("p k n -> p (k n)"), WH[slot][:, :, :].rearrange("p k n -> p (k n)")
                pool.tensor_tensor(h[:, 0:FEW], f[:, 0:FEW], zero.to_broadcast([P, FEW]), ALU.add).then_inc(w_hi, 1)
                pool.tensor_scalar(h[:, FEW:k * P], f[:, FEW:k * P], 1.0, 1.0, ALU.mult, ALU.mult).then_inc(w_hi, 1)
                pool.wait_ge(w_hi, n * 2 + 2)
                pool.tensor_tensor(WL[slot][:, 0:k, :], WF[slot][:, 0:k, :], WH[slot][:, 0:k, :].bitcast(F32),
                                   ALU.subtract).then_inc(w_split, 1)

            pool.wait_ge(consts_in, 32)
            for n in range(N_OUT1 + 2):
                split_w(n, n % 2, 1 if n in MIXES else KD, first=n < 2)
            with pool.Fori(0, 3) as it:
                for s in range(2):
                    split_w(it * 2 + (N_OUT1 + 2 + s), s, KD)
            for g, gk in enumerate(GROUPS):
                with pool.Fori(0, gk) as it:
                    for s in range(2):
                        split_w(it * 2 + (N_UP[g] + s), s, KD)
                with pool.Fori(0, 4) as it:
                    for s in range(2):
                        split_w(it * 2 + (N_DOWN[g] + s), s, gk)
            for n0, count, k1 in ((N_ATT2, 12, KD), (N_GF, 16, 4), (N_A, 8, KD), (N_GA, 8, 4), (N_OUT2, 4, KD)):
                with pool.Fori(0, count) as it:
                    split_w(it * 2 + n0, 0, KD)
                    split_w(it * 2 + (n0 + 1), 1, k1)

        @block.tensor
        def _(pe):
            def gemm(n, slot, hi, lo, k_n=KD, ready=None, context=None, last_chunk=None):
                pe.wait_ge(w_split, n + 1)
                if not isinstance(n, int) or n >= 2:
                    pe.wait_ge(acc_read, n - 1)
                for k in range(k_n):
                    if ready is not None:
                        pe.wait_ge(ready, hl_base[0] + k + 1)
                    if k == k_n - 1 and last_chunk is not None:
                        pe.wait_ge(post_done, last_chunk)
                    for w, x in ((WH, hi), (WH, lo), (WL, hi)):
                        for c in range(2):
                            last = pe.matmul(acc[:, slot, HALF * c:HALF * c + HALF], w[slot][:, k, :],
                                             x[:, k, HALF * c:HALF * c + HALF],
                                             start=(k == 0 and w is WH and x is hi), stop=(k == k_n - 1 and w is WL))
                if context is not None:
                    for k in range(k_n):
                        for w, x in ((WH, HCH), (WH, HCL), (WL, HCH)):
                            last = pe.matmul(context[:, 0:CTX], w[slot][:, k, :], x[:, k, :],
                                             start=(k == 0 and w is WH and x is HCH), stop=(k == k_n - 1 and w is WL))
                last.then_inc(acc_done, 1)

            hl_base = [0]

            def stats(q, k, first, last, nt=TT):
                pe.wait_ge(sq_ready, q * KD + k + 1)
                for t in range(nt):
                    mm = pe.matmul(bank6[:, t:t + 1], SQ[slot_of(k)][:, P * t:P * t + P], one,
                                   start=(first and t == 0), stop=last, skip_group_check=True)
                mm.then_inc(sq_used, 1)

            slot_now = [0]

            def slot_of(k):
                return k % 2 if isinstance(k, int) else slot_now[0]

            def spread_rs(q, nt=TT):
                pe.wait_ge(rs_ready, q + 1)
                for t in range(nt):
                    mm = pe.matmul(turn[:, P * t:P * t + P], RS[:, t:t + 1].to_broadcast([P, P]), ident,
                                   start=True, stop=True)
                mm.then_inc(rb_done, 1)

            pe.wait_ge(consts_in, 32)
            for k in range(KD):
                pe.wait_ge(sq_ready, k + 1)
                for t in range(TT):
                    mm = pe.matmul(bank6[:, t:t + 1], SQ1[:, k, P * t:P * t + P], one,
                                   start=(k == 0 and t == 0), stop=(k == KD - 1), skip_group_check=True)
                mm.then_inc(sq_used, 1)
            spread_rs(0)

            def rotate(m):
                n = [0, 2, 3, 4, 5][m]
                pe.wait_ge(sqh_ready, m + 1)
                if m == 0:
                    for c in range(2):
                        mm = pe.matmul(turn[:, HALF * c:HALF * c + HALF], con("headmean", P),
                                       CV[n % 2][:, HALF * c:HALF * c + HALF], start=True, stop=True)
                    mm.then_inc(kms_done, 1)
                    pe.wait_ge(ksd_ready, 1)
                else:
                    for t in range(TT):
                        mm = pe.matmul(bank6[:, 64 + t * NQ + 2 * (m - 1):64 + t * NQ + 2 * m],
                                       CV[n % 2][:, P * t:P * t + P], con("headsel", 2), start=True, stop=True)
                    mm.then_inc(qstat_done, 1)
                if m > 0:
                    pe.wait_ge(post_done, [0, 2, 3, 4, 5][m - 1] + 1)
                for c in range(2):
                    mm = pe.matmul(turn[:, HALF * c:HALF * c + HALF], con("rot", P), EV[n % 2][:, HALF * c:HALF * c + HALF],
                                   start=True, stop=True)
                mm.then_inc(rot_done, 1)

            for n in range(N_OUT1):
                if n in MIXES:
                    g = MIXES[n]
                    pe.wait_ge(w_split, n + 1)
                    pe.wait_ge(acc_read, n - 1)
                    pe.wait_ge(pll_ready, g + 1)
                    for w, x in ((WH, PLH), (WH, PLL), (WL, PLH)):
                        for c in range(2):
                            mm = pe.matmul(acc[:, n % 2, HALF * c:HALF * c + HALF], w[n % 2][:, 0, :],
                                           x[:, HALF * c:HALF * c + HALF],
                                           start=(w is WH and x is PLH), stop=(w is WL))
                    mm.then_inc(acc_done, 1)
                else:
                    gemm(n, n % 2, HH, HL, ready=hl_ready if n == 0 else None)
                if n == 1:
                    rotate(0)
                if 3 <= n <= 6:
                    rotate(n - 2)
            for t in range(TT):
                mm = pe.transpose(turn[:, P * t:P * t + P], VN[:, P * t:P * t + P], ident)
            mm.then_inc(vt_done, 1)
            pe.wait_ge(kst_act, 4)
            pe.wait_ge(kst_dve, 4)
            pe.wait_ge(acc_read, N_OUT1)
            pe.wait_ge(vl_ready, 1)

            def scores(it, u):
                s, h = u // 8 % 2, u % 8
                if u % 8 == 0:
                    pe.wait_ge(qst_act, it * 4 + (2 * (u // 8) + 2))
                    pe.wait_ge(qst_dve, it * 4 + (2 * (u // 8) + 2))
                if u >= 2:
                    pe.wait_ge(exp_done, it * 16 + (u - 1))
                for ks in (KSH, KSL):
                    for c in range(2):
                        mm = pe.matmul(acc[:, u % 2, HALF * c:HALF * c + HALF], QST[s][:, h, :],
                                       ks[:, h // 4, HALF * c:HALF * c + HALF], start=(ks is KSH), stop=(ks is KSL))
                mm.then_inc(scores_done, 1)

            def attend(it, last):
                for u in range(16):
                    now = it * 32 + 2 * u
                    if u % 4 != 0 and (u < 14 or not last):
                        scores(it, u + 2)
                    pe.wait_ge(dga_ready, it * 16 + (u + 1))
                    for h in range(2):
                        pe.wait_ge(ptl_ready, now + (h + 1))
                        for k in range(4 * h, 4 * h + 4):
                            mm = pe.matmul(turn[:, P * k:P * k + P], EX[u % 4][:, P * k:P * k + P], DG[u % 2][:, :],
                                           start=True, stop=True)
                        mm.then_inc(pt_done, 1)
                    if u % 4 == 3:
                        if u < 13 or not last:
                            scores(it, u + 3)
                        b = u // 4
                        pe.wait_ge(o_ready, it * 4 + (b + 1))
                        for k in range(TT):
                            if k % 4 == 0:
                                pe.wait_ge(ptl_ready, now + (2 + k // 4 + 1))
                            for x in (PTH, PTL):
                                mm = pe.matmul(bank6[:, :], VTOK[:, k, b % 2, :], x[:, k, :, :],
                                               start=(k == 0 and x is PTH), stop=(k == TT - 1 and x is PTL))
                        mm.then_inc(pv_done, 1)

            for u in range(3):
                scores(0, u)
            with pe.Fori(0, 3) as it:
                attend(it, False)
            attend(3, True)
            pe.wait_ge(o_ready, 17)
            pe.wait_ge(ml_ready, 8)
            pe.wait_ge(mh_ready, 8)
            pe.wait_ge(exp_done, 64)

            def residual_tiles(q, n0, hi, lo, k_n, with_stats, last_chunk=None):
                def pair(it, first):
                    for s in range(2):
                        gemm(it * 2 + (n0 + s), s, hi, lo, k_n, last_chunk=last_chunk if first and s == 0 else None)
                        if with_stats and not (first and s == 0):
                            slot_now[0] = 1 - s
                            stats(q, it * 2 + (s - 1), first and s == 1, False)
                pair(0, True)
                with pe.Fori(1, 4) as it:
                    pair(it, False)
                if with_stats:
                    stats(q, KD - 1, False, True)

            residual_tiles(1, N_OUT1, MH, ML, KD, True)
            spread_rs(1)
            for g, gk in enumerate(GROUPS):
                hl_base[0] = KD
                gemm(N_UP[g], 0, HH, HL, ready=hl_ready if g == 0 else None)
                gemm(N_UP[g] + 1, 1, HH, HL)
                if g == 2:
                    pe.wait_ge(csq_ready, 1)
                    for t in range(2):
                        for k in range(KD):
                            mm = pe.matmul(bank6[:, 16 + t:17 + t], SQC[:, k, P * t:P * t + P], one,
                                           start=(k == 0), stop=(k == KD - 1))
                    mm.then_inc(cstat_done, 1)
                with pe.Fori(1, gk) as it:
                    for s in range(2):
                        gemm(it * 2 + (N_UP[g] + s), s, HH, HL)
                if g == 2:
                    pe.wait_ge(crs_ready, 1)
                    for t in range(2):
                        mm = pe.matmul(turn[:, P * t:P * t + P], RC2[:, t:t + 1].to_broadcast([P, P]), ident,
                                       start=True, stop=True)
                    mm.then_inc(crb_done, 1)
                pe.wait_ge(post_done, N_UP[g] + 2 * gk - 2)
                residual_tiles(2, N_DOWN[g], GH, GL, gk, g == 2, last_chunk=N_UP[g] + 2 * gk)

            pe.wait_ge(cxn_ready, 1)
            spread_rs(2)
            hl_base[0] = 2 * KD

            def att_pair(n, pair, first):
                u0 = pair * 16
                if not first:
                    pe.wait_ge(exp2_done, u0)
                    pe.wait_ge(o2_ready, u0)
                else:
                    pe.wait_ge(hcl_ready, 1)
                gemm(n, 0, HH, HL, ready=hl_ready if first else None, context=bank7)
                gemm(n + 1, 1, HH, HL, context=bank6)
                gemm(n + 2, 0, HH, HL)
                pe.wait_ge(acc_read, n + 2)
                if first:
                    pe.wait_ge(xn_ready, 3 * KD)

                def turn_values(b, c0, c1):
                    if b > 0:
                        pe.wait_ge(vtok2_ready, pair * 3 + b)
                    for c in range(c0, c1):
                        mm = pe.transpose(turn[:, P * (c - c0):P * (c - c0) + P], VT2[:, P * c:P * c + P], ident)
                    mm.then_inc(vt2_done, 1)

                turn_values(0, 0, 8)
                gemm(n + 3, 1, HH, HL)
                turn_values(1, 8, 16)
                turn_values(2, 16, 18)

                def scores(u):
                    j, half, c = u // 8, u // 4 % 2, u % NB
                    a = acc[:, u % 2, :]
                    if u < 2:
                        pe.wait_ge(acc_read, n + 4)
                    else:
                        pe.wait_ge(exp2_done, u0 + (u - 1))
                    rows = K2[HD * j:HD * j + HD, 0:T].rearrange("p (r c) -> p r c", c=GRID)
                    q = Q2[HD * j:HD * j + HD, HALF * half + P * c:HALF * half + P * c + P]
                    pe.matmul(a[:, P:P + NLOC], q, rows[:, 4 * half:4 * half + 12, KCS[c]:KCS[c] + KW], start=True, stop=True)
                    pe.matmul(a[:, HALF:HALF + CTX], q, K2[HD * j:HD * j + HD, T:T + CTX], start=True, stop=True
                              ).then_inc(scores2_done, 1)

                def turn_probs(u):
                    pe.wait_ge(dg_ready, u0 + (u + 1))
                    if u == 0:
                        pe.wait_ge(vtok2_ready, pair * 3 + 3)
                    else:
                        pe.wait_ge(pt2_ready, u0 + u)
                    for k in range(NKEY // P):
                        mm = pe.matmul(turn[:, P * k:P * k + P], EX2[u % 4][:, P * k:P * k + P], DG[u % 2][:, :],
                                       start=True, stop=True)
                    mm.then_inc(pt2_done, 1)

                def values(u):
                    half, c = u // 4 % 2, u % NB
                    pe.wait_ge(pt2_ready, u0 + (u + 1))
                    if u >= 2:
                        pe.wait_ge(o2_ready, u0 + (u - 1))
                    bank = (bank6, bank7)[u % 2]
                    for k in range(NKEY // P):
                        kc = 4 * c + half + k if k < 3 else 4 * NB + k - 3
                        mm = pe.matmul(bank[:, 0:P], VTOK2[:, kc, :], PT2[u % 2][:, P * k:P * k + P],
                                       start=(k == 0), stop=(k == NKEY // P - 1))
                    mm.then_inc(pv2_done, 1)

                scores(0)
                scores(1)
                for u in range(16):
                    if u < 14:
                        scores(u + 2)
                    if u > 0:
                        values(u - 1)
                    turn_probs(u)
                values(15)

            att_pair(N_ATT2, 0, True)
            with pe.Fori(1, 4) as it:
                att_pair(it * 4 + N_ATT2, it, False)

            pe.wait_ge(exp2_done, 64)
            pe.wait_ge(o2_ready, 64)
            pe.wait_ge(dft_in, 16)
            COS_T, SIN_T = DFT[:, 0:4 * HALF], DFT[:, 4 * HALF:8 * HALF]
            COS_C, SIN_C = DFT[:, 8 * HALF:8 * HALF + P], DFT[:, 8 * HALF + P:8 * HALF + 2 * P]
            SIGNS = DFT[0:1, 8 * HALF + 2 * P:NDFT]

            def channels(it):
                pe.wait_ge(fold_ready, it + 1)
                pe.wait_ge(y_ready, it * 2 + 1)
                for f, c, o in ((FE, COS_C, 0), (FO, SIN_C, HALF)):
                    for t in range(4):
                        pe.matmul(turn[:, o + P * t:o + P * t + P], f[:, P * t:P * t + P], c, start=True, stop=True)
                pe.matmul(bank6[0:1, 0:P], FE[:, HALF:HALF + 1], COS_C, start=True, stop=True)
                pe.matmul(bank6[:, P:P + 1], COS_C, ALT[:, 2:3], start=True, stop=True).then_inc(chan_done, 1)

            def tokens(it):
                pe.wait_ge(vw_ready, it * 2 + 2)
                for t in range(4):
                    pe.matmul(bank7[:, :], VW[:, t, :], COS_T[:, HALF * t:HALF * t + HALF], start=(t == 0), stop=False)
                pe.matmul(bank7[:, :], VROW[0:1, :], SIGNS, start=False, stop=True)
                for t in range(4):
                    mm = pe.matmul(bank6[:, :], VW[:, 4 + t, :], SIN_T[:, HALF * t:HALF * t + HALF], start=(t == 0), stop=(t == 3))
                mm.then_inc(seq_done, 1)

            gemm(N_F, 0, HH, HL)
            gemm(N_F + 1, 1, HH, HL)
            channels(0)
            with pe.Fori(1, 4) as it:
                n = it * 2 + N_F
                gemm(n, 0, HH, HL)
                tokens(it - 1)
                gemm(n + 1, 1, HH, HL)
                channels(it)
            tokens(3)

            def gates(n0, hi, lo, sem_, value):
                with pe.Fori(0, KD) as it:
                    gemm(it * 2 + n0, 0, HH, HL)
                    pe.wait_ge(sem_, value)
                    gemm(it * 2 + (n0 + 1), 1, hi, lo, 4)

            gates(N_GF, BRH, BRL, post_done, N_GF)
            gates(N_GC, CBH, CBL, cbl_ready, 1)
            with pe.Fori(0, 8) as it:
                for s in range(2):
                    gemm(it * 2 + (N_A + s), s, HH, HL)
            gates(N_GA, BRH, BRL, post_done, N_GA)
            pe.wait_ge(post_done, N_OUT2)
            residual_tiles(3, N_OUT2, SH, SL, KD, True)
            spread_rs(3)

        @block.scalar
        def _(act):
            steps = Steps(act, act_step)

            def evac_wait(n):
                act.wait_ge(acc_done, n + 1)
                if not isinstance(n, int) or n >= 2:
                    act.wait_ge(post_done, n - 1)

            def square(q, k, slot, src):
                if not isinstance(k, int) or q * KD + k >= 2:
                    act.wait_ge(sq_used, q * KD + k - 1)
                act.activation(SQ[slot][:, :], src, ACT.Square).then_inc(sq_ready, 1)

            def root(q, nt=TT):
                act.wait_ge(sq_used, q * KD + KD)
                act.activation(SD[:, 0:nt], bank6[:, 0:nt], ACT.Sqrt, bias=eps, scale=1.0 / D).then_inc(sd_ready, 1)

            def modulate(q, scale, shift, hh):
                for k in range(KD):
                    act.wait_ge(xn_ready, q * KD + k + 1)
                    if k >= 2:
                        act.wait_ge(hl_ready, q * KD + k - 1)
                    act.activation(CV[k % 2][:, :], EV[k % 2][:, :], ACT.Identity, bias=shift(k), scale=scale(k)
                                   ).then_inc(hf_ready, 1)
                    act.wait_ge(hf_ready, q * KD + k + 1)
                    act.activation(hh[:, k, :], CV[k % 2][:, :], ACT.Copy).then_inc(hh_ready, 1)

            act.wait_ge(consts_in, 32)
            act.wait_ge(cond_in, 16)
            act.activation(C1A[:, :], C1A[:, :], ACT.Silu).then_inc(cond_ready, 1)
            for k in range(KD):
                if k % 4 == 0:
                    act.wait_ge(x_in[k // 4], 16)
                act.activation(SQ1[:, k, :], XT[:, k, :], ACT.Square).then_inc(sq_ready, 1)
            root(0)
            act.wait_ge(mods_ready, 1)
            modulate(0, lambda k: A1[:, k:k + 1], lambda k: MOD1[:, k:k + 1], HH)

            act.wait_ge(cond_in, 48)
            for v in range(2):
                act.activation(C2B[v][:, :], C2B[v][:, :], ACT.Silu).then_inc(cond_ready, 1)

            def pool_first(g):
                act.wait_ge(pooled, g + 1)
                if g > 0:
                    act.wait_ge(acc_done, [8, 10, 12, 13][g - 1] + 1)
                act.activation(PLH[:, :], UP[:, PAD:PAD + T], ACT.Copy).then_inc(plh_ready, 1)

            for n in range(N_OUT1):
                evac_wait(n)
                src, slot = acc[:, n % 2, :], n % 2
                if n == 1 or n in POOLS:
                    act.activation(EV[slot][:, :], src, ACT.Copy).then_inc(acc_read, 1)
                elif n in MIXES:
                    g = MIXES[n]
                    act.activation(EV[slot][:, :], src, ACT.Copy, scale=vec("pool_scale", g)).then_inc(acc_read, 1)
                    act.wait_ge(acc_read, n + 1)
                    act.activation(MH[:, 4 + g, :], EV[slot][:, :], ACT.Copy).then_inc(mixh_ready, 1)
                else:
                    m = [0, None, 1, 2, 3, 4][n]
                    if m > 1:
                        act.wait_ge(qstat_done, m - 1)
                    steps.did(act.activation(CV[slot][:, :], src, ACT.Square))
                    act.activation(EV[slot][:, :], src, ACT.Copy, scale=vec("k_norm_g" if n == 0 else "q_norm_g")
                                   ).then_inc(acc_read, 1)
                    act.wait_ge(acc_read, n + 1)
                    steps.settle()
                    act.activation(SUM[:, 7:8], eps, ACT.Copy).then_inc(sqh_ready, 1)
                    if m == 0:
                        act.wait_ge(kms_done, 1)
                        act.activation(CV[1][:, :], turn[:, :], ACT.Sqrt, bias=eps).then_inc(ksd_ready, 1)
                if n in (7, 9, 11, 12):
                    pool_first([7, 9, 11, 12].index(n))
            act.wait_ge(qstat_done, 4)
            act.activation(QSD[:, :, :], bank6[:, 64:64 + TT * NQ].rearrange("p (t h) -> p t h", h=NQ), ACT.Sqrt, bias=eps,
                           scale=1.0 / HD).then_inc(qsd_ready, 1)
            act.wait_ge(post_done, N_OUT1)
            act.activation(KHI[:, :], KN[:, :], ACT.Copy).then_inc(khi_ready, 1)
            act.wait_ge(khi_ready, 1)
            for kv in range(NKV):
                for b in range(2):
                    act.activation(KSH[64 * b:64 * b + 64, kv, :], KHI[64 * kv:64 * kv + 64, :].bitcast(F32), ACT.Copy
                                   ).then_inc(kst_act, 1)
            act.wait_ge(vt_done, 1)
            vt = turn[:, :].rearrange("p (a d) -> p a d", d=HD)
            vdst = VTOK[:, :, :, :].rearrange("p t v d -> p (t v) d")
            act.wait_ge(acc_done, N_OUT1)
            act.wait_ge(kst_act, 4)
            act.activation(vdst[:, :, 0:HD], vt, ACT.Copy).then_inc(vh_ready, 1)

            act.wait_ge(kst_dve, 4)
            def stack_queries(it, s):
                m = 2 * it + s
                if not (isinstance(m, int) and m == 0):
                    act.wait_ge(qst_dve, it * 4 + 2 * s)
                    act.wait_ge(qst_act, it * 4 + 2 * s)
                act.activation(QH[:, :, :], QN[:, :, span(it * 256 + 128 * s)], ACT.Copy).then_inc(qh_ready, 1)
                act.wait_ge(qh_ready, it * 2 + (s + 1))
                for b in range(2):
                    dst = QST[s % 2][0:64, :, :].rearrange("p (i j) q -> p i j q", j=2)[:, :, b, :]
                    act.activation(dst, QH[64 * b:64 * b + 64, :, :].bitcast(F32), ACT.Copy).then_inc(qst_act, 1)

            def exponents(it, u):
                act.wait_ge(nb_ready, it * 16 + (u + 1))
                act.activation(EX[u % 4][:, :], acc[:, u % 2, :], ACT.Exp, bias=NBI[:, u % 2:u % 2 + 1],
                               scale=column(RSP, it * 16 + u), accum_out=SUM[:, u % 2:u % 2 + 1]).then_inc(exp_done, 1)

            def attend(it, last):
                for u in range(16):
                    if u % 4 == 0 and not (isinstance(it, int) and it == 0 and u == 0):
                        act.wait_ge(pv_done, it * 4 + (u // 4))
                    for h in range(2):
                        act.wait_ge(pt_done, it * 32 + (2 * u + h + 1))
                        act.activation(PTH[:, 4 * h:4 * h + 4, u % 4, :],
                                       turn[:, HALF * h:HALF * h + HALF].rearrange("p (k q) -> p k q", q=P), ACT.Copy
                                       ).then_inc(pth_ready, 1)
                    if u < 14 or not last:
                        exponents(it, u + 2)
                    if u % 4 == 0:
                        if u > 0:
                            gather_o(it, u // 4 - 1)
                    if u == 1:
                        stack_queries(it, 1)
                    if u == 9 and not last:
                        stack_queries(it, 2)
                gather_o(it, 3)

            def gather_o(it, b):
                act.wait_ge(pv_done, it * 4 + (b + 1))
                act.wait_ge(o_ready, it * 4 + (b + 1))
                act.activation(OTMP[0:64, :], bank6[64:128, :], ACT.Copy).then_inc(otmp_ready, 1)
                if b % 2 == 1:
                    act.wait_ge(o_ready, it * 4 + (b + 2))
                    act.activation(MH[:, 0:4, span(it * 256 + 128 * (b // 2))], OT[:, :, :], ACT.Copy).then_inc(mh_ready, 1)

            act.wait_ge(cond_in, 64)
            act.activation(C1B[:, :], C1B[:, :], ACT.Silu).then_inc(cond_ready, 1)
            stack_queries(0, 0)
            exponents(0, 0)
            exponents(0, 1)
            with act.Fori(0, 3) as it:
                attend(it, False)
            attend(3, True)
            act.wait_ge(ml_ready, 8)

            def residual_tiles(q, n0, gate, with_stats, stream=XT):
                with act.Fori(0, 4) as it:
                    for s in range(2):
                        n = it * 2 + (n0 + s)
                        evac_wait(n)
                        act.activation(EV[s][:, :], acc[:, s, :], ACT.Copy,
                                       scale=gate(it * 2 + s)).then_inc(acc_read, 1)
                        if with_stats:
                            act.wait_ge(post_done, n + 1)
                            square(q, it * 2 + s, s, stream[:, bass.ds(it * 2 + s, 1), :])

            act.wait_ge(mods_ready, 2)
            residual_tiles(1, N_OUT1, lambda k: MOD1[:, bass.ds(k + 16, 1)], True)
            root(1)
            modulate(1, lambda k: A2[:, k:k + 1], lambda k: MOD1[:, 24 + k:25 + k], HH)
            def gated_chunk(g, it):
                f0 = sum(GROUPS[:g])
                for s in range(2):
                    n = it * 2 + (N_UP[g] + s)
                    evac_wait(n)
                    if s == 0:
                        act.wait_ge(post_done, n)
                    act.activation(EV[s][:, :], acc[:, s, :], ACT.Copy).then_inc(act_step, 1)
                    f = it + (f0 + FC * s)
                    act.activation(CV[s][:, :], acc[:, s, :], ACT.Identity, bias=vec("conv_b", f), scale=vec("conv_w", f + 44)
                                   ).then_inc(acc_read, 1)
                act.wait_ge(gated, it * 3 + (3 * f0 + 1))
                act.activation(EV[0][:, :], CV[0][:, :], ACT.Silu).then_inc(silu_done, 1)
                act.wait_ge(gated, it * 3 + (3 * f0 + 3))
                act.activation(GH[:, block_of(it), :], CV[0][:, :], ACT.Copy).then_inc(gh_ready, 1)

            for g, gk in enumerate(GROUPS):
                if g == 2:
                    act.wait_ge(cx_in, 16)
                    act.activation(SQC[:, :, :], CX[:, :, :], ACT.Square).then_inc(csq_ready, 1)
                gated_chunk(g, 0)
                if g == 2:
                    act.wait_ge(cstat_done, 1)
                    act.activation(SD2[:, :], bank6[:, 16:18], ACT.Sqrt, bias=eps, scale=1.0 / D).then_inc(csd_ready, 1)
                with act.Fori(1, gk) as it:
                    gated_chunk(g, it)
                if g == 2:
                    act.wait_ge(cxn_ready, 1)
                    for k in range(KD):
                        act.activation(CX[:, k, :], CX[:, k, :], ACT.Identity, bias=MOD2[:, k, 1:2], scale=A3[:, k, 1:2]
                                       ).then_inc(ch_ready, 1)
                    act.wait_ge(ch_ready, KD)
                    act.activation(HCH[:, :, :], CX[:, :, :], ACT.Copy).then_inc(hch_ready, 1)
                residual_tiles(2, N_DOWN[g], lambda k: MOD1[:, bass.ds(k + 40, 1)], g == 2)

            root(2)
            modulate(2, lambda k: A3[:, k, 0:1], lambda k: MOD2[:, k, 0:1], HH)
            def b_in(j):
                return vec("b_in_2", j)

            with act.Fori(0, 4) as it:
                n, u0 = it * 4 + N_ATT2, it * 16
                act.wait_ge(acc_done, n + 1)
                steps.did(act.activation(K2[:, 0:T], acc[:, 0, :], ACT.Identity, bias=b_in(it + 28)))
                act.activation(K2[:, T:], bank7[:, 0:CTX], ACT.Identity, bias=b_in(it + 28)).then_inc(acc_read, 1)
                act.wait_ge(acc_done, n + 2)
                v = acc[:, 1, :].rearrange("p (r c) -> p r c", c=GRID)
                for b in range(NB):
                    dst = VT2[:, HALF * b:HALF * b + HALF].rearrange("p (r c) -> p r c", c=KW)
                    act.activation(dst, v[:, :, KCS[b]:KCS[b] + KW], ACT.Identity, bias=b_in(it + 32))
                act.activation(VT2[:, NB * HALF:], bank6[:, 0:CTX], ACT.Identity, bias=b_in(it + 32)).then_inc(acc_read, 1)
                act.wait_ge(acc_done, n + 3)
                for half in range(2):
                    src = acc[:, 0, HALF * half:HALF * half + HALF].rearrange("p (r n c) -> p n r c", n=NB, c=QW)
                    dst = Q2[:, HALF * half:HALF * half + HALF].rearrange("p (n r c) -> p n r c", n=NB, c=QW)
                    ins = act.activation(dst, src, ACT.Identity, bias=BQ8[:, bass.ds(it, 1)], scale=SCALE)
                ins.then_inc(acc_read, 1)

                def values_by_key(b, c0, c1):
                    act.wait_ge(vt2_done, it * 3 + (b + 1))
                    act.activation(VTOK2[:, c0:c1, :], turn[:, 0:P * (c1 - c0)].rearrange("p (c d) -> p c d", d=P), ACT.Copy
                                   ).then_inc(vtok2_ready, 1)

                act.wait_ge(x_saved, 16)
                values_by_key(0, 0, 8)
                act.wait_ge(acc_done, n + 4)
                act.activation(SZ[:, :], acc[:, 1, :], ACT.Silu, bias=b_in(it + 36)).then_inc(acc_read, 1)
                values_by_key(1, 8, 16)
                values_by_key(2, 16, 18)

                def turned(u):
                    act.wait_ge(pt2_done, u0 + (u + 1))
                    if u >= 2:
                        act.wait_ge(pv2_done, u0 + (u - 1))
                    act.activation(PT2[u % 2][:, :], turn[:, 0:NKEY], ACT.Copy).then_inc(pt2_ready, 1)

                def exponents(u):
                    act.wait_ge(nb2_ready, u0 + (u + 1))
                    act.activation(EX2[u % 4][:, :], acc[:, u % 2, P:P + NKEY], ACT.Exp, bias=NBI[:, u % 2:u % 2 + 1],
                                   accum_out=SUM[:, u % 2:u % 2 + 1]).then_inc(exp2_done, 1)

                exponents(0)
                exponents(1)
                for u in range(16):
                    if u < 14:
                        exponents(u + 2)
                    turned(u)
                act.wait_ge(pv2_done, u0 + 16)

            act.wait_ge(o2_ready, 64)
            act.activation(CBH[:, :, :], CBF[:, :, :], ACT.Copy).then_inc(cbh_ready, 1)

            def channels(it):
                act.wait_ge(chan_done, it + 1)
                act.activation(VW[:, :, :], turn[:, :].rearrange("p (c d) -> p c d", d=P), ACT.Copy).then_inc(vw_ready, 1)
                act.activation(VROW[0:1, :], bank6[0:1, 0:P], ACT.Copy)
                act.activation(ALT[:, 3:4], bank6[:, P:P + 1], ACT.Copy).then_inc(vw_ready, 1)

            def tokens(it):
                act.wait_ge(seq_done, it + 1)
                act.activation(SB[:, :], bank6[:, :], ACT.Copy).then_inc(sb_ready, 1)
                act.wait_ge(y_ready, it * 2 + 3)
                act.activation(BRH[:, block_of(it), :], CV[1][:, :], ACT.Copy).then_inc(brh_ready, 1)

            def project(it):
                n = it * 2 + N_F
                act.wait_ge(acc_done, n + 1)
                act.wait_ge(fold_ready, it) if not isinstance(it, int) else act.wait_ge(post_done, N_F)
                act.activation(EV[0][:, :], acc[:, 0, :], ACT.Identity, bias=b_in(it + 16)).then_inc(acc_read, 1)
                if not isinstance(it, int):
                    tokens(it - 1)
                evac_wait(n + 1)
                act.activation(EV[1][:, :], acc[:, 1, :], ACT.Silu, bias=b_in(it + 20)).then_inc(acc_read, 1)
                channels(it)

            project(0)
            with act.Fori(1, 4) as it:
                project(it)
            tokens(3)

            def gates(n0, b0, last=False):
                with act.Fori(0, KD) as it:
                    n = it * 2 + n0
                    evac_wait(n)
                    act.activation(EV[0][:, :], acc[:, 0, :], ACT.Sigmoid, bias=b_in(it + b0)).then_inc(acc_read, 1)
                    evac_wait(n + 1)
                    act.activation(EV[1][:, :], acc[:, 1, :], ACT.Copy).then_inc(acc_read, 1)
                    if last:
                        act.wait_ge(sums_ready, it + 1)
                        act.activation(SH[:, bass.ds(it, 1), :], S[:, bass.ds(it, 1), :], ACT.Copy).then_inc(sh_ready, 1)

            gates(N_GF, 56 - 8)
            gates(N_GC, 56)
            with act.Fori(0, 4) as it:
                n = it * 4 + N_A
                for j, (s, b0, fn) in enumerate(((0, 0, ACT.Identity), (1, 8, ACT.Identity), (0, 4, ACT.Identity),
                                                 (1, 12, ACT.Silu))):
                    evac_wait(n + j)
                    act.activation(EV[s][:, :], acc[:, s, :], fn, bias=b_in(it + b0)).then_inc(acc_read, 1)
                act.wait_ge(y_ready, it + 10)
                act.activation(BRH[:, bass.ds(it, 1), :], CV[0][:, :], ACT.Copy).then_inc(brh_ready, 1)
            gates(N_GA, 40, last=True)

            residual_tiles(3, N_OUT2, lambda k: MOD2[:, bass.ds(k + 16, 1), 0], True, XT2)
            root(3)

        @block.vector
        def _(dve):
            steps = Steps(dve, dve_step)

            def link(ins):
                steps.did(ins)
                steps.settle()

            def invert(q, nt=TT):
                dve.wait_ge(sd_ready, q + 1)
                dve.reciprocal(RS[:, 0:nt], SD[:, 0:nt]).then_inc(rs_ready, 1)

            def normed(q, src, hh, hl, w=T):
                dve.wait_ge(rb_done, q + 1)

                def second(k):
                    dve.wait_ge(hh_ready, q * KD + k + 1)
                    dve.tensor_tensor(hl[:, k, :], CV[k % 2][:, 0:w], hh[:, k, :].bitcast(F32), ALU.subtract
                                      ).then_inc(hl_ready, 1)

                for k in range(KD):
                    if k >= 2:
                        dve.wait_ge(hf_ready, q * KD + k - 1)
                    dve.tensor_tensor(EV[k % 2][:, 0:w], src(k), turn[:, 0:w], ALU.mult).then_inc(xn_ready, 1)
                    if k > 0:
                        second(k - 1)
                second(KD - 1)

            def modulation(w, cond, out):
                ins = dve.scalar_tensor_tensor(out=w, in0=w, scalar=1.0, in1=cond[:, :], op0=ALU.mult, op1=ALU.mult, accum_out=out)
                ins.then_inc(ada_used, 1)

            dve.wait_ge(cond_ready, 1)
            for j in range(4):
                dve.wait_ge(ada1_in[j], 16)
                for b in range(4):
                    modulation(ADA1[j][:, b, :], C1A, MOD1[:, 4 * j + b:4 * j + b + 1])
                if j == 1:
                    invert(0)
            link(dve.tensor_copy(MX[:, 6:7], eps))
            link(dve.tensor_tensor(MOD1[:, 0:16], MOD1[:, 0:16], vec("b_ada", 0, 16), ALU.add))
            dve.scalar_tensor_tensor(out=A1[:, :], in0=MOD1[:, 8:16], scalar=1.0, in1=vec("norm1_g", 0, KD), op0=ALU.add,
                                     op1=ALU.mult).then_inc(mods_ready, 1)
            normed(0, lambda k: XT[:, k, :], HH, HL)
            dve.wait_ge(rope_in, 32)
            for b in (UP, *WINS):
                steps.did(dve.memset(b[:, 0:PAD], 0.0))
                steps.did(dve.memset(b[:, PAD + T:], 0.0))
            steps.settle()

            def rope(n, m):
                dst = KN[:, :] if m == 0 else QN[:, m - 1, :]
                e = EV[n % 2]
                steps.settle()
                if n > 0:
                    dve.wait_ge(post_done, n)
                if m == 0:
                    dve.wait_ge(ksd_ready, 1)
                    link(dve.reciprocal(CV[1][:, :], CV[1][:, :]))
                dve.wait_ge(acc_read, n + 1)
                steps.did(dve.tensor_tensor(ROPE1[:, :], e[:, :], COS[:, :], ALU.mult))
                dve.wait_ge(rot_done, m + 1)
                link(dve.tensor_tensor(ROPE2[:, :], turn[:, :], SIN[:, :], ALU.mult))
                if m == 0:
                    link(dve.tensor_tensor(ROPE1[:, :], ROPE1[:, :], ROPE2[:, :], ALU.add))
                    dve.tensor_tensor(dst, ROPE1[:, :], CV[1][:, :], ALU.mult).then_inc(post_done, 1)
                else:
                    dve.tensor_tensor(dst, ROPE1[:, :], ROPE2[:, :], ALU.add).then_inc(post_done, 1)

            def windows(n, g):
                dve.wait_ge(acc_read, n + 1)
                if g > 0:
                    dve.wait_ge(plh_ready, g)
                    dve.wait_ge(pll_ready, g)
                dve.tensor_copy(UP[:, PAD:PAD + T], EV[n % 2][:, :]).then_inc(post_done, 1)
                dve.wait_ge(post_done, n + 1)
                w, half = POOL_W[g], POOL_W[g] // 2
                src, r = UP, 0
                link(dve.tensor_tensor(WINS[0][:, 1:T + 2 * PAD], UP[:, 1:T + 2 * PAD], UP[:, 0:T + 2 * PAD - 1], ALU.add))
                h = 1
                while 2 * h < w:
                    a, b = WINS[r], WINS[1 - r]
                    lo, hi = 2 * h, T + 2 * PAD - 2 * h + 1
                    link(dve.tensor_tensor(b[:, lo:hi], a[:, lo + h:hi + h], a[:, lo - h:hi - h], ALU.add))
                    r, h = 1 - r, 2 * h
                win = WINS[r]
                edge = con("edge", 16, 16 * g)
                steps.did(dve.tensor_tensor(win[:, PAD:PAD + 8], win[:, PAD:PAD + 8], edge[:, 0:8], ALU.mult))
                link(dve.tensor_tensor(win[:, PAD + T - 8:PAD + T], win[:, PAD + T - 8:PAD + T], edge[:, 8:16], ALU.mult))
                dve.scalar_tensor_tensor(out=UP[:, PAD:PAD + T], in0=win[:, PAD:PAD + T], scalar=1.0 / w, in1=UP[:, PAD:PAD + T],
                                         op0=ALU.mult, op1=ALU.subtract).then_inc(pooled, 1)
                dve.wait_ge(plh_ready, g + 1)
                dve.tensor_tensor(PLL[:, :], UP[:, PAD:PAD + T], PLH[:, :].bitcast(F32), ALU.subtract).then_inc(pll_ready, 1)
                dve.wait_ge(pll_ready, g + 1)

            def mix_second(n, g):
                dve.wait_ge(mixh_ready, g + 1)
                dve.tensor_tensor(ML[:, 4 + g, :], EV[n % 2][:, :], MH[:, 4 + g, :].bitcast(F32), ALU.subtract
                                  ).then_inc(post_done, 1)

            def modulation2(t):
                w = ADA2[t // 2 % 2][:, t % 2, :]
                dve.wait_ge(ada2_in[t // 2 % 2], 16 * (t // 4 + 1))
                if t < 16:
                    dve.wait_ge(cond_ready, 3)
                    link(dve.scalar_tensor_tensor(out=ROPE1[:, :], in0=w, scalar=1.0, in1=C2B[1][:, :], op0=ALU.mult, op1=ALU.mult,
                                                  accum_out=MOD2[:, t, 1:2]))
                modulation(w, C2B[0], MOD2[:, t, 0:1])

            for n in range(N_OUT1):
                if n < 8:
                    if n > 0:
                        dve.wait_ge(post_done, n)
                    for t in range(3 * n, 3 * n + 3):
                        modulation2(t)
                if n == 1:
                    dve.wait_ge(acc_read, 2)
                    dve.tensor_copy(VN[:, :], EV[1][:, :]).then_inc(post_done, 1)
                elif n in POOLS:
                    windows(n, POOLS[n])
                elif n in MIXES:
                    mix_second(n, MIXES[n])
                else:
                    rope(n, [0, None, 1, 2, 3, 4][n])
            dve.wait_ge(qsd_ready, 1)
            link(dve.reciprocal(QSD[:, :, :], QSD[:, :, :]))
            steps.did(dve.tensor_scalar(RSP[:, :, :], QSD[:, :, :], SCALE, None, ALU.mult))
            steps.did(dve.tensor_scalar(RSN[:, :, :], QSD[:, :, :], -SCALE, None, ALU.mult))
            dve.wait_ge(khi_ready, 1)
            dve.tensor_tensor(KLO[:, :], KN[:, :], KHI[:, :].bitcast(F32), ALU.subtract).then_inc(klo_ready, 1)
            dve.wait_ge(klo_ready, 1)
            for kv in range(NKV):
                for b in range(2):
                    dve.tensor_copy(KSL[64 * b:64 * b + 64, kv, :], KLO[64 * kv:64 * kv + 64, :]).then_inc(kst_dve, 1)
            dve.wait_ge(vh_ready, 1)
            vt = turn[:, :].rearrange("p (a d) -> p a d", d=HD)
            vdst = VTOK[:, :, :, :].rearrange("p t v d -> p (t v) d")
            dve.tensor_tensor(vdst[:, :, HD:P], vt, vdst[:, :, 0:HD].bitcast(F32), ALU.subtract).then_inc(vl_ready, 1)
            dve.wait_ge(vl_ready, 1)
            dve.wait_ge(kst_dve, 4)
            dve.wait_ge(kst_act, 4)

            dve.tensor_copy(MX[:, 7:8], eps).then_inc(ptl_ready, 2)
            dve.tensor_copy(MX[:, 6:7], eps).then_inc(o_ready, 1)

            def stack_queries(it, s):
                dve.wait_ge(qh_ready, it * 2 + (s + 1))
                link(dve.tensor_tensor(QL[:, :, :], QN[:, :, span(it * 256 + 128 * s)], QH[:, :, :].bitcast(F32), ALU.subtract))
                for b in range(2):
                    dst = QST[s % 2][64:128, :, :].rearrange("p (i j) q -> p i j q", j=2)[:, :, b, :]
                    dve.tensor_copy(dst, QL[64 * b:64 * b + 64, :, :]).then_inc(qst_dve, 1)
                dve.wait_ge(qst_dve, it * 4 + (2 * s + 2))

            def largest(it, u):
                j = u % 2
                dve.wait_ge(scores_done, it * 16 + (u + 1))
                link(dve.tensor_reduce(MX[:, j:j + 1], acc[:, j, :], AX.X, ALU.max))
                dve.tensor_tensor(NBI[:, j:j + 1], MX[:, j:j + 1], column(RSN, it * 16 + u), ALU.mult).then_inc(nb_ready, 1)

            def diagonal(it, u):
                j = u % 2
                dve.wait_ge(exp_done, it * 16 + (u + 1))
                dve.reciprocal(RC[:, j:j + 1], SUM[:, j:j + 1]).then_inc(rc_ready, 1)
                dve.wait_ge(rc_ready, it * 16 + (u + 1))
                dve.tensor_scalar(DG[j][:, :], ident, RC[:, j:j + 1], None, ALU.mult).then_inc(dga_ready, 1)

            def gather_o(it, b):
                dve.wait_ge(otmp_ready, it * 4 + (b + 1))
                g = b % 2
                o = bank6[0:64, :].rearrange("p (i j q) -> p i j q", j=2, q=P)
                m = OTMP[0:64, :].rearrange("p (i j q) -> p i j q", j=2, q=P)
                link(dve.tensor_tensor(OT[0:64, 2 * g:2 * g + 2, :], o[:, :, 0, :], m[:, :, 0, :], ALU.add))
                dve.tensor_tensor(OT[64:128, 2 * g:2 * g + 2, :], o[:, :, 1, :], m[:, :, 1, :], ALU.add).then_inc(o_ready, 1)
                if g == 1:
                    dve.wait_ge(mh_ready, it * 2 + (b // 2 + 1))
                    sl = span(it * 256 + 128 * (b // 2))
                    dve.tensor_tensor(ML[:, 0:4, sl], OT[:, :, :], MH[:, 0:4, sl].bitcast(F32), ALU.subtract).then_inc(ml_ready, 1)
                    dve.wait_ge(ml_ready, it * 2 + (b // 2 + 1))

            def attend(it, last):
                for u in range(16):
                    if u < 14 or not last:
                        largest(it, u + 2)
                    if u < 15 or not last:
                        diagonal(it, u + 1)
                    for h in range(2):
                        dve.wait_ge(pth_ready, it * 32 + (2 * u + h + 1))
                        dve.tensor_tensor(PTL[:, 4 * h:4 * h + 4, u % 4, :],
                                          turn[:, HALF * h:HALF * h + HALF].rearrange("p (k q) -> p k q", q=P),
                                          PTH[:, 4 * h:4 * h + 4, u % 4, :].bitcast(F32), ALU.subtract).then_inc(ptl_ready, 1)
                    if u % 4 == 0 and u > 0:
                        gather_o(it, u // 4 - 1)
                    if u == 1:
                        stack_queries(it, 1)
                    if u == 9 and not last:
                        stack_queries(it, 2)
                    if u % 2 == 1:
                        j = u // 2
                        dve.wait_ge(ada3_in[j % 2], it * 64 + 16 * (j // 2 + 1))
                        modulation(ADA3[j % 2][:, :], C1B, MOD1[:, block_of(it * 8 + (16 + j))])
                gather_o(it, 3)

            dve.wait_ge(cond_ready, 4)
            stack_queries(0, 0)
            largest(0, 0)
            largest(0, 1)
            diagonal(0, 0)
            with steps.loop(3, 22) as it:
                attend(it, False)
            attend(3, True)
            link(dve.tensor_copy(MX[:, 6:7], eps))
            link(dve.tensor_tensor(MOD1[:, 16:48], MOD1[:, 16:48], vec("b_ada", 16, 32), ALU.add))
            link(dve.tensor_tensor(MOD2[:, :, 0], MOD2[:, :, 0], vec("b_ada_2", 0, 24), ALU.add))
            link(dve.tensor_tensor(MOD2[:, 0:16, 1], MOD2[:, 0:16, 1], vec("b_ada_2", 0, 16), ALU.add))
            link(dve.scalar_tensor_tensor(out=A2[:, :], in0=MOD1[:, 32:40], scalar=1.0, in1=vec("norm2_g", 0, KD), op0=ALU.add,
                                          op1=ALU.mult))
            for v in range(2):
                link(dve.scalar_tensor_tensor(out=A3[:, :, v], in0=MOD2[:, 8:16, v], scalar=1.0, in1=vec("norm_g_2", 0, KD),
                                              op0=ALU.add, op1=ALU.mult))
            link(dve.tensor_scalar(BQ8[:, 0:4], vec("b_in_2", 24, 4), SCALE, None, ALU.mult))
            dve.tensor_copy(MX[:, 6:7], eps).then_inc(mods_ready, 1)

            def residual_tiles(n0, arrivals=None, stream=XT):
                def pair(it):
                    for s in range(2):
                        if arrivals:
                            dve.wait_ge(arrivals[2 * it + s], 16)
                        dve.wait_ge(acc_read, it * 2 + (n0 + s + 1))
                        x = stream[:, 2 * it + s, :] if isinstance(it, int) else stream[:, bass.ds(it * 2 + s, 1), :]
                        dve.tensor_tensor(x, x, EV[s][:, :], ALU.add).then_inc(post_done, 1)
                if arrivals:
                    for it in range(4):
                        pair(it)
                else:
                    with dve.Fori(0, 4) as it:
                        pair(it)

            residual_tiles(N_OUT1, x_again)
            invert(1)
            normed(1, lambda k: XT[:, k, :], HH, HL)

            def shifted(s, f):
                link(dve.scalar_tensor_tensor(out=CV[s][:, 1:T], in0=EV[s][:, 0:T - 1], scalar=vec("conv_w", f), in1=CV[s][:, 1:T],
                                              op0=ALU.mult, op1=ALU.add))
                return dve.scalar_tensor_tensor(out=CV[s][:, 0:T - 1], in0=EV[s][:, 1:T], scalar=vec("conv_w", f + 88),
                                                in1=CV[s][:, 0:T - 1], op0=ALU.mult, op1=ALU.add)

            def gated_chunk(g, it):
                f0 = sum(GROUPS[:g])
                n = it * 2 + N_UP[g]
                dve.wait_ge(acc_read, n + 1)
                shifted(0, it + f0).then_inc(gated, 1)
                dve.wait_ge(acc_read, n + 2)
                shifted(1, it + (f0 + FC)).then_inc(gated, 1)
                dve.wait_ge(silu_done, it + (f0 + 1))
                dve.wait_ge(gated, it * 3 + (3 * f0 + 2))
                dve.tensor_tensor(CV[0][:, :], EV[0][:, :], CV[1][:, :], ALU.mult).then_inc(gated, 1)
                dve.wait_ge(gh_ready, it + (f0 + 1))
                dve.tensor_tensor(GL[:, block_of(it), :], CV[0][:, :], GH[:, block_of(it), :].bitcast(F32), ALU.subtract
                                  ).then_inc(post_done, 2)
                dve.wait_ge(post_done, n + 2)

            for g, gk in enumerate(GROUPS):
                gated_chunk(g, 0)
                if g == 2:
                    dve.wait_ge(csd_ready, 1)
                    dve.reciprocal(RC2[:, :], SD2[:, :]).then_inc(crs_ready, 1)
                with steps.loop(gk - 1, 2) as it:
                    gated_chunk(g, it + 1)
                if g == 2:
                    dve.wait_ge(crb_done, 1)
                    dve.tensor_tensor(CX[:, :, :], CX[:, :, :], turn[:, 0:CTX].unsqueeze(1).to_broadcast([P, KD, CTX]), ALU.mult
                                      ).then_inc(cxn_ready, 1)
                    dve.wait_ge(hch_ready, 1)
                    dve.tensor_tensor(HCL[:, :, :], CX[:, :, :], HCH[:, :, :].bitcast(F32), ALU.subtract).then_inc(hcl_ready, 1)
                residual_tiles(N_DOWN[g])

            invert(2)
            normed(2, lambda k: XT[:, k, :], HH, HL)

            with steps.loop(4, 32) as it:
                n, u0 = it * 4 + N_ATT2, it * 16

                def largest(u):
                    j, half, c, a = u // 8, u // 4 % 2, u % NB, acc[:, u % 2, :]
                    if u % 8 == 0:
                        dve.wait_ge(bias_in[j], it * 16 + 16)
                    dve.wait_ge(scores2_done, u0 + (u + 1))
                    link(dve.tensor_tensor(a[:, P:P + NLOC], a[:, P:P + NLOC], BIAS[j][:, 3 * half + KIND[c], :], ALU.add))
                    link(dve.tensor_reduce(MX[:, u % 2:u % 2 + 1], a[:, P:P + NKEY], AX.X, ALU.max))
                    dve.tensor_scalar(NBI[:, u % 2:u % 2 + 1], MX[:, u % 2:u % 2 + 1], -1.0, None, ALU.mult).then_inc(nb2_ready, 1)

                def diagonal(u):
                    dve.wait_ge(exp2_done, u0 + (u + 1))
                    dve.reciprocal(RC[:, u % 2:u % 2 + 1], SUM[:, u % 2:u % 2 + 1]).then_inc(rc_ready, 1)
                    dve.wait_ge(rc_ready, u0 + (64 + u + 1))
                    dve.tensor_scalar(DG[u % 2][:, :], ident, RC[:, u % 2:u % 2 + 1], None, ALU.mult).then_inc(dg_ready, 1)

                def gather(u):
                    j, half, c = u // 8, u // 4 % 2, u % NB
                    if u == 0:
                        dve.wait_ge(acc_read, n + 4)
                    dve.wait_ge(pv2_done, u0 + (u + 1))
                    rows = slice(HD * j, HD * j + HD)

                    def grid(x):
                        return x[rows, HALF * half:HALF * half + HALF].rearrange("p (r c) -> p r c", c=GRID)[:, :, QW * c:QW * c + QW]

                    branch = CBF[rows, bass.ds(it, 1), :].rearrange("p a t -> p (a t)")
                    dve.tensor_tensor(branch[:, HALF * half:HALF * half + HALF].rearrange("p (r c) -> p r c", c=GRID)
                                      [:, :, QW * c:QW * c + QW],
                                      (bank6, bank7)[u % 2][rows, 0:P].rearrange("p (r c) -> p r c", c=QW), grid(SZ), ALU.mult
                                      ).then_inc(o2_ready, 1)

                largest(0)
                largest(1)
                for u in range(16):
                    diagonal(u)
                    if u < 14:
                        largest(u + 2)
                    if u > 0:
                        gather(u - 1)
                gather(15)
                dve.wait_ge(o2_ready, u0 + 16)
                dve.tensor_copy(MX[:, 6:7], eps).then_inc(post_done, 4)
                dve.wait_ge(post_done, n + 4)
            dve.wait_ge(cbh_ready, 1)
            dve.tensor_tensor(CBL[:, :, :], CBF[:, :, :], CBH[:, :, :].bitcast(F32), ALU.subtract).then_inc(cbl_ready, 1)

            dve.wait_ge(dft_in, 16)
            dve.tensor_copy(FO[:, 0:1], zero).then_inc(y_ready, 1)
            def fold(it):
                n, u = it * 2 + N_F, EV[0]
                dve.wait_ge(acc_read, n + 1)
                steps.did(dve.tensor_tensor(FE[:, 1:HALF], u[:, 1:HALF], u[:, T - 1:HALF:-1], ALU.add))
                steps.did(dve.tensor_tensor(FO[:, 1:HALF], u[:, 1:HALF], u[:, T - 1:HALF:-1], ALU.subtract))
                steps.did(dve.tensor_copy(FE[:, 0:HALF + 1:HALF], u[:, 0:HALF + 1:HALF]))
                pairs = u[:, :].rearrange("p (t a) -> p a t", a=2)
                link(dve.tensor_reduce(ALT[:, 0:2], pairs, AX.X, ALU.add))
                dve.tensor_tensor(ALT[:, 2:3], ALT[:, 0:1], ALT[:, 1:2], ALU.subtract).then_inc(fold_ready, 1)

            def unfold(it):
                dve.wait_ge(sb_ready, it + 1)
                y = CV[0]
                dve.tensor_tensor(y[:, 0:HALF], bank7[:, :], SB[:, :], ALU.subtract)
                dve.tensor_tensor(y[:, HALF + 1:T], bank7[:, HALF - 1:0:-1], SB[:, HALF - 1:0:-1], ALU.add).then_inc(y_ready, 1)
                steps.did(dve.tensor_copy(y[:, HALF:HALF + 1], ALT[:, 3:4]))
                dve.wait_ge(y_ready, it * 2 + 2)
                steps.settle()
                dve.wait_ge(acc_read, it * 2 + (N_F + 2))
                dve.tensor_tensor(CV[1][:, :], y[:, :], EV[1][:, :], ALU.mult).then_inc(y_ready, 1)
                dve.wait_ge(brh_ready, it + 1)
                dve.tensor_tensor(BRL[:, block_of(it), :], CV[1][:, :], BRH[:, block_of(it), :].bitcast(F32), ALU.subtract
                                  ).then_inc(post_done, 2)
                dve.wait_ge(post_done, it * 2 + (N_F + 2))

            fold(0)
            with steps.loop(3, 5) as it:
                fold(it + 1)
                unfold(it)
            unfold(3)

            with dve.Fori(0, KD) as it:
                dve.wait_ge(acc_read, it * 2 + (N_GF + 2))
                dve.tensor_tensor(S[:, bass.ds(it, 1), :], EV[0][:, :], EV[1][:, :], ALU.mult).then_inc(post_done, 2)

            def gates(n0, last=False):
                with steps.loop(KD, 1) as it:
                    s = S[:, bass.ds(it, 1), :]
                    dve.wait_ge(acc_read, it * 2 + (n0 + 2))
                    link(dve.tensor_tensor(CV[0][:, :], EV[0][:, :], EV[1][:, :], ALU.mult))
                    if last:
                        dve.tensor_tensor(s, s, CV[0][:, :], ALU.add).then_inc(sums_ready, 1)
                        dve.wait_ge(sh_ready, it + 1)
                        dve.tensor_tensor(SL[:, bass.ds(it, 1), :], s, SH[:, bass.ds(it, 1), :].bitcast(F32), ALU.subtract
                                          ).then_inc(post_done, 2)
                    else:
                        dve.tensor_tensor(s, s, CV[0][:, :], ALU.add).then_inc(post_done, 2)
                    dve.wait_ge(post_done, it * 2 + (n0 + 2))

            dve.wait_ge(post_done, N_GC)
            gates(N_GC)
            with steps.loop(4, 5) as it:
                n = it * 4 + N_A
                dve.wait_ge(acc_read, n + 2)
                dve.tensor_tensor(CV[1][:, :], EV[0][:, :], EV[1][:, :], ALU.mult).then_inc(post_done, 2)
                dve.wait_ge(post_done, n + 2)

                def tap(i):
                    return vec("w_conv_2", it + 4 * i)

                link(dve.tensor_scalar(CV[0][:, :], CV[1][:, :], tap(1), vec("b_conv_2", it), ALU.mult, ALU.add))
                link(dve.scalar_tensor_tensor(out=CV[0][:, 1:T], in0=CV[1][:, 0:T - 1], scalar=tap(0), in1=CV[0][:, 1:T],
                                              op0=ALU.mult, op1=ALU.add))
                link(dve.scalar_tensor_tensor(out=CV[0][:, 0:T - 1], in0=CV[1][:, 1:T], scalar=tap(2), in1=CV[0][:, 0:T - 1],
                                              op0=ALU.mult, op1=ALU.add))
                dve.wait_ge(acc_read, n + 3)
                link(dve.tensor_tensor(CV[0][:, :], CV[0][:, :], EV[0][:, :], ALU.mult))
                dve.tensor_copy(MX[:, 6:7], eps).then_inc(post_done, 1)
                dve.wait_ge(acc_read, n + 4)
                dve.tensor_tensor(CV[0][:, :], CV[0][:, :], EV[1][:, :], ALU.mult).then_inc(y_ready, 1)
                dve.wait_ge(brh_ready, it + 5)
                steps.did(dve.tensor_tensor(BRL[:, bass.ds(it, 1), :], CV[0][:, :], BRH[:, bass.ds(it, 1), :].bitcast(F32),
                                            ALU.subtract))
                steps.settle()
                dve.tensor_copy(MX[:, 6:7], eps).then_inc(post_done, 1)
                dve.wait_ge(post_done, n + 4)
            gates(N_GA, last=True)

            dve.wait_ge(x_back, 16)
            residual_tiles(N_OUT2, stream=XT2)
            invert(3)
            dve.wait_ge(rb_done, 4)
            for k in range(KD):
                dve.scalar_tensor_tensor(out=XT2[:, k, :], in0=XT2[:, k, :], scalar=vec("final_g_2", k), in1=turn[:, :],
                                         op0=ALU.mult, op1=ALU.mult).then_inc(out_ready, 1)


def tiles_of(w):
    i, o = w.shape
    return np.ascontiguousarray(w.reshape(i // P, P, o // P, P).transpose(2, 1, 0, 3)).reshape(o // P, P, -1)


def cols_of(v):
    return np.asarray(v).reshape(-1, P).T


def layout(x):
    f = {k: np.asarray(v) for k, v in x.items()}
    vec = {
        "b_ada": cols_of(f["b_ada"]), "norm1_g": cols_of(f["norm1_g"]), "pool_scale": cols_of(f["pool_scale"]),
        "norm2_g": cols_of(f["norm2_g"]), "conv_w": cols_of(f["conv_w"]), "conv_b": cols_of(f["conv_b"]),
        "b_ada_2": cols_of(f["b_ada_2"]), "norm_g_2": cols_of(f["norm_g_2"]), "b_in_2": cols_of(f["b_in_2"]),
        "w_conv_2": cols_of(f["w_conv_2"]), "b_conv_2": cols_of(f["b_conv_2"]), "final_g_2": cols_of(f["final_g_2"]),
        "q_norm_g": np.concatenate([f["q_norm_g"][0]] * 2)[:, None],
        "k_norm_g": np.concatenate([f["k_norm_g"][0]] * 2)[:, None],
    }
    w_in, w_up, w_down = (f[k][0] for k in ("w_in", "w_up", "w_down"))
    tin, tup = tiles_of(w_in), tiles_of(w_up)
    stream = [tin[4:5], tin[5:6], tin[0:4], tin[6:10], tiles_of(f["w_out"][0])]
    w6, f0 = None, 0
    for gk in GROUPS:
        stream.append(np.stack([tup[f0:f0 + gk], tup[FC + f0:FC + f0 + gk]], axis=1).reshape(2 * gk, P, -1))
        down = tiles_of(w_down[f0 * P:(f0 + gk) * P])
        if gk == KD:
            stream.append(down)
        else:
            w6 = down
        f0 += gk
    w2 = tiles_of(f["w_in_2"][0])
    col = {name: o // P for name, o in (("a_x", 0), ("a_b", 512), ("a_c", 1024), ("a_z", 1536), ("f_u", 2048), ("f_z", 2560),
                                        ("q", 3072), ("k", 3584), ("v", 4096), ("c_z", 4608), ("g_a", 5120), ("g_f", 6144),
                                        ("g_c", 7168))}

    def in_turn(names, count):
        return w2[[col[name] + i for i in range(count) for name in names]]

    stream += [in_turn(("k", "v", "q", "c_z"), 4), in_turn(("f_u", "f_z"), 4), in_turn(("g_f",), 8), in_turn(("g_c",), 8),
               in_turn(("a_x", "a_c", "a_b", "a_z"), 4), in_turn(("g_a",), 8), tiles_of(f["w_out_2"][0])]
    w4 = np.concatenate([tiles_of(f[name][0]) for name in ("w_br_f_2", "w_br_c_2", "w_br_a_2")])
    ada = np.ascontiguousarray(np.concatenate([f["w_ada"][0].T, f["w_ada_2"][0].T])).reshape(72, P, D)
    conds = np.ascontiguousarray(np.stack([np.broadcast_to(f[k].reshape(1, D), (P, D)) for k in ("c", "c_2", "c_ctx_2")]))
    con = np.zeros((P, NCONST), np.float32)
    con[:, CCOL["ident"]:CCOL["ident"] + P] = np.eye(P)
    r = np.arange(P)
    con[:, CCOL["headmean"]:CCOL["headmean"] + P] = (r[:, None] // HD == r[None, :] // HD) / HD
    rot = np.zeros((P, P))
    for i in range(P):
        if i % 32 < 16:
            rot[i + 16, i] = -1.0
        else:
            rot[i - 16, i] = 1.0
    con[:, CCOL["rot"]:CCOL["rot"] + P] = rot
    con[:, CCOL["headsel"]:CCOL["headsel"] + 2] = r[:, None] // HD == np.arange(2)[None, :]
    con[:, CCOL["one"]] = 1.0
    con[:, CCOL["eps"]] = EPS
    for g, w in enumerate(POOL_W):
        t = np.r_[0:8, T - 8:T]
        count = np.minimum(t + w // 2 - 1, T - 1) - np.maximum(t - w // 2, 0) + 1
        con[:, CCOL["edge"] + 16 * g:CCOL["edge"] + 16 * g + 16] = w / count
    inv = (1.0 / (10000.0 ** (np.arange(0, 32, 2, dtype=np.float32) / 32))).astype(np.float32)
    pos = np.stack([np.repeat(np.arange(ROWS), GRID), np.tile(np.arange(GRID), ROWS)]).astype(np.float32)
    d = r % HD
    ang = pos[d // 32] * inv[d % 16][:, None]
    rope = np.stack([np.cos(ang), np.sin(ang)]).astype(np.float32)
    query, key = np.arange(P), np.arange(NLOC)
    bias = np.full((NQ, P, 6, NLOC), NEG, np.float32)
    for half in range(2):
        qr, kr = 8 * half + query // QW, 4 * half + key // KW
        r0 = np.clip(qr - KH // 2, 0, ROWS - KH)
        row_ok = (kr[None] >= r0[:, None]) & (kr[None] < r0[:, None] + KH)
        for kind, b in enumerate((0, 1, 3)):
            qc, kc = QW * b + query % QW, KCS[b] + key % KW
            c0 = np.clip(qc - QW // 2, 0, GRID - QW)
            ok = row_ok & (kc[None] >= c0[:, None]) & (kc[None] < c0[:, None] + QW)
            dr = np.clip(kr[None] - qr[:, None] + KH - 1, 0, 2 * KH - 2)
            dc = np.clip(kc[None] - qc[:, None] + QW - 1, 0, 2 * QW - 2)
            bias[:, :, 3 * half + kind] = np.where(ok[None], f["rpb_2"][0][:, dr, dc], np.float32(NEG))
    t = np.arange(HALF)
    ang_t = 2 * np.pi / T * (np.outer(t, t) % T)
    ang_c = 2 * np.pi / P * (np.outer(r, r) % P)
    rows = lambda m: m.reshape(4, P, HALF).transpose(1, 0, 2).reshape(P, -1)
    norm = 1.0 / math.sqrt(T * P)
    dft = np.concatenate([rows(np.cos(ang_t)), rows(np.sin(ang_t)), np.cos(ang_c) * norm, np.sin(ang_c) * norm,
                          np.tile(1.0 - 2.0 * (t % 2), (P, 1))], axis=1).astype(np.float32)
    return {
        "ctxT": np.ascontiguousarray(f["ctx_2"][0].T).reshape(KD, P, CTX), "bias": bias, "dft": dft, "w4": w4,
        "xT": np.ascontiguousarray(f["x"][0].T).reshape(KD, P, T),
        "vecs": np.ascontiguousarray(np.concatenate([vec[n] for n, _ in _VECS], axis=1)),
        "consts": con, "rope": rope,
        "w8": np.concatenate(stream), "w6": w6, "w1": np.ascontiguousarray(f["w_pool"][0]),
        "ada": ada, "conds": conds,
    }


def kernel(**inputs):
    import concourse.bacc as bacc
    from concourse.bass_utils import run_bass_kernel_spmd as run

    nc = bacc.Bacc("TRN2", target_bir_lowering=False, num_devices=1)
    arrays = layout(inputs)
    aps = {name: nc.dram_tensor(f"in_{name}", a.shape, mybir.dt.from_np(a.dtype), kind="ExternalInput").ap()
           for name, a in arrays.items()}
    out = nc.dram_tensor("out_xT", (KD, P, T), F32, kind="ExternalOutput").ap()
    build(nc, aps, out)
    r = run(nc, [{f"in_{name}": a for name, a in arrays.items()}], core_ids=[0])
    return np.ascontiguousarray(r.results[0]["out_xT"].reshape(D, T).T).reshape(1, T, D)
```

```python
import math
from contextlib import ExitStack, contextmanager

import numpy as np

import concourse.bass as bass
from concourse import mybir

F32 = mybir.dt.float32
F32R = mybir.dt.float32r
ACT = mybir.ActivationFunctionType
ALU = mybir.AluOpType
AX = mybir.AxisListType

P = 128
D = 1024
T = 1024
KD = D // P
TT = T // P
HALF = 512
HD = 64
NQ, NKV = 8, 2
FF = 2816
FC = FF // P
GROUPS = (8, 8, 6)
POOL_W = (2, 4, 8, 16)
GRID = 64
ROWS = T // GRID
CTX = 256
KH, KW, QW = 8, 32, 16
NLOC = 12 * KW
NB = GRID // QW
EPS = 1e-6
NEG = -1e30
FEW = 16
KCS = [min(max(n * QW - 8, 0), GRID - KW) for n in range(NB)]
KIND = [0, 1, 1, 2]
SCALE = HD ** -0.5

NKEY = NLOC + CTX
NCH = 4 * NB + 2
NDFT = 2 * 4 * HALF + 2 * P + HALF

PARTS = ((0, 1, 2), (3, 4))


def part_col(k):
    return P * k if k < 3 else HALF + P * (k - 3)


N_IN, N_OUT1 = 0, 14
IN_ORDER = ("k", "v", "p0", "q0", "p1", "m0", "q1", "p2", "m1", "q2", "p3", "m2", "q3", "m3")
MIX_AT = [IN_ORDER.index(f"m{g}") for g in range(4)]
POOL_AT = [IN_ORDER.index(f"p{g}") for g in range(4)]
TURN_AT = [IN_ORDER.index(name) for name in ("k", "q0", "q1", "q2", "q3")]
MIXES, POOLS = {n: g for g, n in enumerate(MIX_AT)}, {n: g for g, n in enumerate(POOL_AT)}
TURNS = {n: m for m, n in enumerate(TURN_AT)}
ADA_LATE = [*range(24, 48), *range(60, 72)]
ADA2_AT = {0: 3, 1: 3, 3: 3, 6: 3}
N_UP, N_DOWN = [], []
_n = N_OUT1 + KD
for _g in GROUPS:
    N_UP.append(_n)
    N_DOWN.append(_n + 2 * _g)
    _n += 2 * _g + KD
N_ATT2 = _n
N_F = N_ATT2 + 16
N_GF = N_F + 8
N_GC = N_GF + 16
N_A = N_GC + 16
N_GA = N_A + 16
N_OUT2 = N_GA + 16

_VECS = [("b_ada", 48), ("norm1_g", 8), ("pool_scale", 4), ("norm2_g", 8), ("conv_w", 132), ("conv_b", 44),
         ("b_ada_2", 24), ("norm_g_2", 8), ("b_in_2", 64), ("w_conv_2", 12), ("b_conv_2", 4), ("final_g_2", 8),
         ("q_norm_g", 1), ("k_norm_g", 1)]
VCOL, NVEC = {}, 0
for _name, _w in _VECS:
    VCOL[_name] = NVEC
    NVEC += _w
_CONSTS = [("ident", 128), ("headmean", 128), ("rot", 128), ("headsel", 2), ("one", 1), ("eps", 1), ("zero", 1), ("edge", 64)]
CCOL, NCONST = {}, 0
for _name, _w in _CONSTS:
    CCOL[_name] = NCONST
    NCONST += _w


class Steps:

    def __init__(self, eng, sem):
        self.eng, self.sem, self.done, self.before = eng, sem, 0, 0

    def did(self, ins):
        ins.then_inc(self.sem, 1)
        self.done += 1

    def settle(self):
        self.eng.wait_ge(self.sem, self.before + self.done)

    @contextmanager
    def loop(self, count, each):
        first = self.done
        with self.eng.Fori(0, count) as it:
            self.before = it * each
            yield it
        assert self.done - first == each, (self.done - first, each)
        self.before, self.done = 0, first + count * each


def build(nc, A, out):
    ctx = ExitStack()
    with ctx:
        BASE = 16512

        def at(name, kb, shape, dt=F32):
            return nc.alloc_sbuf_tensor_at(name, shape, dt, offset=BASE + int(kb * 1024))

        def sem(name):
            return ctx.enter_context(nc.semaphore(name))

        XT = at("XT", 0, [P, KD, T])
        QN = at("QN", 0, [P, 4, T])
        KN = at("KN", 16, [P, T])
        VN = at("VN", 20, [P, T])
        ROPE1 = at("ROPE1", 24, [P, T])
        ROPE2 = at("ROPE2", 28, [P, T])
        KHI = at("KHI", 24, [P, T], F32R)
        KLO = at("KLO", 28, [P, T])
        QST = [at(f"QST{s}", 24 + 4 * s, [P, NQ, P], F32R) for s in range(2)]
        HH = at("HH", 32, [P, KD, T], F32R)
        HL = at("HL", 64, [P, KD, T], F32R)
        SQ = [at(f"SQ{s}", 64 + 4 * s, [P, T]) for s in range(2)]
        PTH = at("PTH", 32, [P, TT, 4, P], F32R)
        PTL = at("PTL", 48, [P, TT, 4, P], F32R)
        EX = [at(f"EX{s}", kb, [P, T]) for s, kb in enumerate((64, 68, 16, 20))]
        VTOK = at("VTOK", 72, [P, TT, NKV, P], F32R)
        C1B = at("C1B", 80, [P, D])
        QH = at("QH", 88, [P, 4, P], F32R)
        QL = at("QL", 90, [P, 4, P])
        OT = at("OT", 92, [P, 4, P])
        OTMP = at("OTMP", 94, [P, HALF])
        ADA1 = [at(f"ADA1{j}", 96 + 16 * j, [P, 4, D]) for j in range(4)]
        C1A = at("C1A", 56, [P, D])
        SQS = at("SQS", 72, [P, T])
        SQ1 = at("SQ1", 64, [P, KD, T])
        ADA2 = [at(f"ADA2{s}", kb, [P, 2, D]) for s, kb in enumerate((8, 152))]
        C2B = [at(f"C2B{v}", 120 + 4 * v, [P, D]) for v in range(2)]
        MH = at("MH", 96, [P, KD, T], F32R)
        ML = at("ML", 128, [P, KD, T], F32R)
        COS = at("COS", 96, [P, T])
        SIN = at("SIN", 100, [P, T])
        PLH = at("PLH", 104, [P, T], F32R)
        PLL = at("PLL", 108, [P, T], F32R)
        PAD = 8
        UP = at("UP", 128, [P, T + 2 * PAD])
        WINS = [at("WIN0", 132.5, [P, T + 2 * PAD]), at("WIN1", 137, [P, T + 2 * PAD])]
        GH = at("GH", 96, [P, 8, T], F32R)
        GL = at("GL", 128, [P, 8, T], F32R)
        CX = at("CX", 152, [P, KD, CTX])
        SQC = at("SQC", 120, [P, KD, CTX])
        HCH = at("HCH", 120, [P, KD, CTX], F32R)
        HCL = at("HCL", 152, [P, KD, CTX], F32R)
        BIAS = [at(f"BIAS{j}", 9 * j, [P, 6, NLOC]) for j in range(2)]
        VTOK2 = at("VTOK2", 18, [P, NCH, P])
        PT2 = [at("PT20", 27, [P, NKEY]), at("PT21", 117, [P, NKEY])]
        EX2 = [at(f"EX2{s}", kb, [P, NKEY]) for s, kb in enumerate((112, 114.5, 29.5))]
        Q2 = at("Q2", 128, [P, T])
        K2 = at("K2", 128, [P, T + CTX])
        KC2H = at("KC2H", 133, [P, 2, CTX], F32R)
        K2L = at("K2L", 141, [P, 2, T + CTX], F32R)
        Q2S = at("Q2S", 184, [P, 2, T], F32R)
        K2H = at("K2H", 192, [P, 2, T], F32R)
        SZ = at("SZ", 137, [P, T])
        VT2 = at("VT2", 141, [P, NB * ROWS * KW + CTX])
        CBF = at("CBF", 96, [P, 4, T])
        DFT = at("DFT", 0, [P, NDFT])
        VW = at("VW", 20, [P, 8, P])
        VROW = at("VROW", 24, [P, P])
        FE = at("FE", 25, [P, HALF + 1])
        FO = at("FO", 27.25, [P, HALF])
        SB = at("SB", 29.25, [P, HALF])
        ALT = at("ALT", 31.25, [P, 4])
        BRH = at("BRH", 128, [P, 4, T], F32R)
        BRL = at("BRL", 144, [P, 4, T], F32R)
        CBL = at("CBL", 96, [P, 4, T], F32R)
        CBH = at("CBH", 112, [P, 4, T], F32R)
        S = at("S", 0, [P, KD, T])
        SL = at("SL", 0, [P, KD, T], F32R)
        SH = at("SH", 96, [P, KD, T], F32R)
        XT2 = at("XT2", 32, [P, KD, T])
        WF = [at(f"WF{s}", 160 + 4 * s, [P, KD, P]) for s in range(2)]
        C2C = [at(f"C2C{v}", 84 + 4 * v, [P, D]) for v in range(2)]
        JUNK = at("JUNK", 92, [P, D])
        ADA4 = [at(f"ADA4{s}", 32 + 16 * s, [P, 4, D]) for s in range(2)]
        ADA3 = [at(f"ADA3{s}", 160 + 4 * s, [P, D]) for s in range(2)]
        WH = [at(f"WH{s}", 168 + 4 * s, [P, KD, P], F32R) for s in range(2)]
        WL = [at(f"WL{s}", 176 + 4 * s, [P, KD, P], F32R) for s in range(2)]
        EV = [at(f"EV{s}", 184 + 4 * s, [P, T]) for s in range(2)]
        CV = [at(f"CV{s}", 192 + 4 * s, [P, T]) for s in range(2)]
        KSH = at("KSH", 184, [P, NKV, T], F32R)
        KSL = at("KSL", 192, [P, NKV, T], F32R)
        VEC = at("VEC", 200, [P, NVEC])
        CON = at("CON", 200 + 1.5625, [P, NCONST])
        small = 200 + 1.5625 + 1.8125
        MOD1 = at("MOD1", small, [P, 48])
        MOD2 = at("MOD2", small + 0.1875, [P, 24, 2])
        A1 = at("A1", small + 0.375, [P, KD])
        A2 = at("A2", small + 0.40625, [P, KD])
        A3 = at("A3", small + 0.4375, [P, KD, 2])
        SD = at("SD", small + 0.59375, [P, TT])
        RS = at("RS", small + 0.625, [P, TT])
        QSD = at("QSD", small + 0.65625, [P, TT, NQ])
        RSP = at("RSP", small + 0.90625, [P, TT, NQ])
        RSN = at("RSN", small + 1.15625, [P, TT, NQ])
        NIL = at("NIL", small + 0.5625, [P, 1])
        RC2 = at("RC2", small + 0.5, [P, 2])
        SD2 = at("SD2", small + 0.53125, [P, 2])
        MX = at("MX", small + 1.40625, [P, 8])
        NBI = at("NBI", small + 1.4375, [P, 8])
        SUM = at("SUM", small + 1.46875, [P, 8])
        RC = at("RC", small + 1.5, [P, 8])
        DG = [at(f"DG{s}", small + 1.625 + 0.5 * s, [P, P]) for s in range(2)]
        BQ8 = at("BQ8", small + 1.53125, [P, 8])

        def vec(name, j=0, w=1):
            c = VCOL[name] + j
            return VEC[:, c:c + w] if isinstance(j, int) else VEC[:, bass.ds(c, w)]

        def con(name, w, j=0):
            return CON[:, CCOL[name] + j:CCOL[name] + j + w]

        ident, one, eps, zero = con("ident", P), con("one", 1), con("eps", 1), con("zero", 1)

        acc = ctx.enter_context(nc.psum_tensor("acc", [P, 2, T], F32))
        turn = ctx.enter_context(nc.psum_tensor("turn", [P, T], F32))
        bank6 = ctx.enter_context(nc.psum_tensor("bank6", [P, HALF], F32))
        bank7 = ctx.enter_context(nc.psum_tensor("bank7", [P, HALF], F32))

        turns = [turn[:, 0:HALF], turn[:, HALF:], bank7[:, :]]

        consts_in, x_in, rope_in = sem("consts_in"), [sem("x_in0"), sem("x_in1")], sem("rope_in")
        cond_in, cond_ready = sem("cond_in"), sem("cond_ready")
        ada1_in = [sem(f"ada1_in{j}") for j in range(4)]
        ada2_in, ada3_in = [sem("ada2_in0"), sem("ada2_in1")], [sem("ada3_in0"), sem("ada3_in1")]
        ada4_in = [sem("ada4_in0"), sem("ada4_in1")]
        ada_used = sem("ada_used")
        w_in = [sem("w_in0"), sem("w_in1")]
        w_hi, w_split = sem("w_hi"), sem("w_split")
        acc_done, acc_read, post_done = sem("acc_done"), sem("acc_read"), sem("post_done")
        act_step, dve_step, pool_step = sem("act_step"), sem("dve_step"), sem("pool_step")
        sq_ready, sq_used = sem("sq_ready"), sem("sq_used")
        sd_ready, rs_ready, rb_done = sem("sd_ready"), sem("rs_ready"), sem("rb_done")
        xn_ready, hf_ready, hh_ready, hl_ready = sem("xn_ready"), sem("hf_ready"), sem("hh_ready"), sem("hl_ready")
        hl0_ready, sq_summed, stat_done = sem("hl0_ready"), sem("sq_summed"), sem("stat_done")
        mods_ready = sem("mods_ready")
        sqh_ready, qstat_done, rot_done, kms_done = sem("sqh_ready"), sem("qstat_done"), sem("rot_done"), sem("kms_done")
        ksd_ready, qsd_ready, pooled, plh_ready, pll_ready = (
            sem("ksd_ready"), sem("qsd_ready"), sem("pooled"), sem("plh_ready"), sem("pll_ready"))
        mixh_ready = sem("mixh_ready")
        khi_ready, klo_ready, kst_act, kst_dve = sem("khi_ready"), sem("klo_ready"), sem("kst_act"), sem("kst_dve")
        vt_done, vh_ready, vl_ready = sem("vt_done"), sem("vh_ready"), sem("vl_ready")
        qh_ready, qst_act, qst_pool = sem("qh_ready"), sem("qst_act"), sem("qst_pool")
        scores_done, nb_ready, exp_done, rc_ready, dga_ready = (
            sem("scores_done"), sem("nb_ready"), sem("exp_done"), sem("rc_ready"), sem("dga_ready"))
        pt_done, pth_ready, ptl_ready, pv_done, otmp_ready, o_ready, mh_ready, ml_ready = (
            sem("pt_done"), sem("pth_ready"), sem("ptl_ready"), sem("pv_done"), sem("otmp_ready"), sem("o_ready"),
            sem("mh_ready"), sem("ml_ready"))
        x_again = [sem(f"x_again{k}") for k in range(KD)]
        gated, gh_ready = sem("gated"), sem("gh_ready")
        silu_done = sem("silu_done")
        cx_in, csq_ready, cstat_done, csd_ready, crs_ready, crb_done = (
            sem("cx_in"), sem("csq_ready"), sem("cstat_done"), sem("csd_ready"), sem("crs_ready"), sem("crb_done"))
        cxn_ready, ch_ready, hch_ready, hcl_ready = sem("cxn_ready"), sem("ch_ready"), sem("hch_ready"), sem("hcl_ready")
        x_saved, x_back = sem("x_saved"), sem("x_back")
        bias_in = [sem("bias_in0"), sem("bias_in1")]
        q2_ready, q2_hi, q2_split, k2_ready, k2_hi, k2_split = (
            sem("q2_ready"), sem("q2_hi"), sem("q2_split"), sem("k2_ready"), sem("k2_hi"), sem("k2_split"))
        vt2_done, vtok2_ready = sem("vt2_done"), sem("vtok2_ready")
        scores2_done, nb2_ready, exp2_done, dg_ready, pt2_done, pt2_ready, pv2_done, o2_ready = (
            sem("scores2_done"), sem("nb2_ready"), sem("exp2_done"), sem("dg_ready"), sem("pt2_done"), sem("pt2_ready"),
            sem("pv2_done"), sem("o2_ready"))
        cbh_ready, cbl_ready = sem("cbh_ready"), sem("cbl_ready")
        dft_in, fold_ready, chan_done, vw_ready, seq_done, sb_ready, y_ready, brh_ready = (
            sem("dft_in"), sem("fold_ready"), sem("chan_done"), sem("vw_ready"), sem("seq_done"), sem("sb_ready"),
            sem("y_ready"), sem("brh_ready"))
        sums_ready, sh_ready = sem("sums_ready"), sem("sh_ready")
        out_ready, out_sent = sem("out_ready"), sem("out_sent")

        def span(t):
            return slice(t, t + P) if isinstance(t, int) else bass.ds(t, P)

        def block_of(k):
            return slice(k, k + 1) if isinstance(k, int) else bass.ds(k, 1)

        def column(x, c):
            x = x[:, :, :].rearrange("p t h -> p (t h)")
            return x[:, c:c + 1] if isinstance(c, int) else x[:, bass.ds(c, 1)]

        block = ctx.enter_context(nc.Block())

        @block.sync
        def _(sp):
            def load_w(n, slot, name, index, k, first=False):
                if not first:
                    sp.wait_ge(w_split, n - 1)
                sp.dma_start(WF[slot][:, 0:k, :], A[name][index, :, :].rearrange("p (k n) -> p k n", n=P)
                             if isinstance(index, int) else
                             A[name][bass.ds(index, 1), :, :].rearrange("a p (k n) -> (a p) k n", n=P)
                             ).then_inc(w_in[slot], 16)

            sp.dma_start(VEC[:, :], A["vecs"]).then_inc(consts_in, 16)
            sp.dma_start(CON[:, :], A["consts"]).then_inc(consts_in, 16)
            sp.dma_start(C1A[:, :], A["conds"][0]).then_inc(cond_in, 16)
            for j in range(2):
                sp.dma_start(XT[:, 4 * j:4 * j + 4, :], A["xT"][4 * j:4 * j + 4].rearrange("k p t -> p k t")).then_inc(x_in[j], 16)
            w8 = 0
            for j in range(4):
                sp.dma_start(ADA1[j][:, :, :], A["ada"][4 * j:4 * j + 4].rearrange("a p i -> p a i")).then_inc(ada1_in[j], 16)
                if j in (1, 2):
                    load_w(w8, w8, "w8", w8, KD, first=True)
                    w8 += 1
            sp.wait_ge(mods_ready, 4)
            sp.dma_start(COS[:, :], A["rope"][0]).then_inc(rope_in, 16)
            sp.dma_start(SIN[:, :], A["rope"][1]).then_inc(rope_in, 16)
            for v in range(2):
                sp.dma_start(C2B[v][:, :], A["conds"][1 + v]).then_inc(cond_in, 16)

            def load_ada2(h):
                if h >= 2:
                    sp.wait_ge(ada_used, 16 + 2 * h - 2)
                sp.dma_start(ADA2[h % 2][:, :, :], A["ada"][48 + 2 * h:50 + 2 * h].rearrange("a p i -> p a i")
                             ).then_inc(ada2_in[h % 2], 16)

            sp.wait_ge(xn_ready, KD)
            load_ada2(0)
            load_ada2(1)
            ada2_next = 2
            for n in range(2, N_OUT1 + 2):
                if n in MIXES:
                    load_w(n, n % 2, "w1", MIXES[n], 1)
                else:
                    load_w(n, n % 2, "w8", w8, KD)
                    w8 += 1
                used = sum(count for t, count in ADA2_AT.items() if t <= n - 2)
                while ada2_next < min(6, used // 2 + 2):
                    load_ada2(ada2_next)
                    ada2_next += 1
            sp.wait_ge(acc_done, N_OUT1)
            sp.wait_ge(hl0_ready, KD)
            sp.dma_start(C1B[:, :], A["conds"][0]).then_inc(cond_in, 16)
            sp.wait_ge(w_split, N_OUT1 + 2)
            for s in range(2):
                sp.dma_start(ADA3[s][:, :], A["ada"][16 + s]).then_inc(ada3_in[s], 16)
            with sp.Fori(1, 4) as it:
                for s in range(2):
                    src = A["ada"][bass.ds(it * 2 + (16 + s), 1), :, :].rearrange("a p i -> (a p) i")
                    sp.wait_ge(ada_used, it * 2 + (28 + s - 1))
                    sp.dma_start(ADA3[s][:, :], src).then_inc(ada3_in[s], 16)
            def load_ada4(j):
                if j >= 2:
                    sp.wait_ge(ada_used, 36 + 4 * (j - 1))
                i = ADA_LATE[4 * j]
                sp.dma_start(ADA4[j % 2][:, :, :], A["ada"][i:i + 4].rearrange("a p i -> p a i")).then_inc(ada4_in[j % 2], 16)

            sp.wait_ge(qst_pool, 16)
            for v in range(2):
                sp.dma_start(C2C[v][:, :], A["conds"][1 + v]).then_inc(cond_in, 16)
            sp.wait_ge(pv_done, 34)
            for k in range(KD):
                sp.dma_start(XT[:, k, :], A["xT"][k]).then_inc(x_again[k], 16)
                if k < 2:
                    load_ada4(k)
            sp.wait_ge(ada_used, 36)
            for n in range(2, KD):
                load_w(N_OUT1 + n, n % 2, "w8", w8 + n - 2, KD)
                load_ada4(n)
            load_ada4(8)
            w8 += 6
            for g, gk in enumerate(GROUPS):
                for s in range(2):
                    load_w(N_UP[g] + s, s, "w8", w8 + s, KD)
                if g == 2:
                    sp.wait_ge(acc_done, N_UP[2])
                    sp.dma_start(CX[:, :, :], A["ctxT"].rearrange("k p t -> p k t")).then_inc(cx_in, 16)
                with sp.Fori(1, gk) as it:
                    for s in range(2):
                        load_w(it * 2 + (N_UP[g] + s), s, "w8", it * 2 + (w8 + s), KD)
                w8 += 2 * gk
                name, first = ("w8", w8) if gk == KD else ("w6", 0)
                with sp.Fori(0, 4) as it:
                    for s in range(2):
                        load_w(it * 2 + (N_DOWN[g] + s), s, name, it * 2 + (first + s), gk)
                if gk == KD:
                    w8 += KD
            for s in range(2):
                load_w(N_ATT2 + s, s, "w8", w8 + s, KD)
            sp.wait_ge(post_done, N_ATT2)
            sp.dma_start(out.rearrange("k p t -> p k t"), XT[:, :, :]).then_inc(x_saved, 16)
            sp.wait_ge(x_saved, 16)
            sp.wait_ge(xn_ready, 3 * KD)
            for j in range(2):
                sp.dma_start(BIAS[j][:, :, :], A["bias"][j]).then_inc(bias_in[j], 16)
            for s in range(2):
                load_w(N_ATT2 + 2 + s, s, "w8", w8 + 2 + s, KD)
            with sp.Fori(1, 4) as it:
                for s in range(2):
                    load_w(it * 4 + (N_ATT2 + s), s, "w8", it * 4 + (w8 + s), KD)
                for j in range(2):
                    src = A["bias"][bass.ds(it * 2 + j, 1), :, :, :].rearrange("a p k n -> (a p) k n")
                    sp.wait_ge(nb2_ready, it * 16 + (8 * j - 8))
                    sp.dma_start(BIAS[j][:, :, :], src).then_inc(bias_in[j], 16)
                for s in range(2):
                    load_w(it * 4 + (N_ATT2 + 2 + s), s, "w8", it * 4 + (w8 + 2 + s), KD)
            w8 += 16
            for s in range(2):
                load_w(N_F + s, s, "w8", w8 + s, KD)
            sp.wait_ge(nb2_ready, 64)
            sp.wait_ge(pt2_done, 128)
            sp.wait_ge(pv2_done, 64)
            sp.dma_start(DFT[:, :], A["dft"]).then_inc(dft_in, 16)
            with sp.Fori(1, 4) as it:
                for s in range(2):
                    load_w(it * 2 + (N_F + s), s, "w8", it * 2 + (w8 + s), KD)
            w8 += 8

            def gate_weights(n0, w8, w4):
                with sp.Fori(0, KD) as it:
                    load_w(it * 2 + n0, 0, "w8", it + w8, KD)
                    load_w(it * 2 + (n0 + 1), 1, "w4", it + w4, 4)

            gate_weights(N_GF, w8, 0)
            gate_weights(N_GC, w8 + KD, KD)
            w8 += 2 * KD
            with sp.Fori(0, 8) as it:
                for s in range(2):
                    load_w(it * 2 + (N_A + s), s, "w8", it * 2 + (w8 + s), KD)
            w8 += 16
            gate_weights(N_GA, w8, 2 * KD)
            w8 += KD
            for s in range(2):
                load_w(N_OUT2 + s, s, "w8", w8 + s, KD)
            sp.wait_ge(acc_done, N_OUT2 - 1)
            sp.dma_start(XT2[:, :, :], out.rearrange("k p t -> p k t")).then_inc(x_back, 16)
            with sp.Fori(1, 4) as it:
                for s in range(2):
                    load_w(it * 2 + (N_OUT2 + s), s, "w8", it * 2 + (w8 + s), KD)
            for k in range(KD):
                sp.wait_ge(out_ready, k + 1)
                sp.dma_start(out[k], XT2[:, k, :]).then_inc(out_sent, 16)
            sp.wait_ge(out_sent, 16 * KD)

        @block.gpsimd
        def _(pool):
            steps = Steps(pool, pool_step)

            def split_w(n, slot, k, first=False):
                pool.wait_ge(w_in[slot], (n - slot) * 8 + 16)
                if not first:
                    pool.wait_ge(acc_done, n - 1)
                f, h = WF[slot][:, :, :].rearrange("p k n -> p (k n)"), WH[slot][:, :, :].rearrange("p k n -> p (k n)")
                pool.tensor_tensor(h[:, 0:FEW], f[:, 0:FEW], zero.to_broadcast([P, FEW]), ALU.add).then_inc(w_hi, 1)
                pool.tensor_scalar(h[:, FEW:k * P], f[:, FEW:k * P], 1.0, 1.0, ALU.mult, ALU.mult).then_inc(w_hi, 1)
                pool.wait_ge(w_hi, n * 2 + 2)
                pool.tensor_tensor(WL[slot][:, 0:k, :], WF[slot][:, 0:k, :], WH[slot][:, 0:k, :].bitcast(F32),
                                   ALU.subtract).then_inc(w_split, 1)

            pool.wait_ge(consts_in, 32)
            for n in range(N_OUT1 + 2):
                split_w(n, n % 2, 1 if n in MIXES else KD, first=n < 2)
                if n < 2:
                    for k in range(4 * n, 4 * n + 4):
                        pool.wait_ge(hh_ready, k + 1)
                        pool.tensor_tensor(HL[:, k, :], CV[k % 2][:, :], HH[:, k, :].bitcast(F32), ALU.subtract
                                           ).then_inc(hl0_ready, 1)
            def stack_queries(it, s, step, done=None):
                if step == 0:
                    pool.wait_ge(qh_ready, it * 2 + (s + 1))
                    steps.did(pool.tensor_tensor(QL[:, :, :], QN[:, :, span(it * 256 + 128 * s)], QH[:, :, :].bitcast(F32),
                                                 ALU.subtract))
                else:
                    b = step - 1
                    steps.settle()
                    if done is not None:
                        pool.wait_ge(dga_ready, done)
                    dst = QST[s % 2][64:128, :, :].rearrange("p (i j) q -> p i j q", j=2)[:, :, b, :]
                    pool.tensor_tensor(dst, QL[64 * b:64 * b + 64, :, :],
                                       zero[64 * b:64 * b + 64, :].unsqueeze(2).to_broadcast([HD, 4, P]), ALU.add
                                       ).then_inc(qst_pool, 1)
                    pool.wait_ge(qst_pool, it * 4 + (2 * s + b + 1))

            def diagonal(it, u):
                pool.wait_ge(rc_ready, it * 16 + (u + 1))
                pool.tensor_tensor(DG[u % 2][:, :], ident, RC[:, u % 2:u % 2 + 1].to_broadcast([P, P]), ALU.mult
                                   ).then_inc(dga_ready, 1)

            def attend(it, last):
                for u in range(16):
                    if u < 15 or not last:
                        diagonal(it, u + 1)
                    if 1 <= u <= 3:
                        stack_queries(it, 1, u - 1, it * 16 + (u + 2))
                    if 9 <= u <= 11 and not last:
                        stack_queries(it, 2, u - 9, it * 16 + (u + 2))
                    if u == 8:
                        branch_second(it, 0)
                branch_second(it, 1)

            def branch_second(it, s):
                pool.wait_ge(mh_ready, it * 2 + (s + 1))
                sl = span(it * 256 + 128 * s)
                pool.tensor_tensor(ML[:, 0:4, sl], OT[:, :, :], MH[:, 0:4, sl].bitcast(F32), ALU.subtract).then_inc(ml_ready, 1)

            pool.tensor_tensor(NIL[:, :], zero, zero, ALU.add).then_inc(ml_ready, 1)
            pool.wait_ge(kst_dve, 4)
            pool.wait_ge(kst_act, 4)
            for step in range(3):
                stack_queries(0, 0, step)
            diagonal(0, 0)
            with steps.loop(3, 2) as it:
                attend(it, False)
            attend(3, True)
            with pool.Fori(0, 3) as it:
                for s in range(2):
                    split_w(it * 2 + (N_OUT1 + 2 + s), s, KD)
            for g, gk in enumerate(GROUPS):
                with pool.Fori(0, gk) as it:
                    for s in range(2):
                        split_w(it * 2 + (N_UP[g] + s), s, KD)
                with pool.Fori(0, 4) as it:
                    for s in range(2):
                        split_w(it * 2 + (N_DOWN[g] + s), s, gk)
            for n0, count, k1 in ((N_ATT2, 12, KD), (N_GF, 16, 4), (N_A, 8, KD), (N_GA, 8, 4), (N_OUT2, 4, KD)):
                with pool.Fori(0, count) as it:
                    split_w(it * 2 + n0, 0, KD)
                    split_w(it * 2 + (n0 + 1), 1, k1)

        @block.tensor
        def _(pe):
            def gemm(n, slot, hi, lo, k_n=KD, ready=None, context=None, last_chunk=None):
                pe.wait_ge(w_split, n + 1)
                if not isinstance(n, int) or n >= 2:
                    pe.wait_ge(acc_read, n - 1)
                if context is not None:
                    for k in range(k_n):
                        for w, x in ((WH, HCH), (WH, HCL), (WL, HCH)):
                            pe.matmul(context[:, 0:CTX], w[slot][:, k, :], x[:, k, :],
                                      start=(k == 0 and w is WH and x is HCH), stop=(k == k_n - 1 and w is WL))
                for k in range(k_n):
                    if ready is not None:
                        pe.wait_ge(ready, hl_base[0] + k + 1)
                    if k == k_n - 1 and last_chunk is not None:
                        pe.wait_ge(post_done, last_chunk)
                    for w, x in ((WH, hi), (WH, lo), (WL, hi)):
                        for c in range(2):
                            last = pe.matmul(acc[:, slot, HALF * c:HALF * c + HALF], w[slot][:, k, :],
                                             x[:, k, HALF * c:HALF * c + HALF],
                                             start=(k == 0 and w is WH and x is hi), stop=(k == k_n - 1 and w is WL))
                last.then_inc(acc_done, 1)

            hl_base = [0]

            def stats(q, sums):
                pe.wait_ge(sq_summed, q + 1)
                for t in range(TT):
                    mm = pe.matmul(bank6[:, t:t + 1], sums[:, P * t:P * t + P], one, start=True, stop=True)
                mm.then_inc(stat_done, 1)

            def spread_rs(q, nt=TT):
                pe.wait_ge(rs_ready, q + 1)
                for t in range(nt):
                    mm = pe.matmul(turn[:, P * t:P * t + P], RS[:, t:t + 1].to_broadcast([P, P]), ident,
                                   start=True, stop=True)
                mm.then_inc(rb_done, 1)

            pe.wait_ge(consts_in, 32)
            stats(0, SQ1[:, 0, :])
            spread_rs(0)

            def rotate(m):
                n = TURN_AT[m]
                pe.wait_ge(sqh_ready, m + 1)
                if m == 0:
                    for c in range(2):
                        mm = pe.matmul(turn[:, HALF * c:HALF * c + HALF], con("headmean", P),
                                       CV[n % 2][:, HALF * c:HALF * c + HALF], start=True, stop=True)
                    mm.then_inc(kms_done, 1)
                    pe.wait_ge(ksd_ready, 1)
                else:
                    for t in range(TT):
                        mm = pe.matmul(bank6[:, 64 + t * NQ + 2 * (m - 1):64 + t * NQ + 2 * m],
                                       CV[n % 2][:, P * t:P * t + P], con("headsel", 2), start=True, stop=True)
                    mm.then_inc(qstat_done, 1)
                if m > 0:
                    pe.wait_ge(post_done, TURN_AT[m - 1] + 1)
                for c in range(2):
                    mm = pe.matmul(turn[:, HALF * c:HALF * c + HALF], con("rot", P), EV[n % 2][:, HALF * c:HALF * c + HALF],
                                   start=True, stop=True)
                mm.then_inc(rot_done, 1)

            for n in range(N_OUT1):
                if n in MIXES:
                    g = MIXES[n]
                    pe.wait_ge(w_split, n + 1)
                    pe.wait_ge(acc_read, n - 1)
                    pe.wait_ge(pll_ready, g + 1)
                    for w, x in ((WH, PLH), (WH, PLL), (WL, PLH)):
                        for c in range(2):
                            mm = pe.matmul(acc[:, n % 2, HALF * c:HALF * c + HALF], w[n % 2][:, 0, :],
                                           x[:, HALF * c:HALF * c + HALF],
                                           start=(w is WH and x is PLH), stop=(w is WL))
                    mm.then_inc(acc_done, 1)
                else:
                    gemm(n, n % 2, HH, HL, ready=hl0_ready if n == 0 else None)
                if n - 1 in TURNS:
                    rotate(TURNS[n - 1])
            pe.wait_ge(post_done, TURN_AT[-1] + 1)
            for t in range(TT):
                mm = pe.transpose(turn[:, P * t:P * t + P], VN[:, P * t:P * t + P], ident)
            mm.then_inc(vt_done, 1)
            pe.wait_ge(kst_act, 4)
            pe.wait_ge(kst_dve, 4)
            pe.wait_ge(acc_read, N_OUT1)
            pe.wait_ge(vl_ready, 1)

            def scores(it, u):
                s, h = u // 8 % 2, u % 8
                if u % 8 == 0:
                    pe.wait_ge(qst_act, it * 4 + (2 * (u // 8) + 2))
                    pe.wait_ge(qst_pool, it * 4 + (2 * (u // 8) + 2))
                if u >= 2:
                    pe.wait_ge(exp_done, it * 16 + (u - 1))
                for ks in (KSH, KSL):
                    for c in range(2):
                        mm = pe.matmul(acc[:, u % 2, HALF * c:HALF * c + HALF], QST[s][:, h, :],
                                       ks[:, h // 4, HALF * c:HALF * c + HALF], start=(ks is KSH), stop=(ks is KSL))
                mm.then_inc(scores_done, 1)

            def attend(it, last):
                for u in range(16):
                    now = it * 32 + 2 * u
                    if u % 2 == 1 and (u < 14 or not last):
                        scores(it, u + 2)
                    pe.wait_ge(dga_ready, it * 16 + (u + 1))
                    for h in range(2):
                        q = 2 * u + h
                        pe.wait_ge(ptl_ready, now + (h if q >= 2 else h + 1))
                        for k in range(4 * h, 4 * h + 4):
                            mm = pe.matmul(turns[q % 3][:, P * (k % 4):P * (k % 4) + P], EX[u % 4][:, P * k:P * k + P], DG[u % 2][:, :],
                                           start=True, stop=True)
                        mm.then_inc(pt_done, 1)
                    if u % 2 == 1:
                        if u < 13 or not last:
                            scores(it, u + 3)
                        b, c = u // 4, u % 4 - 1
                        if c == 0:
                            pe.wait_ge(o_ready, it * 4 + (b + 1))
                        for k in range(TT):
                            if k % 4 == 0:
                                pe.wait_ge(ptl_ready, now + (2 + k // 4 + 1))
                            for x in (PTH, PTL):
                                mm = pe.matmul(bank6[:, P * c:P * c + 2 * P], VTOK[:, k, b % 2, :], x[:, k, c:c + 2, :],
                                               start=(k == 0 and x is PTH), stop=(k == TT - 1 and x is PTL))
                        mm.then_inc(pv_done, 1)

            pe.matmul(bank6[0:1, 0:1], one, one, start=True, stop=True).then_inc(pv_done, 2)
            for u in range(3):
                scores(0, u)
            with pe.Fori(0, 3) as it:
                attend(it, False)
            attend(3, True)
            pe.wait_ge(o_ready, 17)
            pe.wait_ge(ml_ready, 9)
            pe.wait_ge(mh_ready, 8)
            pe.wait_ge(exp_done, 64)

            def residual_tiles(q, n0, hi, lo, k_n, with_stats, last_chunk=None):
                for s in range(2):
                    gemm(n0 + s, s, hi, lo, k_n, last_chunk=last_chunk if s == 0 else None)
                with pe.Fori(1, 4) as it:
                    for s in range(2):
                        gemm(it * 2 + (n0 + s), s, hi, lo, k_n)
                if with_stats:
                    stats(q, SQS)

            residual_tiles(1, N_OUT1, MH, ML, KD, True)
            spread_rs(1)
            for g, gk in enumerate(GROUPS):
                hl_base[0] = 0
                gemm(N_UP[g], 0, HH, HL, ready=hl_ready if g == 0 else None)
                gemm(N_UP[g] + 1, 1, HH, HL)
                if g == 2:
                    pe.wait_ge(csq_ready, 1)
                    for t in range(2):
                        for k in range(KD):
                            mm = pe.matmul(bank6[:, 16 + t:17 + t], SQC[:, k, P * t:P * t + P], one,
                                           start=(k == 0), stop=(k == KD - 1))
                    mm.then_inc(cstat_done, 1)
                with pe.Fori(1, gk) as it:
                    for s in range(2):
                        gemm(it * 2 + (N_UP[g] + s), s, HH, HL)
                if g == 2:
                    pe.wait_ge(crs_ready, 1)
                    for t in range(2):
                        mm = pe.matmul(turn[:, P * t:P * t + P], RC2[:, t:t + 1].to_broadcast([P, P]), ident,
                                       start=True, stop=True)
                    mm.then_inc(crb_done, 1)
                pe.wait_ge(post_done, N_UP[g] + 2 * gk - 2)
                residual_tiles(2, N_DOWN[g], GH, GL, gk, g == 2, last_chunk=N_UP[g] + 2 * gk)

            pe.wait_ge(cxn_ready, 1)
            spread_rs(2)
            hl_base[0] = KD

            def att_pair(n, pair, first):
                u0 = pair * 16
                if not first:
                    pe.wait_ge(exp2_done, u0)
                    pe.wait_ge(o2_ready, u0)
                else:
                    pe.wait_ge(hcl_ready, 1)
                gemm(n, 0, HH, HL, ready=hl_ready if first else None, context=bank7)
                gemm(n + 1, 1, HH, HL)
                pe.wait_ge(acc_read, n + 1)
                if first:
                    pe.wait_ge(xn_ready, 3 * KD)

                def turn_values(b, c0, c1):
                    if b > 0:
                        pe.wait_ge(vtok2_ready, pair * 3 + b)
                    for c in range(c0, c1):
                        mm = pe.transpose(turn[:, P * (c - c0):P * (c - c0) + P], VT2[:, P * c:P * c + P], ident)
                    mm.then_inc(vt2_done, 1)

                turn_values(0, 0, 8)
                turn_values(1, 8, 16)
                turn_values(2, 16, 18)
                gemm(n + 2, 0, HH, HL, context=bank6)
                gemm(n + 3, 1, HH, HL)

                def scores(u):
                    j, half, c = u // 8, u // 4 % 2, u % NB
                    a = acc[:, u % 2, :]
                    if u < 2:
                        pe.wait_ge(acc_read, n + 4)
                        pe.wait_ge(q2_split, pair * 2 + 2)
                        pe.wait_ge(k2_split, pair * 2 + 2)
                    else:
                        pe.wait_ge(exp2_done, u0 + (u - 1))
                    q = Q2S[:, j, HALF * half + P * c:HALF * half + P * c + P]
                    for part in (K2H, K2L):
                        rows = part[:, j, 0:T].rearrange("p (r c) -> p r c", c=GRID)
                        pe.matmul(a[:, P:P + NLOC], q, rows[:, 4 * half:4 * half + 12, KCS[c]:KCS[c] + KW],
                                  start=(part is K2H), stop=(part is K2L))
                    pe.matmul(a[:, HALF:HALF + CTX], q, KC2H[:, j, :], start=True, stop=False)
                    pe.matmul(a[:, HALF:HALF + CTX], q, K2L[:, j, T:], start=False, stop=True).then_inc(scores2_done, 1)

                def turn_probs(u):
                    pe.wait_ge(dg_ready, u0 + (u + 1))
                    if u == 0:
                        pe.wait_ge(vtok2_ready, pair * 3 + 3)
                    for h, ks in enumerate(PARTS):
                        if u > 0:
                            pe.wait_ge(pt2_ready, 2 * u0 + (2 * u + h - 1))
                        for k in ks:
                            mm = pe.matmul(turn[:, part_col(k):part_col(k) + P], EX2[u % 3][:, P * k:P * k + P], DG[u % 2][:, :],
                                           start=True, stop=True)
                        mm.then_inc(pt2_done, 1)

                def values(u):
                    half, c = u // 4 % 2, u % NB
                    if u >= 2:
                        pe.wait_ge(o2_ready, u0 + (u - 1))
                    bank = (bank6, bank7)[u % 2]
                    for k in range(NKEY // P):
                        if k in (PARTS[0][0], PARTS[1][0]):
                            pe.wait_ge(pt2_ready, 2 * u0 + (2 * u + (1 if k == 0 else 2)))
                        kc = 4 * c + half + k if k < 3 else 4 * NB + k - 3
                        mm = pe.matmul(bank[:, 0:P], VTOK2[:, kc, :], PT2[u % 2][:, P * k:P * k + P],
                                       start=(k == 0), stop=(k == NKEY // P - 1))
                    mm.then_inc(pv2_done, 1)

                scores(0)
                scores(1)
                for u in range(16):
                    if u < 14:
                        scores(u + 2)
                    if u > 0:
                        values(u - 1)
                    turn_probs(u)
                values(15)

            att_pair(N_ATT2, 0, True)
            with pe.Fori(1, 4) as it:
                att_pair(it * 4 + N_ATT2, it, False)

            pe.wait_ge(exp2_done, 64)
            pe.wait_ge(o2_ready, 64)
            COS_T, SIN_T = DFT[:, 0:4 * HALF], DFT[:, 4 * HALF:8 * HALF]
            COS_C, SIN_C = DFT[:, 8 * HALF:8 * HALF + P], DFT[:, 8 * HALF + P:8 * HALF + 2 * P]
            SIGNS = DFT[0:1, 8 * HALF + 2 * P:NDFT]

            def channels(it):
                pe.wait_ge(dft_in, 16)
                pe.wait_ge(fold_ready, it + 1)
                pe.wait_ge(y_ready, it * 2 + 1)
                for f, c, o in ((FE, COS_C, 0), (FO, SIN_C, HALF)):
                    for t in range(4):
                        pe.matmul(turn[:, o + P * t:o + P * t + P], f[:, P * t:P * t + P], c, start=True, stop=True)
                pe.matmul(bank6[0:1, 0:P], FE[:, HALF:HALF + 1], COS_C, start=True, stop=True)
                pe.matmul(bank6[:, P:P + 1], COS_C, ALT[:, 2:3], start=True, stop=True).then_inc(chan_done, 1)

            def tokens(it):
                pe.wait_ge(vw_ready, it * 2 + 2)
                for t in range(4):
                    pe.matmul(bank7[:, :], VW[:, t, :], COS_T[:, HALF * t:HALF * t + HALF], start=(t == 0), stop=False)
                pe.matmul(bank7[:, :], VROW[0:1, :], SIGNS, start=False, stop=True)
                for t in range(4):
                    mm = pe.matmul(bank6[:, :], VW[:, 4 + t, :], SIN_T[:, HALF * t:HALF * t + HALF], start=(t == 0), stop=(t == 3))
                mm.then_inc(seq_done, 1)

            gemm(N_F, 0, HH, HL)
            gemm(N_F + 1, 1, HH, HL)
            channels(0)
            with pe.Fori(1, 4) as it:
                n = it * 2 + N_F
                gemm(n, 0, HH, HL)
                tokens(it - 1)
                gemm(n + 1, 1, HH, HL)
                channels(it)
            tokens(3)

            def gates(n0, hi, lo, sem_, value):
                with pe.Fori(0, KD) as it:
                    gemm(it * 2 + n0, 0, HH, HL)
                    pe.wait_ge(sem_, value)
                    gemm(it * 2 + (n0 + 1), 1, hi, lo, 4)

            gates(N_GF, BRH, BRL, post_done, N_GF)
            gates(N_GC, CBH, CBL, cbl_ready, 1)
            with pe.Fori(0, 8) as it:
                for s in range(2):
                    gemm(it * 2 + (N_A + s), s, HH, HL)
            gates(N_GA, BRH, BRL, post_done, N_GA)
            pe.wait_ge(post_done, N_OUT2 - 2)
            residual_tiles(3, N_OUT2, SH, SL, KD, True, last_chunk=N_OUT2)
            spread_rs(3)

        @block.scalar
        def _(act):
            steps = Steps(act, act_step)

            def evac_wait(n):
                act.wait_ge(acc_done, n + 1)
                if not isinstance(n, int) or n >= 2:
                    act.wait_ge(post_done, n - 1)

            def square(q, k, slot, src):
                if not isinstance(k, int) or q * KD + k >= 2:
                    act.wait_ge(sq_used, q * KD + k - 1)
                act.activation(SQ[slot][:, :], src, ACT.Square).then_inc(sq_ready, 1)

            def root(q, nt=TT):
                act.wait_ge(stat_done, q + 1)
                act.activation(SD[:, 0:nt], bank6[:, 0:nt], ACT.Sqrt, bias=eps, scale=1.0 / D).then_inc(sd_ready, 1)

            def second_parts(q, count):
                return (hl0_ready, count) if q == 0 else (hl_ready, (q - 1) * KD + count)

            def modulate(q, scale, shift, hh):
                for k in range(KD):
                    act.wait_ge(xn_ready, q * KD + k + 1)
                    if k >= 2:
                        act.wait_ge(*second_parts(q, k - 1))
                    act.activation(CV[k % 2][:, :], EV[k % 2][:, :], ACT.Identity, bias=shift(k), scale=scale(k)
                                   ).then_inc(hf_ready, 1)
                    act.wait_ge(hf_ready, q * KD + k + 1)
                    act.activation(hh[:, k, :], CV[k % 2][:, :], ACT.Copy).then_inc(hh_ready, 1)

            act.wait_ge(consts_in, 32)
            act.wait_ge(cond_in, 16)
            act.activation(C1A[:, :], C1A[:, :], ACT.Silu).then_inc(cond_ready, 1)
            for k in range(KD):
                if k % 4 == 0:
                    act.wait_ge(x_in[k // 4], 16)
                act.activation(SQ1[:, k, :], XT[:, k, :], ACT.Square).then_inc(sq_ready, 1)
            root(0)
            modulate(0, lambda k: A1[:, k:k + 1], lambda k: MOD1[:, k:k + 1], HH)

            act.wait_ge(cond_in, 48)
            for v in range(2):
                act.activation(C2B[v][:, :], C2B[v][:, :], ACT.Silu).then_inc(cond_ready, 1)

            def pool_first(g):
                act.wait_ge(pooled, g + 1)
                if g > 0:
                    act.wait_ge(acc_done, MIX_AT[g - 1] + 1)
                act.activation(PLH[:, :], UP[:, PAD:PAD + T], ACT.Copy).then_inc(plh_ready, 1)

            for n in range(N_OUT1):
                evac_wait(n)
                src, slot = acc[:, n % 2, :], n % 2
                if n == 1 or n in POOLS:
                    act.activation(EV[slot][:, :], src, ACT.Copy).then_inc(acc_read, 1)
                elif n in MIXES:
                    g = MIXES[n]
                    act.activation(EV[slot][:, :], src, ACT.Copy, scale=vec("pool_scale", g)).then_inc(acc_read, 1)
                    act.wait_ge(acc_read, n + 1)
                    act.activation(MH[:, 4 + g, :], EV[slot][:, :], ACT.Copy).then_inc(mixh_ready, 1)
                else:
                    m = TURNS[n]
                    if m > 1:
                        act.wait_ge(qstat_done, m - 1)
                    steps.did(act.activation(CV[slot][:, :], src, ACT.Square))
                    act.activation(EV[slot][:, :], src, ACT.Copy, scale=vec("k_norm_g" if n == 0 else "q_norm_g")
                                   ).then_inc(acc_read, 1)
                    act.wait_ge(acc_read, n + 1)
                    steps.settle()
                    act.activation(SUM[:, 7:8], eps, ACT.Copy).then_inc(sqh_ready, 1)
                    if m == 0:
                        act.wait_ge(kms_done, 1)
                        act.activation(CV[1][:, :], turn[:, :], ACT.Sqrt, bias=eps).then_inc(ksd_ready, 1)
                if n - 1 in POOLS:
                    pool_first(POOLS[n - 1])
            act.wait_ge(qstat_done, 4)
            act.activation(QSD[:, :, :], bank6[:, 64:64 + TT * NQ].rearrange("p (t h) -> p t h", h=NQ), ACT.Sqrt, bias=eps,
                           scale=1.0 / HD).then_inc(qsd_ready, 1)
            act.wait_ge(post_done, N_OUT1)
            act.activation(KHI[:, :], KN[:, :], ACT.Copy).then_inc(khi_ready, 1)
            act.wait_ge(khi_ready, 1)
            for kv in range(NKV):
                for b in range(2):
                    act.activation(KSH[64 * b:64 * b + 64, kv, :], KHI[64 * kv:64 * kv + 64, :].bitcast(F32), ACT.Copy
                                   ).then_inc(kst_act, 1)
            act.wait_ge(vt_done, 1)
            vt = turn[:, :].rearrange("p (a d) -> p a d", d=HD)
            vdst = VTOK[:, :, :, :].rearrange("p t v d -> p (t v) d")
            act.wait_ge(acc_done, N_OUT1)
            act.wait_ge(kst_act, 4)
            act.activation(vdst[:, :, 0:HD], vt, ACT.Copy).then_inc(vh_ready, 1)

            act.wait_ge(kst_dve, 4)
            def stack_queries(it, s):
                m = 2 * it + s
                if not (isinstance(m, int) and m == 0):
                    act.wait_ge(qst_pool, it * 4 + 2 * s)
                    act.wait_ge(qst_act, it * 4 + 2 * s)
                act.activation(QH[:, :, :], QN[:, :, span(it * 256 + 128 * s)], ACT.Copy).then_inc(qh_ready, 1)
                act.wait_ge(qh_ready, it * 2 + (s + 1))
                for b in range(2):
                    dst = QST[s % 2][0:64, :, :].rearrange("p (i j) q -> p i j q", j=2)[:, :, b, :]
                    act.activation(dst, QH[64 * b:64 * b + 64, :, :].bitcast(F32), ACT.Copy).then_inc(qst_act, 1)

            def exponents(it, u):
                act.wait_ge(nb_ready, it * 16 + (u + 1))
                act.activation(EX[u % 4][:, :], acc[:, u % 2, :], ACT.Exp, bias=NBI[:, u % 2:u % 2 + 1],
                               scale=column(RSP, it * 16 + u), accum_out=SUM[:, u % 2:u % 2 + 1]).then_inc(exp_done, 1)

            def attend(it, last):
                for u in range(16):
                    if u % 4 == 0 and u > 0:
                        other_parts(it, u // 4 - 1)
                    if u % 2 == 0:
                        act.wait_ge(pv_done, it * 8 + (u // 2 + 1))
                    for h in range(2):
                        act.wait_ge(pt_done, it * 32 + (2 * u + h + 1))
                        act.activation(PTH[:, 4 * h:4 * h + 4, u % 4, :],
                                       turns[(2 * u + h) % 3].rearrange("p (k q) -> p k q", q=P), ACT.Copy
                                       ).then_inc(pth_ready, 1)
                    if u < 14 or not last:
                        exponents(it, u + 2)
                    if u == 1:
                        stack_queries(it, 1)
                    if u == 8:
                        branch_first(it, 0)
                    if u == 9 and not last:
                        stack_queries(it, 2)
                other_parts(it, 3)
                branch_first(it, 1)

            def other_parts(it, b):
                act.wait_ge(pv_done, it * 8 + (2 * b + 4))
                act.wait_ge(o_ready, it * 4 + (b + 1))
                act.activation(OTMP[0:64, :], bank6[64:128, :], ACT.Copy).then_inc(otmp_ready, 1)

            def branch_first(it, s):
                act.wait_ge(o_ready, it * 4 + (2 * s + 3))
                act.activation(MH[:, 0:4, span(it * 256 + 128 * s)], OT[:, :, :], ACT.Copy).then_inc(mh_ready, 1)

            act.wait_ge(cond_in, 64)
            act.activation(C1B[:, :], C1B[:, :], ACT.Silu).then_inc(cond_ready, 1)
            stack_queries(0, 0)
            exponents(0, 0)
            exponents(0, 1)
            with act.Fori(0, 3) as it:
                attend(it, False)
            attend(3, True)
            act.wait_ge(cond_in, 96)
            for v in range(2):
                act.activation(C2C[v][:, :], C2C[v][:, :], ACT.Silu).then_inc(cond_ready, 1)
            act.wait_ge(ml_ready, 9)

            def residual_tiles(q, n0, gate, with_stats, stream=XT):
                with act.Fori(0, 4) as it:
                    for s in range(2):
                        n = it * 2 + (n0 + s)
                        evac_wait(n)
                        act.activation(EV[s][:, :], acc[:, s, :], ACT.Copy,
                                       scale=gate(it * 2 + s)).then_inc(acc_read, 1)
                        if with_stats:
                            act.wait_ge(post_done, n + 1)
                            square(q, it * 2 + s, s, stream[:, bass.ds(it * 2 + s, 1), :])

            act.wait_ge(mods_ready, 5)
            residual_tiles(1, N_OUT1, lambda k: MOD1[:, bass.ds(k + 16, 1)], True)
            root(1)
            modulate(1, lambda k: A2[:, k:k + 1], lambda k: MOD1[:, 24 + k:25 + k], HH)
            def gated_chunk(g, it):
                f0 = sum(GROUPS[:g])
                for s in range(2):
                    n = it * 2 + (N_UP[g] + s)
                    evac_wait(n)
                    if s == 0:
                        act.wait_ge(post_done, n)
                    act.activation(EV[s][:, :], acc[:, s, :], ACT.Copy).then_inc(act_step, 1)
                    f = it + (f0 + FC * s)
                    act.activation(CV[s][:, :], acc[:, s, :], ACT.Identity, bias=vec("conv_b", f), scale=vec("conv_w", f + 44)
                                   ).then_inc(acc_read, 1)
                act.wait_ge(gated, it * 3 + (3 * f0 + 1))
                act.activation(EV[0][:, :], CV[0][:, :], ACT.Silu).then_inc(silu_done, 1)
                act.wait_ge(gated, it * 3 + (3 * f0 + 3))
                act.activation(GH[:, block_of(it), :], CV[0][:, :], ACT.Copy).then_inc(gh_ready, 1)

            for g, gk in enumerate(GROUPS):
                if g == 2:
                    act.wait_ge(cx_in, 16)
                    act.activation(SQC[:, :, :], CX[:, :, :], ACT.Square).then_inc(csq_ready, 1)
                gated_chunk(g, 0)
                if g == 2:
                    act.wait_ge(cstat_done, 1)
                    act.activation(SD2[:, :], bank6[:, 16:18], ACT.Sqrt, bias=eps, scale=1.0 / D).then_inc(csd_ready, 1)
                with act.Fori(1, gk) as it:
                    gated_chunk(g, it)
                if g == 2:
                    act.wait_ge(cxn_ready, 1)
                    for k in range(KD):
                        act.activation(CX[:, k, :], CX[:, k, :], ACT.Identity, bias=MOD2[:, k, 1:2], scale=A3[:, k, 1:2]
                                       ).then_inc(ch_ready, 1)
                    act.wait_ge(ch_ready, KD)
                    act.activation(HCH[:, :, :], CX[:, :, :], ACT.Copy).then_inc(hch_ready, 1)
                residual_tiles(2, N_DOWN[g], lambda k: MOD1[:, bass.ds(k + 40, 1)], g == 2)

            root(2)
            modulate(2, lambda k: A3[:, k, 0:1], lambda k: MOD2[:, k, 0:1], HH)
            def b_in(j):
                return vec("b_in_2", j)

            with act.Fori(0, 4) as it:
                n, u0 = it * 4 + N_ATT2, it * 16
                act.wait_ge(acc_done, n + 1)
                v = acc[:, 0, :].rearrange("p (r c) -> p r c", c=GRID)
                for b in range(NB):
                    dst = VT2[:, HALF * b:HALF * b + HALF].rearrange("p (r c) -> p r c", c=KW)
                    act.activation(dst, v[:, :, KCS[b]:KCS[b] + KW], ACT.Identity, bias=b_in(it + 32))
                act.activation(VT2[:, NB * HALF:], bank7[:, 0:CTX], ACT.Identity, bias=b_in(it + 32)).then_inc(acc_read, 1)

                def values_by_key(b, c0, c1):
                    act.wait_ge(vt2_done, it * 3 + (b + 1))
                    act.activation(VTOK2[:, c0:c1, :], turn[:, 0:P * (c1 - c0)].rearrange("p (c d) -> p c d", d=P), ACT.Copy
                                   ).then_inc(vtok2_ready, 1)

                act.wait_ge(x_saved, 16)
                values_by_key(0, 0, 8)
                values_by_key(1, 8, 16)
                values_by_key(2, 16, 18)
                act.wait_ge(acc_done, n + 2)
                for half in range(2):
                    src = acc[:, 1, HALF * half:HALF * half + HALF].rearrange("p (r n c) -> p n r c", n=NB, c=QW)
                    dst = Q2[:, HALF * half:HALF * half + HALF].rearrange("p (n r c) -> p n r c", n=NB, c=QW)
                    act.activation(dst, src, ACT.Identity, bias=BQ8[:, bass.ds(it, 1)], scale=-SCALE).then_inc(q2_ready, 1)
                act.activation(SUM[:, 7:8], eps, ACT.Copy).then_inc(acc_read, 1)
                act.wait_ge(q2_ready, it * 2 + 2)
                for j in range(2):
                    act.activation(Q2S[0:HD, j, :], Q2[HD * j:HD * j + HD, :], ACT.Copy).then_inc(q2_hi, 1)
                act.wait_ge(acc_done, n + 3)
                act.wait_ge(q2_split, it * 2 + 2)
                act.activation(K2[:, 0:T], acc[:, 0, :], ACT.Identity, bias=b_in(it + 28)).then_inc(k2_ready, 1)
                act.activation(K2[:, T:], bank6[:, 0:CTX], ACT.Identity, bias=b_in(it + 28)).then_inc(k2_ready, 1)
                act.activation(SUM[:, 7:8], eps, ACT.Copy).then_inc(acc_read, 1)
                act.wait_ge(k2_ready, it * 2 + 2)
                for j in range(2):
                    for b in range(2):
                        src = K2[HD * j:HD * j + HD, :]
                        act.activation(K2H[HD * b:HD * b + HD, j, :], src[:, 0:T], ACT.Copy)
                        act.activation(KC2H[HD * b:HD * b + HD, j, :], src[:, T:], ACT.Copy).then_inc(k2_hi, 1)
                act.wait_ge(acc_done, n + 4)
                act.activation(SZ[:, :], acc[:, 1, :], ACT.Silu, bias=b_in(it + 36)).then_inc(acc_read, 1)

                def turned(u):
                    for h, ks in enumerate(PARTS):
                        act.wait_ge(pt2_done, 2 * u0 + (2 * u + h + 1))
                        if u >= 2 and h == 0:
                            act.wait_ge(pv2_done, u0 + (u - 1))
                        act.activation(PT2[u % 2][:, P * ks[0]:P * ks[-1] + P], turn[:, HALF * h:HALF * h + P * len(ks)], ACT.Copy
                                       ).then_inc(pt2_ready, 1)

                def exponents(u):
                    act.wait_ge(nb2_ready, u0 + (u + 1))
                    act.activation(EX2[u % 3][:, :], acc[:, u % 2, P:P + NKEY], ACT.Exp, bias=NBI[:, u % 2:u % 2 + 1], scale=-1.0,
                                   accum_out=SUM[:, u % 2:u % 2 + 1]).then_inc(exp2_done, 1)

                exponents(0)
                exponents(1)
                for u in range(16):
                    turned(u)
                    if u < 14:
                        exponents(u + 2)
                act.wait_ge(pv2_done, u0 + 16)

            act.wait_ge(o2_ready, 64)
            act.activation(CBH[:, :, :], CBF[:, :, :], ACT.Copy).then_inc(cbh_ready, 1)

            def channels(it):
                act.wait_ge(chan_done, it + 1)
                act.activation(VW[:, :, :], turn[:, :].rearrange("p (c d) -> p c d", d=P), ACT.Copy).then_inc(vw_ready, 1)
                act.activation(VROW[0:1, :], bank6[0:1, 0:P], ACT.Copy)
                act.activation(ALT[:, 3:4], bank6[:, P:P + 1], ACT.Copy).then_inc(vw_ready, 1)

            def tokens(it):
                act.wait_ge(seq_done, it + 1)
                act.activation(SB[:, :], bank6[:, :], ACT.Copy).then_inc(sb_ready, 1)
                act.wait_ge(y_ready, it * 2 + 3)
                act.activation(BRH[:, block_of(it), :], CV[1][:, :], ACT.Copy).then_inc(brh_ready, 1)

            def project(it):
                n = it * 2 + N_F
                act.wait_ge(acc_done, n + 1)
                if isinstance(it, int):
                    act.wait_ge(post_done, N_F)
                else:
                    act.wait_ge(fold_ready, it)
                act.activation(EV[0][:, :], acc[:, 0, :], ACT.Identity, bias=b_in(it + 16)).then_inc(acc_read, 1)
                if not isinstance(it, int):
                    tokens(it - 1)
                evac_wait(n + 1)
                act.activation(EV[1][:, :], acc[:, 1, :], ACT.Silu, bias=b_in(it + 20)).then_inc(acc_read, 1)
                channels(it)

            project(0)
            with act.Fori(1, 4) as it:
                project(it)
            tokens(3)

            def gates(n0, b0, last=False):
                with act.Fori(0, KD) as it:
                    n = it * 2 + n0
                    evac_wait(n)
                    act.activation(EV[0][:, :], acc[:, 0, :], ACT.Sigmoid, bias=b_in(it + b0)).then_inc(acc_read, 1)
                    evac_wait(n + 1)
                    act.activation(EV[1][:, :], acc[:, 1, :], ACT.Copy).then_inc(acc_read, 1)
                    if last:
                        act.wait_ge(sums_ready, it + 1)
                        act.activation(SH[:, bass.ds(it, 1), :], S[:, bass.ds(it, 1), :], ACT.Copy).then_inc(sh_ready, 1)

            gates(N_GF, 56 - 8)
            gates(N_GC, 56)
            with act.Fori(0, 4) as it:
                n = it * 4 + N_A
                for j, (s, b0, fn) in enumerate(((0, 0, ACT.Identity), (1, 8, ACT.Identity), (0, 4, ACT.Identity),
                                                 (1, 12, ACT.Silu))):
                    evac_wait(n + j)
                    act.activation(EV[s][:, :], acc[:, s, :], fn, bias=b_in(it + b0)).then_inc(acc_read, 1)
                act.wait_ge(y_ready, it + 10)
                act.activation(BRH[:, bass.ds(it, 1), :], CV[0][:, :], ACT.Copy).then_inc(brh_ready, 1)
            gates(N_GA, 40, last=True)

            residual_tiles(3, N_OUT2, lambda k: MOD2[:, bass.ds(k + 16, 1), 0], True, XT2)
            root(3)

        @block.vector
        def _(dve):
            steps = Steps(dve, dve_step)

            def link(ins):
                steps.did(ins)
                steps.settle()

            def invert(q, nt=TT):
                dve.wait_ge(sd_ready, q + 1)
                dve.reciprocal(RS[:, 0:nt], SD[:, 0:nt]).then_inc(rs_ready, 1)

            def normed(q, src, hh, hl, w=T):
                dve.wait_ge(rb_done, q + 1)

                def second(k):
                    dve.wait_ge(hh_ready, q * KD + k + 1)
                    dve.tensor_tensor(hl[:, k, :], CV[k % 2][:, 0:w], hh[:, k, :].bitcast(F32), ALU.subtract
                                      ).then_inc(hl_ready, 1)

                for k in range(KD):
                    if k >= 2:
                        dve.wait_ge(hf_ready, q * KD + k - 1)
                    dve.tensor_tensor(EV[k % 2][:, 0:w], src(k), turn[:, 0:w], ALU.mult).then_inc(xn_ready, 1)
                    if k > 0:
                        second(k - 1)
                second(KD - 1)

            def modulation(w, cond, out):
                ins = dve.scalar_tensor_tensor(out=w, in0=w, scalar=1.0, in1=cond[:, :], op0=ALU.mult, op1=ALU.mult, accum_out=out)
                ins.then_inc(ada_used, 1)

            for k in range(1, KD):
                dve.wait_ge(sq_ready, k + 1)
                ins = dve.tensor_tensor(SQ1[:, 0, :], SQ1[:, 0, :], SQ1[:, k, :], ALU.add)
                if k < KD - 1:
                    link(ins)
            ins.then_inc(sq_summed, 1)
            dve.tensor_copy(MX[:, 5:6], eps).then_inc(sq_used, KD)
            dve.wait_ge(cond_ready, 1)
            for j in range(4):
                dve.wait_ge(ada1_in[j], 16)
                for b in range(4):
                    c = 2 * j + b // 2 + KD * (b % 2)
                    modulation(ADA1[j][:, b, :], C1A, MOD1[:, c:c + 1])
                link(dve.tensor_copy(MX[:, 6:7], eps))
                for c in (2 * j, KD + 2 * j):
                    link(dve.tensor_tensor(MOD1[:, c:c + 2], MOD1[:, c:c + 2], vec("b_ada", c, 2), ALU.add))
                dve.scalar_tensor_tensor(out=A1[:, 2 * j:2 * j + 2], in0=MOD1[:, KD + 2 * j:KD + 2 * j + 2], scalar=1.0,
                                         in1=vec("norm1_g", 2 * j, 2), op0=ALU.add, op1=ALU.mult).then_inc(mods_ready, 1)
                if j == 0:
                    invert(0)
                    dve.wait_ge(rb_done, 1)
                for k in (2 * j, 2 * j + 1):
                    if k >= 2:
                        dve.wait_ge(hf_ready, k - 1)
                    dve.tensor_tensor(EV[k % 2][:, :], XT[:, k, :], turn[:, :], ALU.mult).then_inc(xn_ready, 1)
            dve.wait_ge(rope_in, 32)
            for b in (UP, *WINS):
                steps.did(dve.memset(b[:, 0:PAD], 0.0))
                steps.did(dve.memset(b[:, PAD + T:], 0.0))
            steps.settle()

            def rope(n, m):
                dst = KN[:, :] if m == 0 else QN[:, m - 1, :]
                e = EV[n % 2]
                steps.settle()
                if n > 0:
                    dve.wait_ge(post_done, n)
                if m == 0:
                    dve.wait_ge(ksd_ready, 1)
                    link(dve.reciprocal(CV[1][:, :], CV[1][:, :]))
                dve.wait_ge(acc_read, n + 1)
                steps.did(dve.tensor_tensor(ROPE1[:, :], e[:, :], COS[:, :], ALU.mult))
                dve.wait_ge(rot_done, m + 1)
                link(dve.tensor_tensor(ROPE2[:, :], turn[:, :], SIN[:, :], ALU.mult))
                if m == 0:
                    link(dve.tensor_tensor(ROPE1[:, :], ROPE1[:, :], ROPE2[:, :], ALU.add))
                    dve.tensor_tensor(dst, ROPE1[:, :], CV[1][:, :], ALU.mult).then_inc(post_done, 1)
                else:
                    dve.tensor_tensor(dst, ROPE1[:, :], ROPE2[:, :], ALU.add).then_inc(post_done, 1)

            def windows(n, g):
                dve.wait_ge(acc_read, n + 1)
                if g > 0:
                    dve.wait_ge(plh_ready, g)
                    dve.wait_ge(pll_ready, g)
                dve.tensor_copy(UP[:, PAD:PAD + T], EV[n % 2][:, :]).then_inc(post_done, 1)
                dve.wait_ge(post_done, n + 1)
                w, half = POOL_W[g], POOL_W[g] // 2
                src, r = UP, 0
                link(dve.tensor_tensor(WINS[0][:, 1:T + 2 * PAD], UP[:, 1:T + 2 * PAD], UP[:, 0:T + 2 * PAD - 1], ALU.add))
                h = 1
                while 2 * h < w:
                    a, b = WINS[r], WINS[1 - r]
                    lo, hi = 2 * h, T + 2 * PAD - 2 * h + 1
                    link(dve.tensor_tensor(b[:, lo:hi], a[:, lo + h:hi + h], a[:, lo - h:hi - h], ALU.add))
                    r, h = 1 - r, 2 * h
                win = WINS[r]
                edge = con("edge", 16, 16 * g)
                steps.did(dve.tensor_tensor(win[:, PAD:PAD + 8], win[:, PAD:PAD + 8], edge[:, 0:8], ALU.mult))
                link(dve.tensor_tensor(win[:, PAD + T - 8:PAD + T], win[:, PAD + T - 8:PAD + T], edge[:, 8:16], ALU.mult))
                dve.scalar_tensor_tensor(out=UP[:, PAD:PAD + T], in0=win[:, PAD:PAD + T], scalar=1.0 / w, in1=UP[:, PAD:PAD + T],
                                         op0=ALU.mult, op1=ALU.subtract).then_inc(pooled, 1)
                dve.wait_ge(plh_ready, g + 1)
                dve.tensor_tensor(PLL[:, :], UP[:, PAD:PAD + T], PLH[:, :].bitcast(F32), ALU.subtract).then_inc(pll_ready, 1)
                dve.wait_ge(pll_ready, g + 1)

            def mix_second(n, g):
                dve.wait_ge(mixh_ready, g + 1)
                dve.tensor_tensor(ML[:, 4 + g, :], EV[n % 2][:, :], MH[:, 4 + g, :].bitcast(F32), ALU.subtract
                                  ).then_inc(post_done, 1)

            def modulation2(w, t, conds, junk):
                if t < 16:
                    link(dve.scalar_tensor_tensor(out=junk[:, :], in0=w, scalar=1.0, in1=conds[1][:, :], op0=ALU.mult, op1=ALU.mult,
                                                  accum_out=MOD2[:, t, 1:2]))
                modulation(w, conds[0], MOD2[:, t, 0:1])

            ada2_next = 0
            for n in range(N_OUT1):
                if n in ADA2_AT:
                    if n > 0:
                        dve.wait_ge(post_done, n)
                    for _ in range(ADA2_AT[n]):
                        dve.wait_ge(ada2_in[ada2_next // 2 % 2], 16 * (ada2_next // 4 + 1))
                        dve.wait_ge(cond_ready, 3)
                        modulation2(ADA2[ada2_next // 2 % 2][:, ada2_next % 2, :], ada2_next, C2B, ROPE1)
                        ada2_next += 1
                if n == 1:
                    dve.wait_ge(acc_read, 2)
                    dve.tensor_copy(VN[:, :], EV[1][:, :]).then_inc(post_done, 1)
                elif n in POOLS:
                    windows(n, POOLS[n])
                elif n in MIXES:
                    mix_second(n, MIXES[n])
                else:
                    rope(n, TURNS[n])
            dve.wait_ge(qsd_ready, 1)
            link(dve.reciprocal(QSD[:, :, :], QSD[:, :, :]))
            steps.did(dve.tensor_scalar(RSP[:, :, :], QSD[:, :, :], SCALE, None, ALU.mult))
            steps.did(dve.tensor_scalar(RSN[:, :, :], QSD[:, :, :], -SCALE, None, ALU.mult))
            dve.wait_ge(khi_ready, 1)
            dve.tensor_tensor(KLO[:, :], KN[:, :], KHI[:, :].bitcast(F32), ALU.subtract).then_inc(klo_ready, 1)
            dve.wait_ge(klo_ready, 1)
            for kv in range(NKV):
                for b in range(2):
                    dve.tensor_copy(KSL[64 * b:64 * b + 64, kv, :], KLO[64 * kv:64 * kv + 64, :]).then_inc(kst_dve, 1)
            dve.wait_ge(vh_ready, 1)
            vt = turn[:, :].rearrange("p (a d) -> p a d", d=HD)
            vdst = VTOK[:, :, :, :].rearrange("p t v d -> p (t v) d")
            dve.tensor_tensor(vdst[:, :, HD:P], vt, vdst[:, :, 0:HD].bitcast(F32), ALU.subtract).then_inc(vl_ready, 1)
            dve.wait_ge(vl_ready, 1)
            dve.wait_ge(kst_dve, 4)
            dve.wait_ge(kst_act, 4)

            dve.tensor_copy(MX[:, 7:8], eps).then_inc(ptl_ready, 2)
            dve.tensor_copy(MX[:, 6:7], eps).then_inc(o_ready, 1)

            def largest(it, u):
                j = u % 2
                dve.wait_ge(scores_done, it * 16 + (u + 1))
                link(dve.tensor_reduce(MX[:, j:j + 1], acc[:, j, :], AX.X, ALU.max))
                dve.tensor_tensor(NBI[:, j:j + 1], MX[:, j:j + 1], column(RSN, it * 16 + u), ALU.mult).then_inc(nb_ready, 1)

            def invert_sums(it, u):
                j = u % 2
                dve.wait_ge(exp_done, it * 16 + (u + 1))
                dve.reciprocal(RC[:, j:j + 1], SUM[:, j:j + 1]).then_inc(rc_ready, 1)

            def gather_o(it, b):
                dve.wait_ge(otmp_ready, it * 4 + (b + 1))
                g = b % 2
                if g == 0:
                    dve.wait_ge(ml_ready, it * 2 + (b // 2 + 1))
                o = bank6[0:64, :].rearrange("p (i j q) -> p i j q", j=2, q=P)
                m = OTMP[0:64, :].rearrange("p (i j q) -> p i j q", j=2, q=P)
                link(dve.tensor_tensor(OT[0:64, 2 * g:2 * g + 2, :], o[:, :, 0, :], m[:, :, 0, :], ALU.add))
                dve.tensor_tensor(OT[64:128, 2 * g:2 * g + 2, :], o[:, :, 1, :], m[:, :, 1, :], ALU.add).then_inc(o_ready, 1)

            def attend(it, last):
                for u in range(16):
                    if u < 14 or not last:
                        largest(it, u + 2)
                    if u < 15 or not last:
                        invert_sums(it, u + 1)
                    if u % 4 == 0 and u > 0:
                        gather_o(it, u // 4 - 1)
                    for h in range(2):
                        dve.wait_ge(pth_ready, it * 32 + (2 * u + h + 1))
                        dve.tensor_tensor(PTL[:, 4 * h:4 * h + 4, u % 4, :],
                                          turns[(2 * u + h) % 3].rearrange("p (k q) -> p k q", q=P),
                                          PTH[:, 4 * h:4 * h + 4, u % 4, :].bitcast(F32), ALU.subtract).then_inc(ptl_ready, 1)
                    if u % 8 == 5:
                        j = u // 8
                        dve.wait_ge(ada3_in[j], it * 16 + 16)
                        modulation(ADA3[j][:, :], C1B, MOD1[:, block_of(it * 2 + (16 + j))])
                gather_o(it, 3)

            dve.wait_ge(cond_ready, 4)
            largest(0, 0)
            largest(0, 1)
            invert_sums(0, 0)
            with steps.loop(3, 20) as it:
                attend(it, False)
            attend(3, True)
            link(dve.tensor_copy(MX[:, 6:7], eps))
            link(dve.tensor_tensor(MOD1[:, 16:24], MOD1[:, 16:24], vec("b_ada", 16, 8), ALU.add))
            link(dve.tensor_scalar(BQ8[:, 0:4], vec("b_in_2", 24, 4), -SCALE, None, ALU.mult))
            dve.tensor_copy(MX[:, 6:7], eps).then_inc(mods_ready, 1)

            def residual_tiles(n0, q=None, arrivals=None, stream=XT):
                def pair(it):
                    for s in range(2):
                        if arrivals:
                            dve.wait_ge(arrivals[2 * it + s], 16)
                        dve.wait_ge(acc_read, it * 2 + (n0 + s + 1))
                        x = stream[:, 2 * it + s, :] if isinstance(it, int) else stream[:, bass.ds(it * 2 + s, 1), :]
                        dve.tensor_tensor(x, x, EV[s][:, :], ALU.add).then_inc(post_done, 1)
                        if q is not None and not (isinstance(it, int) and it == 0 and s == 0):
                            sum_squares(it * 2 + (s - 1), 1 - s)

                def sum_squares(k, slot):
                    dve.wait_ge(sq_ready, k + (q * KD + 1))
                    if isinstance(k, int) and k == 0:
                        ins = dve.tensor_copy(SQS[:, :], SQ[slot][:, :])
                    else:
                        dve.wait_ge(sq_used, k + q * KD)
                        ins = dve.tensor_tensor(SQS[:, :], SQS[:, :], SQ[slot][:, :], ALU.add)
                    ins.then_inc(sq_used, 1)
                    return ins

                if arrivals:
                    for it in range(4):
                        for j in ((0, 1), (2, 3, 4), (5, 6, 7), (8,))[it]:
                            dve.wait_ge(ada4_in[j % 2], 16 * (j // 2 + 1))
                            if j == 6:
                                dve.wait_ge(cond_ready, 6)
                            for b in range(4):
                                i, w = ADA_LATE[4 * j + b], ADA4[j % 2][:, b, :]
                                if i < 48:
                                    modulation(w, C1B, MOD1[:, i:i + 1])
                                else:
                                    modulation2(w, i - 48, C2C, JUNK)
                        pair(it)
                else:
                    pair(0)
                    with dve.Fori(1, 4) as it:
                        pair(it)
                if q is not None:
                    sum_squares(KD - 1, 1)
                    dve.wait_ge(sq_used, q * KD + KD)
                    dve.tensor_copy(MX[:, 4:5], eps).then_inc(sq_summed, 1)

            residual_tiles(N_OUT1, 1, x_again)
            link(dve.tensor_copy(MX[:, 6:7], eps))
            link(dve.tensor_tensor(MOD2[:, :, 0], MOD2[:, :, 0], vec("b_ada_2", 0, 24), ALU.add))
            link(dve.tensor_tensor(MOD2[:, 0:16, 1], MOD2[:, 0:16, 1], vec("b_ada_2", 0, 16), ALU.add))
            for v in range(2):
                link(dve.scalar_tensor_tensor(out=A3[:, :, v], in0=MOD2[:, 8:16, v], scalar=1.0, in1=vec("norm_g_2", 0, KD),
                                              op0=ALU.add, op1=ALU.mult))
            link(dve.tensor_tensor(MOD1[:, 24:48], MOD1[:, 24:48], vec("b_ada", 24, 24), ALU.add))
            link(dve.scalar_tensor_tensor(out=A2[:, :], in0=MOD1[:, 32:40], scalar=1.0, in1=vec("norm2_g", 0, KD), op0=ALU.add,
                                          op1=ALU.mult))
            invert(1)
            normed(1, lambda k: XT[:, k, :], HH, HL)

            def shifted(s, f):
                link(dve.scalar_tensor_tensor(out=CV[s][:, 1:T], in0=EV[s][:, 0:T - 1], scalar=vec("conv_w", f), in1=CV[s][:, 1:T],
                                              op0=ALU.mult, op1=ALU.add))
                return dve.scalar_tensor_tensor(out=CV[s][:, 0:T - 1], in0=EV[s][:, 1:T], scalar=vec("conv_w", f + 88),
                                                in1=CV[s][:, 0:T - 1], op0=ALU.mult, op1=ALU.add)

            def gated_chunk(g, it):
                f0 = sum(GROUPS[:g])
                n = it * 2 + N_UP[g]
                dve.wait_ge(acc_read, n + 1)
                shifted(0, it + f0).then_inc(gated, 1)
                dve.wait_ge(acc_read, n + 2)
                shifted(1, it + (f0 + FC)).then_inc(gated, 1)
                dve.wait_ge(silu_done, it + (f0 + 1))
                dve.wait_ge(gated, it * 3 + (3 * f0 + 2))
                dve.tensor_tensor(CV[0][:, :], EV[0][:, :], CV[1][:, :], ALU.mult).then_inc(gated, 1)
                dve.wait_ge(gh_ready, it + (f0 + 1))
                dve.tensor_tensor(GL[:, block_of(it), :], CV[0][:, :], GH[:, block_of(it), :].bitcast(F32), ALU.subtract
                                  ).then_inc(post_done, 2)
                dve.wait_ge(post_done, n + 2)

            for g, gk in enumerate(GROUPS):
                gated_chunk(g, 0)
                if g == 2:
                    dve.wait_ge(csd_ready, 1)
                    dve.reciprocal(RC2[:, :], SD2[:, :]).then_inc(crs_ready, 1)
                with steps.loop(gk - 1, 2) as it:
                    gated_chunk(g, it + 1)
                if g == 2:
                    dve.wait_ge(crb_done, 1)
                    dve.tensor_tensor(CX[:, :, :], CX[:, :, :], turn[:, 0:CTX].unsqueeze(1).to_broadcast([P, KD, CTX]), ALU.mult
                                      ).then_inc(cxn_ready, 1)
                    dve.wait_ge(hch_ready, 1)
                    dve.tensor_tensor(HCL[:, :, :], CX[:, :, :], HCH[:, :, :].bitcast(F32), ALU.subtract).then_inc(hcl_ready, 1)
                residual_tiles(N_DOWN[g], 2 if g == 2 else None)

            invert(2)
            normed(2, lambda k: XT[:, k, :], HH, HL)

            with steps.loop(4, 16) as it:
                n, u0 = it * 4 + N_ATT2, it * 16

                def largest(u):
                    j, half, c, a = u // 8, u // 4 % 2, u % NB, acc[:, u % 2, :]
                    if u % 8 == 0:
                        dve.wait_ge(bias_in[j], it * 16 + 16)
                    dve.wait_ge(scores2_done, u0 + (u + 1))
                    link(dve.tensor_tensor(a[:, P:P + NLOC], a[:, P:P + NLOC], BIAS[j][:, 3 * half + KIND[c], :], ALU.subtract))
                    dve.tensor_reduce(NBI[:, u % 2:u % 2 + 1], a[:, P:P + NKEY], AX.X, ALU.min).then_inc(nb2_ready, 1)

                def diagonal(u):
                    dve.wait_ge(exp2_done, u0 + (u + 1))
                    dve.reciprocal(RC[:, u % 2:u % 2 + 1], SUM[:, u % 2:u % 2 + 1]).then_inc(rc_ready, 1)
                    dve.wait_ge(rc_ready, u0 + (64 + u + 1))
                    dve.tensor_scalar(DG[u % 2][:, :], ident, RC[:, u % 2:u % 2 + 1], None, ALU.mult).then_inc(dg_ready, 1)

                def gather(u):
                    j, half, c = u // 8, u // 4 % 2, u % NB
                    if u == 0:
                        dve.wait_ge(acc_read, n + 4)
                    dve.wait_ge(pv2_done, u0 + (u + 1))
                    rows = slice(HD * j, HD * j + HD)

                    def grid(x):
                        return x[rows, HALF * half:HALF * half + HALF].rearrange("p (r c) -> p r c", c=GRID)[:, :, QW * c:QW * c + QW]

                    branch = CBF[rows, bass.ds(it, 1), :].rearrange("p a t -> p (a t)")
                    dve.tensor_tensor(branch[:, HALF * half:HALF * half + HALF].rearrange("p (r c) -> p r c", c=GRID)
                                      [:, :, QW * c:QW * c + QW],
                                      (bank6, bank7)[u % 2][rows, 0:P].rearrange("p (r c) -> p r c", c=QW), grid(SZ), ALU.mult
                                      ).then_inc(o2_ready, 1)

                dve.wait_ge(q2_hi, it * 2 + 2)
                for j in range(2):
                    dve.tensor_tensor(Q2S[HD:P, j, :], Q2[HD * j:HD * j + HD, :], Q2S[0:HD, j, :].bitcast(F32), ALU.subtract
                                      ).then_inc(q2_split, 1)
                dve.wait_ge(k2_hi, it * 4 + 4)
                dve.wait_ge(vtok2_ready, it * 3 + 3)
                for j in range(2):
                    src = K2[HD * j:HD * j + HD, :]
                    for b in range(2):
                        rows, hi = slice(HD * b, HD * b + HD), slice(HD * j, HD * j + HD)
                        dve.tensor_tensor(K2L[rows, j, 0:T], src[:, 0:T], K2H[hi, j, :].bitcast(F32), ALU.subtract)
                        ins = dve.tensor_tensor(K2L[rows, j, T:], src[:, T:], KC2H[hi, j, :].bitcast(F32), ALU.subtract)
                    ins.then_inc(k2_split, 1)
                largest(0)
                largest(1)
                for u in range(16):
                    diagonal(u)
                    if u < 14:
                        largest(u + 2)
                    if u > 0:
                        gather(u - 1)
                gather(15)
                dve.wait_ge(o2_ready, u0 + 16)
                dve.tensor_copy(MX[:, 6:7], eps).then_inc(post_done, 4)
                dve.wait_ge(post_done, n + 4)
            dve.wait_ge(cbh_ready, 1)
            dve.tensor_tensor(CBL[:, :, :], CBF[:, :, :], CBH[:, :, :].bitcast(F32), ALU.subtract).then_inc(cbl_ready, 1)

            dve.wait_ge(dft_in, 16)
            dve.tensor_copy(FO[:, 0:1], zero).then_inc(y_ready, 1)
            def fold(it):
                n, u = it * 2 + N_F, EV[0]
                dve.wait_ge(acc_read, n + 1)
                steps.did(dve.tensor_tensor(FE[:, 1:HALF], u[:, 1:HALF], u[:, T - 1:HALF:-1], ALU.add))
                steps.did(dve.tensor_tensor(FO[:, 1:HALF], u[:, 1:HALF], u[:, T - 1:HALF:-1], ALU.subtract))
                steps.did(dve.tensor_copy(FE[:, 0:HALF + 1:HALF], u[:, 0:HALF + 1:HALF]))
                pairs = u[:, :].rearrange("p (t a) -> p a t", a=2)
                link(dve.tensor_reduce(ALT[:, 0:2], pairs, AX.X, ALU.add))
                dve.tensor_tensor(ALT[:, 2:3], ALT[:, 0:1], ALT[:, 1:2], ALU.subtract).then_inc(fold_ready, 1)

            def unfold(it):
                dve.wait_ge(sb_ready, it + 1)
                y = CV[0]
                dve.tensor_tensor(y[:, 0:HALF], bank7[:, :], SB[:, :], ALU.subtract)
                dve.tensor_tensor(y[:, HALF + 1:T], bank7[:, HALF - 1:0:-1], SB[:, HALF - 1:0:-1], ALU.add).then_inc(y_ready, 1)
                steps.did(dve.tensor_copy(y[:, HALF:HALF + 1], ALT[:, 3:4]))
                dve.wait_ge(y_ready, it * 2 + 2)
                steps.settle()
                dve.wait_ge(acc_read, it * 2 + (N_F + 2))
                dve.tensor_tensor(CV[1][:, :], y[:, :], EV[1][:, :], ALU.mult).then_inc(y_ready, 1)
                dve.wait_ge(brh_ready, it + 1)
                dve.tensor_tensor(BRL[:, block_of(it), :], CV[1][:, :], BRH[:, block_of(it), :].bitcast(F32), ALU.subtract
                                  ).then_inc(post_done, 2)
                dve.wait_ge(post_done, it * 2 + (N_F + 2))

            fold(0)
            with steps.loop(3, 5) as it:
                fold(it + 1)
                unfold(it)
            unfold(3)

            with dve.Fori(0, KD) as it:
                dve.wait_ge(acc_read, it * 2 + (N_GF + 2))
                dve.tensor_tensor(S[:, bass.ds(it, 1), :], EV[0][:, :], EV[1][:, :], ALU.mult).then_inc(post_done, 2)

            def gates(n0, last=False):
                with steps.loop(KD, 1) as it:
                    s = S[:, bass.ds(it, 1), :]
                    dve.wait_ge(acc_read, it * 2 + (n0 + 2))
                    link(dve.tensor_tensor(CV[0][:, :], EV[0][:, :], EV[1][:, :], ALU.mult))
                    if last:
                        dve.tensor_tensor(s, s, CV[0][:, :], ALU.add).then_inc(sums_ready, 1)
                        dve.wait_ge(sh_ready, it + 1)
                        dve.tensor_tensor(SL[:, bass.ds(it, 1), :], s, SH[:, bass.ds(it, 1), :].bitcast(F32), ALU.subtract
                                          ).then_inc(post_done, 2)
                    else:
                        dve.tensor_tensor(s, s, CV[0][:, :], ALU.add).then_inc(post_done, 2)
                    dve.wait_ge(post_done, it * 2 + (n0 + 2))

            dve.wait_ge(post_done, N_GC)
            gates(N_GC)
            with steps.loop(4, 5) as it:
                n = it * 4 + N_A
                dve.wait_ge(acc_read, n + 2)
                dve.tensor_tensor(CV[1][:, :], EV[0][:, :], EV[1][:, :], ALU.mult).then_inc(post_done, 2)
                dve.wait_ge(post_done, n + 2)

                def tap(i):
                    return vec("w_conv_2", it + 4 * i)

                link(dve.tensor_scalar(CV[0][:, :], CV[1][:, :], tap(1), vec("b_conv_2", it), ALU.mult, ALU.add))
                link(dve.scalar_tensor_tensor(out=CV[0][:, 1:T], in0=CV[1][:, 0:T - 1], scalar=tap(0), in1=CV[0][:, 1:T],
                                              op0=ALU.mult, op1=ALU.add))
                link(dve.scalar_tensor_tensor(out=CV[0][:, 0:T - 1], in0=CV[1][:, 1:T], scalar=tap(2), in1=CV[0][:, 0:T - 1],
                                              op0=ALU.mult, op1=ALU.add))
                dve.wait_ge(acc_read, n + 3)
                link(dve.tensor_tensor(CV[0][:, :], CV[0][:, :], EV[0][:, :], ALU.mult))
                dve.tensor_copy(MX[:, 6:7], eps).then_inc(post_done, 1)
                dve.wait_ge(acc_read, n + 4)
                dve.tensor_tensor(CV[0][:, :], CV[0][:, :], EV[1][:, :], ALU.mult).then_inc(y_ready, 1)
                dve.wait_ge(brh_ready, it + 5)
                steps.did(dve.tensor_tensor(BRL[:, bass.ds(it, 1), :], CV[0][:, :], BRH[:, bass.ds(it, 1), :].bitcast(F32),
                                            ALU.subtract))
                steps.settle()
                dve.tensor_copy(MX[:, 6:7], eps).then_inc(post_done, 1)
                dve.wait_ge(post_done, n + 4)
            gates(N_GA, last=True)

            dve.wait_ge(x_back, 16)
            residual_tiles(N_OUT2, 3, stream=XT2)
            invert(3)
            dve.wait_ge(rb_done, 4)
            for k in range(KD):
                dve.scalar_tensor_tensor(out=XT2[:, k, :], in0=XT2[:, k, :], scalar=vec("final_g_2", k), in1=turn[:, :],
                                         op0=ALU.mult, op1=ALU.mult).then_inc(out_ready, 1)


def tiles_of(w):
    i, o = w.shape
    return np.ascontiguousarray(w.reshape(i // P, P, o // P, P).transpose(2, 1, 0, 3)).reshape(o // P, P, -1)


def cols_of(v):
    return np.asarray(v).reshape(-1, P).T


def layout(x):
    f = {k: np.asarray(v) for k, v in x.items()}
    vec = {
        "b_ada": cols_of(f["b_ada"]), "norm1_g": cols_of(f["norm1_g"]), "pool_scale": cols_of(f["pool_scale"]),
        "norm2_g": cols_of(f["norm2_g"]), "conv_w": cols_of(f["conv_w"]), "conv_b": cols_of(f["conv_b"]),
        "b_ada_2": cols_of(f["b_ada_2"]), "norm_g_2": cols_of(f["norm_g_2"]), "b_in_2": cols_of(f["b_in_2"]),
        "w_conv_2": cols_of(f["w_conv_2"]), "b_conv_2": cols_of(f["b_conv_2"]), "final_g_2": cols_of(f["final_g_2"]),
        "q_norm_g": np.concatenate([f["q_norm_g"][0]] * 2)[:, None],
        "k_norm_g": np.concatenate([f["k_norm_g"][0]] * 2)[:, None],
    }
    w_in, w_up, w_down = (f[k][0] for k in ("w_in", "w_up", "w_down"))
    tin, tup = tiles_of(w_in), tiles_of(w_up)
    place = {"k": 4, "v": 5, **{f"q{i}": i for i in range(4)}, **{f"p{g}": 6 + g for g in range(4)}}
    stream = [tin[[place[name] for name in IN_ORDER if name in place]], tiles_of(f["w_out"][0])]
    w6, f0 = None, 0
    for gk in GROUPS:
        stream.append(np.stack([tup[f0:f0 + gk], tup[FC + f0:FC + f0 + gk]], axis=1).reshape(2 * gk, P, -1))
        down = tiles_of(w_down[f0 * P:(f0 + gk) * P])
        if gk == KD:
            stream.append(down)
        else:
            w6 = down
        f0 += gk
    w2 = tiles_of(f["w_in_2"][0])
    col = {name: o // P for name, o in (("a_x", 0), ("a_b", 512), ("a_c", 1024), ("a_z", 1536), ("f_u", 2048), ("f_z", 2560),
                                        ("q", 3072), ("k", 3584), ("v", 4096), ("c_z", 4608), ("g_a", 5120), ("g_f", 6144),
                                        ("g_c", 7168))}

    def in_turn(names, count):
        return w2[[col[name] + i for i in range(count) for name in names]]

    stream += [in_turn(("v", "q", "k", "c_z"), 4), in_turn(("f_u", "f_z"), 4), in_turn(("g_f",), 8), in_turn(("g_c",), 8),
               in_turn(("a_x", "a_c", "a_b", "a_z"), 4), in_turn(("g_a",), 8), tiles_of(f["w_out_2"][0])]
    w4 = np.concatenate([tiles_of(f[name][0]) for name in ("w_br_f_2", "w_br_c_2", "w_br_a_2")])
    ada = np.concatenate([f["w_ada"][0].T, f["w_ada_2"][0].T]).reshape(72, P, D)
    ada = ada[[c for k in range(KD) for c in (k, KD + k)] + list(range(2 * KD, 72))]
    conds = np.ascontiguousarray(np.stack([np.broadcast_to(f[k].reshape(1, D), (P, D)) for k in ("c", "c_2", "c_ctx_2")]))
    con = np.zeros((P, NCONST), np.float32)
    con[:, CCOL["ident"]:CCOL["ident"] + P] = np.eye(P)
    r = np.arange(P)
    con[:, CCOL["headmean"]:CCOL["headmean"] + P] = (r[:, None] // HD == r[None, :] // HD) / HD
    rot = np.zeros((P, P))
    for i in range(P):
        if i % 32 < 16:
            rot[i + 16, i] = -1.0
        else:
            rot[i - 16, i] = 1.0
    con[:, CCOL["rot"]:CCOL["rot"] + P] = rot
    con[:, CCOL["headsel"]:CCOL["headsel"] + 2] = r[:, None] // HD == np.arange(2)[None, :]
    con[:, CCOL["one"]] = 1.0
    con[:, CCOL["eps"]] = EPS
    for g, w in enumerate(POOL_W):
        t = np.r_[0:8, T - 8:T]
        count = np.minimum(t + w // 2 - 1, T - 1) - np.maximum(t - w // 2, 0) + 1
        con[:, CCOL["edge"] + 16 * g:CCOL["edge"] + 16 * g + 16] = w / count
    inv = (1.0 / (10000.0 ** (np.arange(0, 32, 2, dtype=np.float32) / 32))).astype(np.float32)
    pos = np.stack([np.repeat(np.arange(ROWS), GRID), np.tile(np.arange(GRID), ROWS)]).astype(np.float32)
    d = r % HD
    ang = pos[d // 32] * inv[d % 16][:, None]
    rope = np.stack([np.cos(ang), np.sin(ang)]).astype(np.float32)
    query, key = np.arange(P), np.arange(NLOC)
    bias = np.full((NQ, P, 6, NLOC), NEG, np.float32)
    for half in range(2):
        qr, kr = 8 * half + query // QW, 4 * half + key // KW
        r0 = np.clip(qr - KH // 2, 0, ROWS - KH)
        row_ok = (kr[None] >= r0[:, None]) & (kr[None] < r0[:, None] + KH)
        for kind, b in enumerate((0, 1, 3)):
            qc, kc = QW * b + query % QW, KCS[b] + key % KW
            c0 = np.clip(qc - QW // 2, 0, GRID - QW)
            ok = row_ok & (kc[None] >= c0[:, None]) & (kc[None] < c0[:, None] + QW)
            dr = np.clip(kr[None] - qr[:, None] + KH - 1, 0, 2 * KH - 2)
            dc = np.clip(kc[None] - qc[:, None] + QW - 1, 0, 2 * QW - 2)
            bias[:, :, 3 * half + kind] = np.where(ok[None], f["rpb_2"][0][:, dr, dc], np.float32(NEG))
    t = np.arange(HALF)
    ang_t = 2 * np.pi / T * (np.outer(t, t) % T)
    ang_c = 2 * np.pi / P * (np.outer(r, r) % P)
    rows = lambda m: m.reshape(4, P, HALF).transpose(1, 0, 2).reshape(P, -1)
    norm = 1.0 / math.sqrt(T * P)
    dft = np.concatenate([rows(np.cos(ang_t)), rows(np.sin(ang_t)), np.cos(ang_c) * norm, np.sin(ang_c) * norm,
                          np.tile(1.0 - 2.0 * (t % 2), (P, 1))], axis=1).astype(np.float32)
    return {
        "ctxT": np.ascontiguousarray(f["ctx_2"][0].T).reshape(KD, P, CTX), "bias": bias, "dft": dft, "w4": w4,
        "xT": np.ascontiguousarray(f["x"][0].T).reshape(KD, P, T),
        "vecs": np.ascontiguousarray(np.concatenate([vec[n] for n, _ in _VECS], axis=1)),
        "consts": con, "rope": rope,
        "w8": np.concatenate(stream), "w6": w6, "w1": np.ascontiguousarray(f["w_pool"][0]),
        "ada": ada, "conds": conds,
    }


def kernel(**inputs):
    import concourse.bacc as bacc
    from concourse.bass_utils import run_bass_kernel_spmd as run

    nc = bacc.Bacc("TRN2", target_bir_lowering=False, num_devices=1)
    arrays = layout(inputs)
    aps = {name: nc.dram_tensor(f"in_{name}", a.shape, mybir.dt.from_np(a.dtype), kind="ExternalInput").ap()
           for name, a in arrays.items()}
    out = nc.dram_tensor("out_xT", (KD, P, T), F32, kind="ExternalOutput").ap()
    build(nc, aps, out)
    r = run(nc, [{f"in_{name}": a for name, a in arrays.items()}], core_ids=[0])
    return np.ascontiguousarray(r.results[0]["out_xT"].reshape(D, T).T).reshape(1, T, D)
```
